# Optimizing a Trainium2 kernel written in Bass

```python
import math
import jax, jax.numpy as jnp
from jax import lax
import numpy as np

D_MODEL = 1024
BATCH = 1
SEQ = 512
DEPTH = 2

HEAD_DIM = 64
N_HEADS = D_MODEL // HEAD_DIM
D_FF = 4 * D_MODEL
DECAY_LORA = 64
AAA_LORA = 64
GATE_LORA = 160
N_SHIFT_MIX = 6
BLOCK_Q = 128
N_A_LAYERS = DEPTH // 2
N_B_LAYERS = DEPTH - N_A_LAYERS
NORM_EPS = 1e-6
GN_EPS = 64e-5


def rmsnorm(x, g, eps=NORM_EPS):
    xf = x.astype(jnp.float32)
    y = xf * lax.rsqrt(jnp.mean(xf * xf, axis=-1, keepdims=True) + eps)
    return (y * g.astype(jnp.float32)).astype(x.dtype)

def to_heads(t):
    b, s, _ = t.shape
    return t.reshape(b, s, N_HEADS, HEAD_DIM)

def rwkv7_time_mix(h, mu, w_rkv, w0, w1, w2, a0, a1, a2, g1, g2,
                   k_k, k_a, r_k, lnx_w, lnx_b, w_o):
    B, T, D = h.shape
    f32 = jnp.float32
    x_prev = jnp.pad(h[:, :-1], ((0, 0), (1, 0), (0, 0)))
    xx = x_prev - h
    xs = h[None] + xx[None] * mu[:, None, None, :]
    x_r, x_w, x_k, x_v, x_a, x_g = xs[0], xs[1], xs[2], xs[3], xs[4], xs[5]
    rkv = jnp.einsum('pbtd,pde->pbte', jnp.stack([x_r, x_k, x_v]), w_rkv)
    r, k, v = rkv[0], rkv[1], rkv[2]
    w = -jax.nn.softplus(-(w0 + jnp.tanh(x_w @ w1) @ w2)) - 0.5
    decay = jnp.exp(-jnp.exp(w.astype(f32)))
    a = jax.nn.sigmoid(a0 + (x_a @ a1) @ a2)
    g = jax.nn.sigmoid(x_g @ g1) @ g2
    kk = to_heads((k * k_k).astype(f32))
    kk = kk / jnp.maximum(jnp.linalg.norm(kk, axis=-1, keepdims=True), 1e-12)
    k = k * (1.0 + (a - 1.0) * k_a)

    r_h = to_heads(r).astype(f32)
    k_h = to_heads(k).astype(f32)
    v_h = to_heads(v).astype(f32)
    a_h = to_heads(a).astype(f32)
    w_h = to_heads(decay)
    b_h = kk * a_h

    def step(S, inp):
        r_t, w_t, k_t, v_t, kk_t, b_t = inp
        sa = jnp.einsum('bhvk,bhk->bhv', S, -kk_t)
        S = (S * w_t[:, :, None, :] + sa[..., None] * b_t[:, :, None, :]
             + v_t[..., None] * k_t[:, :, None, :])
        y_t = jnp.einsum('bhvk,bhk->bhv', S, r_t)
        return S, y_t

    tm = lambda t: jnp.moveaxis(t, 1, 0)
    S0 = jnp.zeros((B, N_HEADS, HEAD_DIM, HEAD_DIM), f32)
    _, y = lax.scan(step, S0, (tm(r_h), tm(w_h), tm(k_h), tm(v_h), tm(kk), tm(b_h)))
    y = jnp.moveaxis(y, 0, 1)

    mean = jnp.mean(y, axis=-1, keepdims=True)
    var = jnp.mean(jnp.square(y - mean), axis=-1, keepdims=True)
    y = (y - mean) * lax.rsqrt(var + GN_EPS)
    y = y.reshape(B, T, D) * lnx_w.astype(f32) + lnx_b.astype(f32)
    bonus = jnp.sum(r_h * k_h * r_k.astype(f32), axis=-1, keepdims=True) * v_h
    y = (y + bonus.reshape(B, T, D)).astype(h.dtype) * g
    return y @ w_o

def shared_kv(x, kv_norm_g, kv_w, kv_f_bias, k_norm_g):
    D = x.shape[-1]
    h = rmsnorm(x, kv_norm_g)
    proj = h @ kv_w
    k = to_heads(proj[..., :D])
    v = to_heads(proj[..., D:2 * D])
    f_logit = (proj[..., 2 * D:] + kv_f_bias).astype(jnp.float32)
    k = rmsnorm(k, k_norm_g)
    log_f = jax.nn.log_sigmoid(f_logit)
    c = jnp.cumsum(jnp.transpose(log_f, (0, 2, 1)), axis=-1)
    return jnp.transpose(k, (0, 2, 1, 3)), jnp.transpose(v, (0, 2, 1, 3)), c

def forgetting_attention(q, k, v, c):
    T = q.shape[2]
    scale = 1.0 / math.sqrt(HEAD_DIM)
    outs = []
    for s in range(0, T, BLOCK_Q):
        e = s + BLOCK_Q
        logits = jnp.einsum('bhqd,bhkd->bhqk', q[:, :, s:e], k[:, :, :e]).astype(jnp.float32) * scale
        logits = logits + (c[:, :, s:e, None] - c[:, :, None, :e])
        causal = jnp.arange(s, e)[:, None] >= jnp.arange(e)[None, :]
        logits = jnp.where(causal, logits, -jnp.inf)
        p = jax.nn.softmax(logits, axis=-1).astype(v.dtype)
        outs.append(jnp.einsum('bhqk,bhkd->bhqd', p, v[:, :, :e]))
    return jnp.concatenate(outs, axis=2)

def fox_layer(h, w_q, q_norm_g, w_o, k_sh, v_sh, c_sh):
    B, T, D = h.shape
    q = rmsnorm(to_heads(h @ w_q), q_norm_g)
    q = jnp.transpose(q, (0, 2, 1, 3))
    o = forgetting_attention(q, k_sh, v_sh, c_sh)
    o = jnp.transpose(o, (0, 2, 1, 3)).reshape(B, T, D)
    return o @ w_o

def sq_relu_mlp(h, w_in, w_out):
    return jnp.square(jax.nn.relu(h @ w_in)) @ w_out

def first_inputs(seed: int = 0) -> dict:
    key = jax.random.key(seed)
    ks = iter(jax.random.split(key, 40))
    D, H, N, F = D_MODEL, N_HEADS, HEAD_DIM, D_FF
    nA, nB = N_A_LAYERS, N_B_LAYERS
    nrm = lambda shape, s: s * jax.random.normal(next(ks), shape, jnp.float32)
    gain = lambda shape: 1.0 + nrm(shape, 0.05)
    decay_base = jnp.linspace(-6.5, -1.5, D, dtype=jnp.float32)
    inp = {}
    inp["x"] = jax.random.normal(next(ks), (BATCH, SEQ, D), jnp.float32)
    inp["rwkv_norm_g"] = gain((nA, D))
    inp["rwkv_mu"] = jax.random.uniform(next(ks), (nA, N_SHIFT_MIX, D), jnp.float32)
    inp["rwkv_w_rkv"] = nrm((nA, 3, D, D), D ** -0.5)
    inp["rwkv_w0"] = decay_base[None] + nrm((nA, D), 0.1)
    inp["rwkv_w1"] = nrm((nA, D, DECAY_LORA), D ** -0.5)
    inp["rwkv_w2"] = nrm((nA, DECAY_LORA, D), 0.1 * DECAY_LORA ** -0.5)
    inp["rwkv_a0"] = nrm((nA, D), 0.1)
    inp["rwkv_a1"] = nrm((nA, D, AAA_LORA), D ** -0.5)
    inp["rwkv_a2"] = nrm((nA, AAA_LORA, D), 0.1 * AAA_LORA ** -0.5)
    inp["rwkv_g1"] = nrm((nA, D, GATE_LORA), D ** -0.5)
    inp["rwkv_g2"] = nrm((nA, GATE_LORA, D), GATE_LORA ** -0.5)
    inp["rwkv_k_k"] = 0.85 + nrm((nA, D), 0.05)
    inp["rwkv_k_a"] = 1.0 + nrm((nA, D), 0.05)
    inp["rwkv_r_k"] = nrm((nA, H, N), 0.1)
    inp["rwkv_lnx_w"] = gain((nA, D))
    inp["rwkv_lnx_b"] = nrm((nA, D), 0.02)
    inp["rwkv_w_o"] = nrm((nA, D, D), 0.5 * D ** -0.5)
    inp["kv_norm_g"] = gain((D,))
    inp["kv_w"] = nrm((D, 2 * D + H), D ** -0.5)
    inp["kv_f_bias"] = jax.random.uniform(next(ks), (H,), jnp.float32, 0.5, 3.0)
    inp["k_norm_g"] = gain((H, N))
    inp["attn_norm_g"] = gain((nB, D))
    inp["attn_w_q"] = nrm((nB, D, D), D ** -0.5)
    inp["q_norm_g"] = gain((nB, H, N))
    inp["attn_w_o"] = nrm((nB, D, D), 0.5 * D ** -0.5)
    inp["mlp_norm_g"] = gain((DEPTH, D))
    inp["mlp_w_in"] = nrm((DEPTH, D, F), D ** -0.5)
    inp["mlp_w_out"] = nrm((DEPTH, F, D), 0.5 * F ** -0.5)
    return inp

def first_block(x, rwkv_norm_g, rwkv_mu, rwkv_w_rkv, rwkv_w0, rwkv_w1, rwkv_w2,
              rwkv_a0, rwkv_a1, rwkv_a2, rwkv_g1, rwkv_g2, rwkv_k_k, rwkv_k_a,
              rwkv_r_k, rwkv_lnx_w, rwkv_lnx_b, rwkv_w_o,
              kv_norm_g, kv_w, kv_f_bias, k_norm_g,
              attn_norm_g, attn_w_q, q_norm_g, attn_w_o,
              mlp_norm_g, mlp_w_in, mlp_w_out):
    k_sh = v_sh = c_sh = None
    for layer in range(DEPTH):
        if layer < N_A_LAYERS:
            i = layer
            h = rmsnorm(x, rwkv_norm_g[i])
            x = x + rwkv7_time_mix(h, rwkv_mu[i], rwkv_w_rkv[i], rwkv_w0[i], rwkv_w1[i],
                                   rwkv_w2[i], rwkv_a0[i], rwkv_a1[i], rwkv_a2[i],
                                   rwkv_g1[i], rwkv_g2[i], rwkv_k_k[i], rwkv_k_a[i],
                                   rwkv_r_k[i], rwkv_lnx_w[i], rwkv_lnx_b[i], rwkv_w_o[i])
        else:
            j = layer - N_A_LAYERS
            h = rmsnorm(x, attn_norm_g[j])
            x = x + fox_layer(h, attn_w_q[j], q_norm_g[j], attn_w_o[j], k_sh, v_sh, c_sh)
        x = x + sq_relu_mlp(rmsnorm(x, mlp_norm_g[layer]), mlp_w_in[layer], mlp_w_out[layer])
        if layer == N_A_LAYERS - 1:
            k_sh, v_sh, c_sh = shared_kv(x, kv_norm_g, kv_w, kv_f_bias, k_norm_g)
    return x


DEPTH_2 = 1

N_HEADS_2 = 8
N_KV = 2
GQA = N_HEADS_2 // N_KV
CMP_BLOCK = 32
CMP_STRIDE = 16
SLC_BLOCK = 64
N_SLC = 16
WINDOW = 512
Q_BLOCK = 128
SLC_Q_BLOCK = 64
FORCE_SCORE = 1e4
SCALE = 1.0 / math.sqrt(HEAD_DIM)
CONV_WIDTH = D_MODEL
CONV_K = 3
D_FF_2 = 4 * D_MODEL
EPS = 1e-6
NEG_INF = -1e30

QW = N_HEADS_2 * HEAD_DIM
KVW = N_KV * HEAD_DIM
SPLITS = (QW, KVW, KVW, KVW, KVW, KVW, KVW, 3 * N_HEADS_2,
          CONV_WIDTH, CONV_WIDTH, CONV_WIDTH, D_MODEL, D_MODEL)
PROJ_WIDTH = sum(SPLITS)
SPLIT_POINTS = tuple(int(v) for v in np.cumsum(SPLITS)[:-1])


def rms_norm(x, g):
    xf = x.astype(jnp.float32)
    y = xf * lax.rsqrt(jnp.mean(xf * xf, axis=-1, keepdims=True) + EPS)
    return (y * g.astype(jnp.float32)).astype(x.dtype)

def alibi_slopes():
    s = 2.0 ** (-8.0 * jnp.arange(1, N_HEADS_2 + 1, dtype=jnp.float32) / N_HEADS_2)
    return s.reshape(N_KV, GQA)

def masked_softmax(s, mask):
    s = jnp.where(mask, s.astype(jnp.float32), NEG_INF)
    m = jnp.max(s, axis=-1, keepdims=True)
    e = jnp.where(mask, jnp.exp(s - m), 0.0)
    return e / jnp.maximum(jnp.sum(e, axis=-1, keepdims=True), 1e-30)

def compress(k, pos_emb, w):
    B_, S_ = k.shape[0], k.shape[1]
    r = CMP_BLOCK // CMP_STRIDE
    c = k.reshape(B_, S_ // CMP_STRIDE, CMP_STRIDE, N_KV, HEAD_DIM)
    nc = S_ // CMP_STRIDE - r + 1
    blocks = jnp.concatenate([c[:, i:i + nc] for i in range(r)], axis=2)
    blocks = blocks + pos_emb[None, None, :, None, :]
    blocks = blocks.transpose(0, 1, 3, 2, 4).reshape(B_, nc, N_KV, CMP_BLOCK * HEAD_DIM)
    return blocks @ w

def hybrid_layer(x, norm1_g, w_in, q_norm_g, k_norm_g, cmp_pos_k, cmp_pos_v,
                 w_cmp_k, w_cmp_v, conv_w, w_branch_a, w_branch_b, w_out,
                 norm2_g, w_up, w_down):
    B_, S_, _ = x.shape
    xn = rms_norm(x, norm1_g)
    proj = xn @ w_in
    (q, k_c, v_c, k_s, v_s, k_w, v_w, g_nsa, conv_b, conv_c, conv_x,
     gate_a, gate_b) = jnp.split(proj, SPLIT_POINTS, axis=-1)

    q = rms_norm(q.reshape(B_, S_, N_HEADS_2, HEAD_DIM), q_norm_g)
    q = q.reshape(B_, S_, N_KV, GQA, HEAD_DIM)
    kv_shape = (B_, S_, N_KV, HEAD_DIM)
    k_s = rms_norm(k_s.reshape(kv_shape), k_norm_g[1])
    k_w = rms_norm(k_w.reshape(kv_shape), k_norm_g[2])
    v_s = v_s.reshape(kv_shape)
    v_w = v_w.reshape(kv_shape)
    kc = rms_norm(compress(k_c.reshape(kv_shape), cmp_pos_k, w_cmp_k), k_norm_g[0])
    vc = compress(v_c.reshape(kv_shape), cmp_pos_v, w_cmp_v)

    slopes = alibi_slopes()
    t = jnp.arange(S_)

    nc = kc.shape[1]
    c_start = jnp.arange(nc) * CMP_STRIDE
    c_end = c_start + CMP_BLOCK - 1
    dist_c = (t[:, None] - c_end[None, :]).astype(jnp.float32)
    s_c = (jnp.einsum('bsgrd,bcgd->bgrsc', q, kc).astype(jnp.float32) * SCALE
           - slopes[:, :, None, None] * dist_c)
    p_c = masked_softmax(s_c, dist_c >= 0)
    o_cmp = jnp.einsum('bgrsc,bcgd->bsgrd', p_c.astype(vc.dtype), vc)

    ns = S_ // SLC_BLOCK
    s_start = jnp.arange(ns) * SLC_BLOCK
    overlap = jnp.clip(jnp.minimum(c_start[:, None] + CMP_BLOCK, s_start[None, :] + SLC_BLOCK)
                       - jnp.maximum(c_start[:, None], s_start[None, :]), 0, None)
    overlap = overlap.astype(jnp.float32) / CMP_BLOCK
    imp = jnp.einsum('bgrsc,cj->bgsj', p_c, overlap)
    cur = (t // SLC_BLOCK)[:, None]
    j = jnp.arange(ns)[None, :]
    forced = (j == 0) | (j == cur) | (j == cur - 1)
    score = jnp.where(forced, FORCE_SCORE, jnp.where(j <= cur, imp, -1.0))
    n_sel = min(N_SLC, ns)
    _, sel_idx = lax.top_k(score, n_sel)

    kb = k_s.reshape(B_, ns, SLC_BLOCK, N_KV, HEAD_DIM).transpose(0, 3, 1, 2, 4)
    vb = v_s.reshape(B_, ns, SLC_BLOCK, N_KV, HEAD_DIM).transpose(0, 3, 1, 2, 4)
    gather = jax.vmap(jax.vmap(lambda blk, ids: blk[ids]))
    m_sel = n_sel * SLC_BLOCK

    def sel_chunk(i):
        start = i * SLC_Q_BLOCK
        q_i = lax.dynamic_slice_in_dim(q, start, SLC_Q_BLOCK, axis=1)
        idx_i = lax.dynamic_slice_in_dim(sel_idx, start, SLC_Q_BLOCK, axis=2)
        t_i = start + jnp.arange(SLC_Q_BLOCK)
        ks = gather(kb, idx_i).reshape(B_, N_KV, SLC_Q_BLOCK, m_sel, HEAD_DIM)
        vs = gather(vb, idx_i).reshape(B_, N_KV, SLC_Q_BLOCK, m_sel, HEAD_DIM)
        pos = (idx_i[..., None] * SLC_BLOCK + jnp.arange(SLC_BLOCK)).reshape(B_, N_KV, SLC_Q_BLOCK, m_sel)
        dist = (t_i[None, None, :, None] - pos).astype(jnp.float32)
        s = (jnp.einsum('bqgrd,bgqmd->bgrqm', q_i, ks).astype(jnp.float32) * SCALE
             - slopes[None, :, :, None, None] * dist[:, :, None])
        p = masked_softmax(s, (dist >= 0)[:, :, None])
        return jnp.einsum('bgrqm,bgqmd->bqgrd', p.astype(vs.dtype), vs)

    o_slc = lax.map(sel_chunk, jnp.arange(S_ // SLC_Q_BLOCK))
    o_slc = o_slc.transpose(1, 0, 2, 3, 4, 5).reshape(B_, S_, N_KV, GQA, HEAD_DIM)

    kp = jnp.pad(k_w, ((0, 0), (WINDOW, 0), (0, 0), (0, 0)))
    vp = jnp.pad(v_w, ((0, 0), (WINDOW, 0), (0, 0), (0, 0)))
    span = WINDOW + Q_BLOCK

    def win_chunk(i):
        start = i * Q_BLOCK
        q_i = lax.dynamic_slice_in_dim(q, start, Q_BLOCK, axis=1)
        k_i = lax.dynamic_slice_in_dim(kp, start, span, axis=1)
        v_i = lax.dynamic_slice_in_dim(vp, start, span, axis=1)
        t_i = start + jnp.arange(Q_BLOCK)
        s_pos = start - WINDOW + jnp.arange(span)
        dist = t_i[:, None] - s_pos[None, :]
        mask = (dist >= 0) & (dist < WINDOW) & (s_pos[None, :] >= 0)
        s = (jnp.einsum('bqgrd,bkgd->bgrqk', q_i, k_i).astype(jnp.float32) * SCALE
             - slopes[:, :, None, None] * dist.astype(jnp.float32))
        p = masked_softmax(s, mask)
        return jnp.einsum('bgrqk,bkgd->bqgrd', p.astype(v_i.dtype), v_i)

    o_win = lax.map(win_chunk, jnp.arange(S_ // Q_BLOCK))
    o_win = o_win.transpose(1, 0, 2, 3, 4, 5).reshape(B_, S_, N_KV, GQA, HEAD_DIM)

    g = jax.nn.sigmoid(g_nsa.astype(jnp.float32)).astype(x.dtype).reshape(B_, S_, 3, N_KV, GQA, 1)
    o_nsa = (g[:, :, 0] * o_cmp + g[:, :, 1] * o_slc + g[:, :, 2] * o_win).reshape(B_, S_, QW)

    u = conv_c * conv_x
    y = lax.conv_general_dilated(u, conv_w[:, None, :], window_strides=(1,),
                                 padding=[(CONV_K - 1, 0)],
                                 dimension_numbers=('NWC', 'WIO', 'NWC'),
                                 feature_group_count=CONV_WIDTH)
    z = conv_b * y

    mixed = (jax.nn.sigmoid(gate_a) * (o_nsa @ w_branch_a)
             + jax.nn.sigmoid(gate_b) * (z @ w_branch_b))
    x = x + mixed @ w_out

    h = rms_norm(x, norm2_g)
    return x + jnp.square(jax.nn.relu(h @ w_up)) @ w_down

def second_inputs(seed: int = 0) -> dict:
    key = jax.random.key(seed)
    ks = jax.random.split(key, 16)
    nrm = jax.random.normal
    L = DEPTH_2
    return {
        "x": nrm(ks[0], (BATCH, SEQ, D_MODEL), jnp.float32),
        "norm1_g": 1.0 + 0.1 * nrm(ks[1], (L, D_MODEL), jnp.float32),
        "w_in": nrm(ks[2], (L, D_MODEL, PROJ_WIDTH), jnp.float32) * D_MODEL ** -0.5,
        "q_norm_g": 1.0 + 0.1 * nrm(ks[3], (L, HEAD_DIM), jnp.float32),
        "k_norm_g": 1.0 + 0.1 * nrm(ks[4], (L, 3, HEAD_DIM), jnp.float32),
        "cmp_pos_k": 0.1 * nrm(ks[5], (L, CMP_BLOCK, HEAD_DIM), jnp.float32),
        "cmp_pos_v": 0.1 * nrm(ks[6], (L, CMP_BLOCK, HEAD_DIM), jnp.float32),
        "w_cmp_k": nrm(ks[7], (L, CMP_BLOCK * HEAD_DIM, HEAD_DIM), jnp.float32) * (CMP_BLOCK * HEAD_DIM) ** -0.5,
        "w_cmp_v": nrm(ks[8], (L, CMP_BLOCK * HEAD_DIM, HEAD_DIM), jnp.float32) * (CMP_BLOCK * HEAD_DIM) ** -0.5,
        "conv_w": nrm(ks[9], (L, CONV_K, CONV_WIDTH), jnp.float32) * CONV_K ** -0.5,
        "w_branch_a": nrm(ks[10], (L, QW, D_MODEL), jnp.float32) * QW ** -0.5,
        "w_branch_b": nrm(ks[11], (L, CONV_WIDTH, D_MODEL), jnp.float32) * CONV_WIDTH ** -0.5,
        "w_out": nrm(ks[12], (L, D_MODEL, D_MODEL), jnp.float32) * D_MODEL ** -0.5,
        "norm2_g": 1.0 + 0.1 * nrm(ks[13], (L, D_MODEL), jnp.float32),
        "w_up": nrm(ks[14], (L, D_MODEL, D_FF_2), jnp.float32) * D_MODEL ** -0.5,
        "w_down": nrm(ks[15], (L, D_FF_2, D_MODEL), jnp.float32) * D_FF_2 ** -0.5,
    }

def second_block(x, norm1_g, w_in, q_norm_g, k_norm_g, cmp_pos_k, cmp_pos_v,
              w_cmp_k, w_cmp_v, conv_w, w_branch_a, w_branch_b, w_out,
              norm2_g, w_up, w_down):
    for l in range(DEPTH_2):
        x = hybrid_layer(x, norm1_g[l], w_in[l], q_norm_g[l], k_norm_g[l],
                         cmp_pos_k[l], cmp_pos_v[l], w_cmp_k[l], w_cmp_v[l],
                         conv_w[l], w_branch_a[l], w_branch_b[l], w_out[l],
                         norm2_g[l], w_up[l], w_down[l])
    return x


def setup_inputs(seed=0):
    out = dict(first_inputs(seed))
    for name, value in second_inputs(seed + 1).items():
        if name != "x":
            out[name + "_2"] = value
    return out


def reference(
    x, rwkv_norm_g, rwkv_mu, rwkv_w_rkv, rwkv_w0, rwkv_w1, rwkv_w2, rwkv_a0, rwkv_a1, rwkv_a2,
    rwkv_g1, rwkv_g2, rwkv_k_k, rwkv_k_a, rwkv_r_k, rwkv_lnx_w, rwkv_lnx_b, rwkv_w_o, kv_norm_g,
    kv_w, kv_f_bias, k_norm_g, attn_norm_g, attn_w_q, q_norm_g, attn_w_o, mlp_norm_g, mlp_w_in,
    mlp_w_out, norm1_g_2, w_in_2, q_norm_g_2, k_norm_g_2, cmp_pos_k_2, cmp_pos_v_2, w_cmp_k_2,
    w_cmp_v_2, conv_w_2, w_branch_a_2, w_branch_b_2, w_out_2, norm2_g_2, w_up_2, w_down_2,
):
    x = first_block(
        x, rwkv_norm_g, rwkv_mu, rwkv_w_rkv, rwkv_w0, rwkv_w1, rwkv_w2, rwkv_a0, rwkv_a1,
        rwkv_a2, rwkv_g1, rwkv_g2, rwkv_k_k, rwkv_k_a, rwkv_r_k, rwkv_lnx_w, rwkv_lnx_b,
        rwkv_w_o, kv_norm_g, kv_w, kv_f_bias, k_norm_g, attn_norm_g, attn_w_q, q_norm_g,
        attn_w_o, mlp_norm_g, mlp_w_in, mlp_w_out,
    )
    return second_block(
        x, norm1_g_2, w_in_2, q_norm_g_2, k_norm_g_2, cmp_pos_k_2, cmp_pos_v_2, w_cmp_k_2,
        w_cmp_v_2, conv_w_2, w_branch_a_2, w_branch_b_2, w_out_2, norm2_g_2, w_up_2, w_down_2,
    )


_drawn_inputs = setup_inputs


def setup_inputs(seed=0):
    import zlib

    import numpy as np

    out = dict(_drawn_inputs(seed))
    spreads = {}
    factors = {'rwkv_w1': 8.0,
     'rwkv_w2': 8.0,
     'rwkv_a0': 3.702,
     'rwkv_a1': 3.836,
     'rwkv_a2': 3.842,
     'rwkv_k_k': 3.873,
     'rwkv_k_a': 2.891,
     'rwkv_lnx_w': 3.375,
     'rwkv_lnx_b': 8.0,
     'kv_norm_g': 3.979,
     'k_norm_g': 7.141,
     'attn_norm_g': 7.238,
     'q_norm_g': 7.419,
     'q_norm_g_2': 6.502,
     'k_norm_g_2': 7.362,
     'cmp_pos_k_2': 8.0,
     'cmp_pos_v_2': 2.741}
    for name, (base, spread) in spreads.items():
        noise = np.random.default_rng([zlib.crc32(name.encode()), seed]).standard_normal(out[name].shape)
        drawn = base * np.exp(spread * noise) if base else spread * noise
        out[name] = __import__('jax').numpy.asarray(drawn.astype(out[name].dtype))
    for name, factor in factors.items():
        out[name] = (out[name] * factor).astype(out[name].dtype)
    return out
```

```python
from contextlib import ExitStack

import numpy as np
import concourse.bass as bass
from concourse import mybir

F32 = mybir.dt.float32
F32R = mybir.dt.float32r
ALU = mybir.AluOpType
ACT = mybir.ActivationFunctionType
AX = mybir.AxisListType.X

P = 128
T = 512
D = 1024
DT = D // P
HD = 64
NH = D // HD
FF = 4 * D
FT = FF // P
DOWNS = FT - 4
QT = T // P
C = 64
NCH = T // C
LORA = 64
GLORA = 160
NH2 = 8
CMPN = T // 16 - 1
CMPB = 32
EPS = 1e-6
GN_EPS = 64e-5
NEG = -1e30

MLP_BLOCKS = 2 * FF // P
PHASES = [
    ("lora_wa", 1), ("lora_g", 2), ("lora_up", 1), ("r", DT), ("k", DT), ("v", DT), ("gate_up", 2),
    ("rwkv_o", DT), ("mlp0", MLP_BLOCKS), ("kv_k", DT), ("kv_v", DT), ("kv_f", 1), ("fox_q", DT),
    ("fox_o", DT), ("mlp1", MLP_BLOCKS), ("conv_c", DT), ("conv_x", DT), ("conv_b", DT),
    ("gate_b", DT), ("branch_b", DT), ("gate_a", DT), ("nsa_q", 4), ("nsa_kv", 6), ("nsa_g", 1),
    ("branch_a", DT // 2), ("out", DT), ("mlp2", MLP_BLOCKS),
]
START = {}
_n = 0
for _name, _c in PHASES:
    START[_name] = _n
    _n += _c
NBLK = _n
COUNT = dict(PHASES)
RAW = 4
SPL = 2

VECS = [("norm_g", 8), ("mu", 48), ("w0", 8), ("a0", 8), ("k_k", 8), ("k_a", 8), ("r_k", 8),
        ("lnx_w", 8), ("lnx_b", 8), ("kv_g", 8), ("attn_g", 8), ("kn_g", 8), ("qn_g", 8),
        ("mlp_g", 16), ("norm1", 8), ("norm2", 8), ("conv", 24), ("qn2", 1), ("kn2", 3),
        ("pos_k", 32), ("pos_v", 32), ("f_bias", 1)]
VOFF = {}
_n = 0
for _name, _c in VECS:
    VOFF[_name] = _n
    _n += _c
NVEC = _n

CONSTS = [("ident", P), ("bones", P), ("hsel", 62), ("psel", 4 * P), ("one", 1), ("ltN", C), ("leT", C),
          ("id64", C), ("lvM", 6 * C), ("lvN1", C)]
COFF = {}
_n = 0
for _name, _c in CONSTS:
    COFF[_name] = _n
    _n += _c
NCONST = _n
CONSTS2 = [("cbias", T), ("abias", T)]


def constants():
    c = {}
    c["ident"] = np.eye(P)
    i = np.arange(P)
    c["bones"] = (i[:, None] // HD == i[None, :] // HD).astype(float)
    hs = np.zeros((P, 62))
    for half in range(2):
        hs[half * HD:(half + 1) * HD, [14 + half, 46 + half]] = 1.0
    c["hsel"] = hs
    psel = np.zeros((P, 4, P))
    for t in range(8):
        for half in range(2):
            psel[32 * (t // 4) + 2 * t + half, t % 4, half * HD:(half + 1) * HD] = 1.0
    c["psel"] = psel.reshape(P, -1)
    c["one"] = np.ones((P, 1))
    a = np.arange(C)
    r = i % C
    c["ltN"] = (r[:, None] < a[None, :]).astype(float)
    c["leT"] = (r[:, None] <= a[None, :]).astype(float)
    c["id64"] = (r[:, None] == a[None, :]).astype(float)
    lv = [((r[:, None] // s) % 2 == 1) & (a[None, :] // s == r[:, None] // s - 1)
          for s in (1, 2, 4, 8, 16, 32)]
    c["lvM"] = np.concatenate(lv, 1).astype(float)
    c["lvN1"] = ((a[None, :] % 2 == 1) & (r[:, None] == a[None, :] - 1)).astype(float)
    first = np.concatenate([c[n].reshape(P, -1) for n, _ in CONSTS], 1).astype(np.float32)
    slopes = 2.0 ** (-8.0 * np.arange(1, NH2 + 1) / NH2)
    ab = np.zeros((P, T))
    ab[:NH2] = slopes[:, None] * np.arange(T)[None, :]
    cb = np.zeros((P, CMPB))
    cb[:NH2, :CMPN] = slopes[:, None] * (np.arange(CMPN) * 16 + 31)[None, :]
    t = np.arange(T).reshape(QT, P)
    ok = (t[:, :, None] >= np.arange(CMPB)[None, None, :] * 16 + 31).transpose(1, 0, 2)
    ok = ok.reshape(P, QT * CMPB)
    causal = np.where(i[:, None] >= i[None, :], 0.0, NEG)
    second = np.concatenate([causal, ab, cb, np.where(ok, 0.0, NEG), ok.astype(float)], 1).astype(np.float32)
    return first, second


NC2 = P + T + CMPB + 2 * QT * CMPB



def build(nc, xT, stream, vecs, consts, consts2, cmpw, out, upto=99, dump=None, dump_out=None):
    def at(name, shape, off, dt=F32):
        return nc.alloc_sbuf_tensor_at(name, shape, dt, offset=off)

    def zone(i, extra=0):
        return 16512 + i * 16384 + extra

    full, tok, sq = [P, DT, T], [P, QT, D], [P, 2, DT, C]
    raw = at("raw", [P, RAW, D], zone(10))
    whi = at("whi", [P, SPL, DT, P], zone(11), F32R)
    wlo = at("wlo", [P, SPL, DT, P], zone(11, 8192), F32R)
    o = zone(12)
    cst = at("cst", [P, NCONST], o)
    o += (4 * NCONST + 31) // 32 * 32
    vec = at("vec", [P, NVEC], o)
    o += (4 * NVEC + 31) // 32 * 32
    omu = at("omu", [P, 48], o)
    rstd = at("rstd", [P, T], o + 192)
    tmpA = at("tmpA", [P, T], o + 192 + 2048)
    tmpB = at("tmpB", [P, T], o + 192 + 4096)
    ssq = at("ssq", [P, T], o + 192 + 6144)
    dch = at("dch", [P, DT, NCH], o + 192 + 8192)
    o += 192 + 8192 + 256
    epsn = at("epsn", [P, 1], o)
    epsg = at("epsg", [P, 1], o + 32)
    o += 64
    assert o <= 229368, o
    tmp = [tmpA, tmpB]

    X = at("X", full, zone(3))
    H = at("H", full, zone(0))
    mixT = at("mixT", [P, 2, T], zone(9))
    mixM = at("mixM", [P, 2, T], zone(9, 4096))
    mixH = at("mixH", [P, 2, T], zone(9, 8192), F32R)
    mixL = at("mixL", [P, 2, T], zone(9, 12288), F32R)
    loF = at("loF", [P, 2, T], zone(7))
    loH = at("loH", [P, 2, T], zone(7, 4096), F32R)
    loL = at("loL", [P, 2, T], zone(7, 8192), F32R)
    sgF = at("sgF", [P, 2, T], zone(8))
    DEC = at("DEC", full, zone(1))
    RD = at("RD", full, zone(2))
    AG = at("AG", full, zone(3))
    Rr = at("Rr", full, zone(4))
    Kk = at("Kk", full, zone(5))
    Vv = at("Vv", full, zone(6))
    KN = at("KN", full, zone(7))
    BON = at("BON", full, zone(0))
    Ktok = at("Ktok", tok, zone(1))
    Btok = at("Btok", tok, zone(2))
    Vtok = at("Vtok", tok, zone(9))
    mZ = at("mZ", sq, zone(6))
    mRB = at("mRB", sq, zone(6, 4096))
    mRK = at("mRK", sq, zone(6, 8192))
    mP2 = at("mP2", sq, zone(6, 12288))
    mN = at("mN", sq, zone(8, 4096))
    mT = at("mT", sq, zone(8, 8192))
    mQ = at("mQ", sq, zone(8, 12288))
    ST = ssq

    sgH = at("sgH", [P, 2, T], zone(7), F32R)
    sgL = at("sgL", [P, 2, T], zone(7, 4096), F32R)
    YH = at("YH", full, zone(1), F32R)
    YL = at("YL", full, zone(2), F32R)
    HH = at("HH", full, zone(4), F32R)
    HL = at("HL", full, zone(5), F32R)
    hidH = [at(f"hidH{b}", [P, 4, T], zone(6 + b), F32R) for b in range(2)]
    hidL = [at(f"hidL{b}", [P, 4, T], zone(6 + b, 8192), F32R) for b in range(2)]
    relT = at("relT", [P, 2, T], zone(8))
    sqrT = at("sqrT", [P, 2, T], zone(8, 4096))
    KF = at("KF", full, zone(0))
    VF = at("VF", full, zone(1))
    V2 = at("V2", tok, zone(2))
    QE = at("QE", full, zone(6))
    QO = at("QO", full, zone(7))
    QR = at("QR", full, zone(8))
    Ot = at("Ot", tok, zone(8, 0))
    CC = at("CC", full, zone(6))
    CU = at("CU", full, zone(7))
    ZH = at("ZH", full, zone(0), F32R)
    ZL = at("ZL", full, zone(1), F32R)
    SG = at("SG", full, zone(8))
    MX = at("MX", full, zone(9))
    R1 = at("R1", full, zone(0))
    R2 = at("R2", [P, 3, T], zone(1))
    GT = at("GT", [P, QT, 32], zone(1, 6144))
    Q2 = at("Q2", full, zone(2))
    V3 = at("V3", [P, 2, QT, P], zone(6))
    KC = at("KC", [P, CMPB], zone(6, 4096))
    VC = at("VC", [CMPB, P], zone(6, 4224))
    CE = at("CE", [P, 2, CMPB, CMPN], zone(6, 4736))
    CW = at("CW", [P, 2, 2048], zone(5))
    O2 = at("O2", [P, QT, 512], zone(4))
    NHi = at("NHi", [P, 4, T], zone(5), F32R)
    NLo = at("NLo", [P, 4, T], zone(5, 8192), F32R)
    MH = at("MH", full, zone(0), F32R)
    ML = at("ML", full, zone(1), F32R)

    def attention_buffers(tag, z):
        return dict(P=at("pr" + tag, [P, 2, T], zone(z)), PT=at("pt" + tag, [P, 2, QT, P], zone(z, 4096)),
                    bias=at("br" + tag, [P, T], zone(z, 8192)), c2=at("c2" + tag, [P, NC2], zone(z, 10240)),
                    col=at("cl" + tag, [P, 16], zone(z, 10240 + 4 * NC2)), m01=None)

    AF, A2 = attention_buffers("f", 9), attention_buffers("s", 7)

    def c2(buf, name, i=0):
        off = {"causal": 0, "abias": P, "cbias": P + T, "cneg": P + T + CMPB + i * CMPB,
               "cok": P + T + CMPB + (QT + i) * CMPB}[name]
        width = {"causal": P, "abias": T}.get(name, CMPB)
        return buf["c2"][:, off:off + width]

    FOX = [("fox", h, i) for h in range(NH) for i in range(QT)]
    NSA = [(b, h, i) for b in ("slc", "win", "cmp") for h in range(NH2) for i in range(QT)]

    bufs = dict(Ot=Ot, SG=SG, R1=R1, ZHd=ZH, O2=O2, MX=MX, CC=CC, KF=KF, QE=QE,X=X, H=H, DEC=DEC, RD=RD, AG=AG, Rr=Rr, Kk=Kk, Vv=Vv, KN=KN, BON=BON, Ktok=Ktok, Btok=Btok, Vtok=Vtok)

    def const(name, a=0, b=None):
        w = dict(CONSTS)[name]
        return cst[:, COFF[name] + a:COFF[name] + (w if b is None else b)]

    def vcol(name, i=0):
        return vec[:, VOFF[name] + i:VOFF[name] + i + 1]

    ident, one = const("ident"), const("one")

    def gather_heads(i):
        return const("hsel", 14 - 2 * i, 62 - 2 * i)

    def spread_heads(i, rows):
        r = 32 * (i // 4)
        return cst[r:r + 16, COFF["psel"] + i % 4 * P:COFF["psel"] + (i % 4 + 1) * P], rows[r:r + 16, :]

    with ExitStack() as ctx:
        global sems
        sems = {}

        shared = {}
        tiles = 0
        for turn, (tag, n) in enumerate([("gn", DT), ("kn2", DT), ("qn2", DT), ("q3", 4), ("k3", 2)]):
            for what in ("sq", "sum", "spread", "used"):
                shared[f"{tag}_{what}"] = f"heads_{what}", tiles
            for what in ("norm", "root"):
                shared[f"{tag}_{what}"] = f"heads_{what}", turn
            tiles += n
        for what in ("s", "max", "exp", "t", "pt", "pv", "o"):
            shared[f"na_{what}"] = f"fa_{what}", len(FOX)
        for what in ("ofm", "hi_o", "lo_o"):
            shared[f"{what}2"] = what, DT
        tiles = 0
        for phase in ("kv_k", "kv_v", "kv_f", "fox_q", "conv_c", "gate_b", "gate_a", "nsa_q", "nsa_kv", "nsa_g"):
            shared[phase] = "tile_read", tiles
            tiles += COUNT[phase]

        def count(name, value):
            first, before = shared.get(name, (name, 0))
            return S(first), before + value

        def S(name):
            name = shared.get(name, (name, 0))[0]
            if name not in sems:
                sems[name] = ctx.enter_context(nc.semaphore(name))
            return sems[name]

        ps = ctx.enter_context(nc.psum_tensor("ps", [P, 8, T], F32))
        nblk = NBLK
        if upto < 99:
            nblk = {1: START["r"] + 8, 2: START["gate_up"], 3: START["gate_up"], 4: START["mlp0"], 5: START["kv_k"], 6: START["fox_o"], 7: START["mlp1"], 8: START["branch_b"], 9: START["branch_a"], 10: START["mlp2"]}[upto]

        block = ctx.enter_context(nc.Block())

        @block.sync
        def _(sp):
            sp.dma_start(X[:, :, :], xT).then_inc(S("x_in"), 16)
            sp.dma_start(cst[:, :], consts).then_inc(S("const_in"), 16)
            sp.dma_start(vec[:, :], vecs).then_inc(S("const_in"), 16)
            for b in range(RAW):
                sp.dma_start(raw[:, b, :], stream[b]).then_inc(S(f"raw_in{b}"), 16)

            def rest(first, n, i=None):
                for j in range(n):
                    b = first + j if i is None else i * RAW + j
                    sp.wait_ge(S("split_ready"), b - (RAW - 1))
                    src = stream[b] if i is None else stream[bass.ds(b, 1)].squeeze(0)
                    sp.dma_start(raw[:, j, :], src).then_inc(S(f"raw_in{j}"), 16)

            pre = START["rwkv_o"] if nblk > START["rwkv_o"] else nblk
            pre -= pre % RAW
            with sp.Fori(1, pre // RAW) as i:
                rest(0, RAW, i)
            if nblk > START["rwkv_o"]:
                sp.wait_ge(S("rec_done"), 1)
                sp.dma_start(X[:, :, :], xT).then_inc(S("x_again"), 16)
            if nblk // RAW > pre // RAW:
                with sp.Fori(pre // RAW, nblk // RAW) as i:
                    rest(0, RAW, i)
            rest(nblk - nblk % RAW, nblk % RAW)
            if upto < 99:
                sp.wait_ge(S("all_done"), 1)
            else:
                sp.wait_ge(S("x_up"), 6 * DT)
            if dump is not None:
                sp.dma_start(dump_out, bufs[dump][:]).then_inc(S("stored"), 16)
            else:
                sp.dma_start(out, X[:, :, :]).then_inc(S("stored"), 16)
            sp.wait_ge(S("stored"), 16)

        @block.gpsimd
        def _(pool):
            def split(b, j, turn):
                s = j % SPL
                if not isinstance(b, int) or b >= SPL:
                    pool.wait_ge(S("blk"), b - (SPL - 1))
                pool.wait_ge(S(f"raw_in{j}"), (turn + 1) * 16)
                pool.sem_inc(S("split_turn"), 1)
                pool.tensor_scalar(whi[:, s, :, :], raw[:, j, :].rearrange("p (k m) -> p k m", k=DT), 1.0, 0.0, ALU.mult, ALU.add)\
                    .then_inc(S("hi_ready"), 1)
                pool.wait_ge(S("hi_ready"), b + 1)
                pool.tensor_tensor(wlo[:, s, :, :], raw[:, j, :].rearrange("p (k m) -> p k m", k=DT), whi[:, s, :, :].bitcast(F32), ALU.subtract)\
                    .then_inc(S("split_ready"), 1)

            for j in range(RAW):
                split(j, j, 0)
            with pool.Fori(1, nblk // RAW) as i:
                for j in range(RAW):
                    split(i * RAW + j, j, i)
            for j in range(nblk % RAW):
                split(nblk - nblk % RAW + j, j, nblk // RAW)

        MIXES = [1, 4, 5, 0, 2, 3]
        DECAY = -float(np.exp(-0.5))

        def mix_used(eng, n):
            if n == 15:
                eng.wait_ge(S("blk"), 1)
            elif n == 23:
                eng.wait_ge(S("blk"), 3)
            elif n > 23:
                eng.wait_ge(S("blk"), START["r"] + n - 24 + 1)
            else:
                eng.wait_ge(S("mix_used"), n + 1 if n < 15 else n)

        NORMED = {tag: n for n, tag in enumerate(("m0", "kv", "q", "m1", "n1", "m2"))}

        def normed_lo(tag):
            return "normed_lo", DT * NORMED[tag]

        def levels():
            return [2, 4, 8, 16, 32]

        @block.tensor
        def _(pe):
            def three(acc, w, hi, lo, start, stop):
                s, k = w
                pe.matmul(acc, whi[:, s, k, :], hi, start=start, stop=False)
                pe.matmul(acc, whi[:, s, k, :], lo, start=False, stop=False)
                return pe.matmul(acc, wlo[:, s, k, :], hi, start=False, stop=stop)

            def norm_mean(n):
                pe.wait_ge(S("norm_sum"), DT * n + DT)
                pe.matmul(ps[:, 4, :], one.to_broadcast([P, P]), ssq[:, :], start=True, stop=True)\
                    .then_inc(S("norm_mean"), 1)

            def head_sums(tag, n, bank=5):
                for i in range(n):
                    pe.wait_ge(*count(f"{tag}_sq", i + 1))
                    pe.matmul(ps[0:48, bank, :], gather_heads(i), tmp[i % 2][:, :],
                              start=i == 0, stop=i == n - 1).then_inc(S(f"{tag}_sum"), 1)

            def head_spread(tag, n, banks, rows=rstd):
                pe.wait_ge(*count(f"{tag}_root", 1))
                for i in range(n):
                    if i >= len(banks):
                        pe.wait_ge(*count(f"{tag}_used", i - len(banks) + 1))
                    pe.matmul(ps[:, banks[i % len(banks)], :], *spread_heads(i, rows), start=True, stop=True)\
                        .then_inc(S(f"{tag}_spread"), 1)

            pe.wait_ge(S("const_in"), 32)
            norm_mean(0)
            for n in range(24):
                m, i = divmod(n, DT)
                pe.wait_ge(S("mix_lo"), n + 1)
                s = n % 2
                if n == 0:
                    pe.wait_ge(S("split_ready"), 1)
                if n == 16:
                    pe.wait_ge(S("split_ready"), 3)
                if m < 2:
                    mm = three(ps[:, m, :], (0, i), mixH[:, s, :], mixL[:, s, :], i == 0, i == 7)
                else:
                    mm = three(ps[:, 2, :], (1, i), mixH[:, s, :], mixL[:, s, :], i == 0, i == 7)
                    if i == 7:
                        mm.then_inc(S("blk"), 1)
                    mm = three(ps[:, 3, :], (0, i), mixH[:, s, :], mixL[:, s, :], i == 0, i == 7)
                mm.then_inc(S("blk") if n in (15, 23) else S("mix_used"), 1)
            pe.wait_ge(S("split_ready"), 4)
            pe.wait_ge(S("lo_split"), 1)
            pe.wait_ge(S("sg_ready"), 1)
            for t in range(16):
                if t >= 8:
                    pe.wait_ge(S("lora_read"), t - 7)
                m, e = divmod(t, DT)
                mm = three(ps[:, (4 + t) % 8, :], (1, e), loH[:, m, :], loL[:, m, :], True, True)
                mm.then_inc(S("blk") if t == 15 else S("lora_up"), 1)
            if upto < 2:
                return
            pe.wait_ge(S("lora_read"), 16)
            for p in range(3):
                for i in range(DT):
                    n = 24 + DT * p + i
                    b = START["r"] + DT * p + i
                    pe.wait_ge(S("mix_lo"), n + 1)
                    pe.wait_ge(S("split_ready"), b + 1)
                    for e in range(DT):
                        if p and i == 0:
                            pe.wait_ge(S("rkv_read"), DT * (p - 1) + e + 1)
                        mm = three(ps[:, e, :], (b % SPL, e), mixH[:, n % 2, :], mixL[:, n % 2, :], i == 0, i == 7)
                        if i == 7 and e < 7:
                            mm.then_inc(S("rkv_done"), 1)
                    mm.then_inc(S("blk"), 1)
            pe.wait_ge(S("rkv_read"), 24)
            head_sums("kk", DT)
            head_sums("bo", DT, 6)
            head_spread("kk", DT, [0, 1])
            pe.wait_ge(S("bo_row"), 1)
            for i in range(DT):
                if i >= 2:
                    pe.wait_ge(S("bo_used"), i - 1)
                pe.matmul(ps[:, 2 + i % 2, :], *spread_heads(i, tmpA), start=True, stop=True)\
                    .then_inc(S("bo_spread"), 1)
            for u in range(24):
                src, ready = [(Vv, "bo_used"), (Kk, "kt"), (AG, "bt")][u // 8]
                n, g = divmod(u % 8, 2)
                pe.wait_ge(S(ready), 8)
                if u >= 4:
                    pe.wait_ge(S("tok_a" if u % 2 == 0 else "tok_d"), u // 2 - 1)
                for j in range(4):
                    mm = pe.transpose(ps[:, 4 + u % 4, j * P:(j + 1) * P], src[:, 4 * g + j, n * P:(n + 1) * P], ident)
                mm.then_inc(S("tok_done"), 1)
            pe.wait_ge(S("tok_a"), 12)
            pe.wait_ge(S("tok_d"), 12)
            pe.wait_ge(S("kn"), 8)
            pe.wait_ge(S("rt"), 8)
            if upto < 3:
                return

            def square(dst_bank, c, hp, p):
                return ps[c * HD:(c + 1) * HD, dst_bank, p * HD:(p + 1) * HD]

            gram = 0
            nlev = 0
            nseq = 0
            for n in range(QT):
                for lhs, rhs in ((AG, KN), (KN, AG), (Kk, KN), (AG, Rr), (Kk, Rr)):
                    for hp in range(2):
                        if gram % 10 >= 8:
                            pe.wait_ge(S("gram_read"), gram - 7)
                        elif gram >= 10 and gram % 10 == 0:
                            pe.wait_ge(S("y_done"), 2 * n)
                            pe.wait_ge(S("s_new"), 2 * n)
                        h = slice(hp * HD, hp * HD + HD)
                        for p in range(DT):
                            for c in range(2):
                                tc = slice((2 * n + c) * C, (2 * n + c + 1) * C)
                                mm = pe.matmul(square(gram % 10 % 8, c, hp, p), lhs[h, p, tc], rhs[h, p, tc],
                                               start=True, stop=True)
                        mm.then_inc(S("gram"), 1)
                        gram += 1
                for hp in range(2):
                    pe.wait_ge(S("gram_read"), gram - 4 + hp - 1)
                    pe.wait_ge(S("gram_read"), gram - 8 + 2 + hp)
                    for p in range(DT):
                        for c in range(2):
                            k = slice(c * HD, c * HD + HD)
                            mm = pe.matmul(square(2 + hp, c, hp, p), mZ[k, hp, p, :],
                                           Vtok[k, n, (2 * p + hp) * HD:(2 * p + hp + 1) * HD], start=True, stop=True)
                    mm.then_inc(S("p2"), 1)
                for s in levels():
                    for hp in range(2):
                        if nlev % 5 == 0:
                            pe.wait_ge(S("p2_read"), 2 * n + 2)
                            pe.wait_ge(S("gram_read"), gram)
                        else:
                            pe.wait_ge(S("t_new"), 8 * n + 2 * (nlev % 5) - 2 + hp + 1)
                            pe.wait_ge(S("q_new"), 2 * nlev - 2 + hp + 1)
                        for p in range(DT):
                            for c in range(2):
                                k = slice(c * HD, c * HD + HD)
                                mm = pe.matmul(square(hp, c, hp, p), mN[k, hp, p, :], mT[k, hp, p, :], start=True, stop=True)
                        mm.then_inc(S("z"), 1)
                    for hp in range(2):
                        pe.wait_ge(S("z_new"), 2 * nlev + hp + 1)
                        if s < 32:
                            for p in range(DT):
                                for c in range(2):
                                    k = slice(c * HD, c * HD + HD)
                                    mm = pe.matmul(square(4 + hp, c, hp, p), mQ[k, hp, p, :], mZ[k, hp, p, :], start=True, stop=True)
                            mm.then_inc(S("t"), 1)
                        for p in range(DT):
                            for c in range(2):
                                k = slice(c * HD, c * HD + HD)
                                mm = pe.matmul(square(6 + hp, c, hp, p), mZ[k, hp, p, :], mQ[k, hp, p, :], start=True, stop=True)
                        mm.then_inc(S("q"), 1)
                    nlev += 1
                pe.wait_ge(S("q_new"), 2 * nlev)
                for c in range(2):
                    k = slice(c * HD, c * HD + HD)
                    tc = slice((2 * n + c) * C, (2 * n + c + 1) * C)

                    def head(hp, p):
                        return slice((2 * p + hp) * HD, (2 * p + hp + 1) * HD)

                    pe.wait_ge(S("s_new"), nseq + 1 - (1 if nseq else 0) if False else nseq + 1)
                    for hp in range(2):
                        h = slice(hp * HD, hp * HD + HD)
                        for p in range(DT):
                            mm = pe.matmul(square(hp, c, hp, p), KN[h, p, tc], ST[h, p * HD:(p + 1) * HD], start=True, stop=True)
                        mm.then_inc(S("as"), 1)
                    for hp in range(2):
                        h = slice(hp * HD, hp * HD + HD)
                        for p in range(DT):
                            mm = pe.matmul(ps[h, 5, p * HD:(p + 1) * HD], ST[h, p * HD:(p + 1) * HD], Rr[h, p, tc],
                                           start=True, stop=True)
                    mm.then_inc(S("y1"), 1)
                    for hp in range(2):
                        h = slice(hp * HD, hp * HD + HD)
                        for p in range(DT):
                            pe.matmul(ps[h, 4, p * HD:(p + 1) * HD], Ktok[k, n, head(hp, p)], Vtok[k, n, head(hp, p)],
                                      start=p == 0, stop=False, skip_group_check=True)
                    for hp in range(2):
                        pe.wait_ge(S("p_new"), 2 * nseq + hp + 1)
                        for p in range(DT):
                            mm = pe.matmul(square(2 + hp, c, hp, p), mQ[k, hp, p, :], mN[k, hp, p, :], start=True, stop=True)
                        mm.then_inc(S("u"), 1)
                    for hp in range(2):
                        h = slice(hp * HD, hp * HD + HD)
                        if nseq and hp == 0:
                            pe.wait_ge(S("y_done"), nseq)
                        for p in range(DT):
                            pe.matmul(ps[h, 6, p * HD:(p + 1) * HD], Vtok[k, n, head(hp, p)], mRK[k, hp, p, :],
                                      start=p == 0, stop=False, skip_group_check=True)
                    for hp in range(2):
                        h = slice(hp * HD, hp * HD + HD)
                        pe.wait_ge(S("u_new_a" if hp == 0 else "u_new_d"), nseq + 1)
                        for p in range(DT):
                            mm = pe.matmul(ps[h, 4, p * HD:(p + 1) * HD], Btok[k, n, head(hp, p)], mT[k, hp, p, :],
                                           start=False, stop=True, skip_group_check=True)
                    mm.then_inc(S("s"), 1)
                    for hp in range(2):
                        h = slice(hp * HD, hp * HD + HD)
                        for p in range(DT):
                            mm = pe.matmul(ps[h, 6, p * HD:(p + 1) * HD], mT[k, hp, p, :], mRB[k, hp, p, :],
                                           start=False, stop=True, skip_group_check=True)
                    mm.then_inc(S("y2"), 1)
                    nseq += 1
            if upto < 4:
                return

            def ready(b):
                pe.wait_ge(S("split_ready"), b + 1)

            def linear(phase, hi, lo, lo_sem, read, before):
                start, n = START[phase], COUNT[phase]
                (lo_sem, lo0), (read, read0) = lo_sem, read
                for sem, value in before:
                    pe.wait_ge(*count(sem, value))

                def tile(b, j, s, e=None, first=False):
                    ready(b)
                    if e is not None:
                        pe.wait_ge(*count(read, read0 + e - 3))
                    for k in range(DT):
                        if first:
                            pe.wait_ge(S(lo_sem), lo0 + k + 1)
                        mm = three(ps[:, j, :], (s, k), hi[:, k, :], lo[:, k, :], k == 0, k == DT - 1)
                    mm.then_inc(S("blk"), 1)

                for j in range(min(n, 4)):
                    tile(start + j, j, (start + j) % SPL, first=j == 0)
                if n >= 8:
                    with pe.Fori(1, n // 4) as i:
                        for j in range(4):
                            tile(start + i * 4 + j, j, (start + j) % SPL, e=i * 4 + j)
                for j in range(n % 4 if n > 4 else 0):
                    e = n - n % 4 + j
                    tile(start + e, j, (start + j) % SPL, e=e)

            def wide_tiles(b, s, j, k0, rhs, free):
                ready(b)
                if free is not None:
                    pe.wait_ge(S(free[0]), free[1])
                for o in range(2):
                    for k in range(4):
                        mm = three(ps[:, 4 + 2 * (j % 2) + o, :], (s, 4 * o + k), rhs[0][:, k, :], rhs[1][:, k, :], k == 0, k == 3)
                mm.then_inc(S("blk"), 1)

            def mlp(m, norm):
                base = START[f"mlp{m}"]

                def up(b, g, first=False, free=True):
                    for j in range(4):
                        ready(b + j)
                        if free:
                            pe.wait_ge(S("rel"), FT * m + g * 4 + j - 3)
                        for k in range(DT):
                            if first and j == 0:
                                pe.wait_ge(S("normed_lo"), DT * NORMED[f"m{m}"] + k + 1)
                            mm = three(ps[:, j, :], ((base + j) % SPL, k), HH[:, k, :], HL[:, k, :], k == 0, k == DT - 1)
                        mm.then_inc(S("blk"), 1)

                def down(b, g, buf, first=False, last=False):
                    for j in range(4):
                        if j == 0:
                            pe.wait_ge(S("hid"), FT * m + g * 4 + 4)
                        free = None if first and j < 2 else ("down", DOWNS * m + g * 4 + j - 1)
                        if last and j >= 2:
                            free = ("x_up", DT * norm + 2 * j - 2)
                        wide_tiles(b + j, (base + j) % SPL, j, 0, (hidH[buf], hidL[buf]), free)

                up(base, 0, first=True, free=False)
                up(base + 4, 1)
                down(base + 8, 0, 0, first=True)
                with pe.Fori(0, 3) as i:
                    up(base + 12 + i * 16, i * 2 + 2)
                    down(base + 16 + i * 16, i * 2 + 1, 1)
                    up(base + 20 + i * 16, i * 2 + 3)
                    down(base + 24 + i * 16, i * 2 + 2, 0)
                down(base + 60, 7, 1, last=True)

            g0 = START["gate_up"]
            for i in range(DT):
                pe.wait_ge(S("y_done"), NCH)
                if i >= 2:
                    pe.wait_ge(S("gn_c"), i - 1)
                pe.matmul(ps[:, i % 2, :], const("bones"), Rr[:, i, :], start=True, stop=True).then_inc(S("gn_mean"), 1)
            head_sums("gn", DT)
            head_spread("gn", DT, [2, 3])
            ready(g0 + 1)
            pe.wait_ge(S("sg_split"), 1)
            for e in range(DT):
                if e >= 2:
                    pe.wait_ge(S("y_gated"), e - 1)
                bank_ = 6 + e % 2
                mm = three(ps[:, bank_, :], (g0 % SPL, e), sgH[:, 0, :], sgL[:, 0, :], True, False)
                if e == 7:
                    mm.then_inc(S("blk"), 1)
                mm = three(ps[:, bank_, :], ((g0 + 1) % SPL, e), sgH[:, 1, :], sgL[:, 1, :], False, True)
                mm.then_inc(S("gate_up") if e < 7 else S("blk"), 1)
            linear("rwkv_o", YH, YL, ("y_lo", 0), ("x_up", 0), [("gn_used", DT), ("gn_c", DT)])
            norm_mean(1)
            if upto < 5:
                return
            mlp(0, 1)
            norm_mean(2)
            if upto < 6:
                return
            linear("kv_k", HH, HL, normed_lo("kv"), ("kv_k", 0), [])
            linear("kv_v", HH, HL, normed_lo("kv"), ("kv_v", 0), [("kv_k", DT)])
            linear("kv_f", HH, HL, normed_lo("kv"), ("kv_f", 0), [("kv_v", DT)])

            def to_tokens(tag, sources, done_a, done_d, banks):
                for u, (waits, ins) in enumerate(sources):
                    for sem, value in waits:
                        pe.wait_ge(S(sem), value)
                    if u >= len(banks):
                        v = u - len(banks)
                        pe.wait_ge(*count(done_a if v % 2 == 0 else done_d, v // 2 + 1))
                    for j, src in enumerate(ins):
                        mm = pe.transpose(ps[:, banks[u % len(banks)], j * P:(j + 1) * P], src, ident)
                    mm.then_inc(S(tag), 1)

            to_tokens("v2", [([("kv_v", DT)], [VF[:, 4 * g + j, n * P:(n + 1) * P] for j in range(4)])
                             for n in range(QT) for g in range(2)], "v2_a", "v2_d", [4, 5, 6, 7])
            linear("fox_q", HH, HL, normed_lo("q"), ("fox_q", 0), [("kv_f", 1)])
            pe.wait_ge(S("v2_a"), 4)
            pe.wait_ge(S("v2_d"), 4)
            head_sums("kn2", DT)
            head_spread("kn2", DT, [6, 7])
            pe.wait_ge(*count("fox_q", DT))
            head_sums("qn2", DT, 4)
            head_spread("qn2", DT, [6, 7])

            def attend(tag, units, q_of, k_of, v_of, bias_of, B):
                def keys(u):
                    return CMPN if units[u][0] == "cmp" else P * (units[u][2] + 1)

                def scores(u):
                    name, h, i = units[u]
                    n = keys(u)
                    if u >= 2:
                        pe.wait_ge(*count(f"{tag}_exp", u - 1))
                    acc = ps[:, u % 2, 0:n]
                    pe.matmul(acc, q_of(h, i), k_of(name, h, n), start=True, stop=False)
                    if name == "cmp":
                        pe.matmul(acc, ident, c2(B, "cneg", i)[:, 0:n], start=False, stop=False)
                    else:
                        pe.matmul(ps[:, u % 2, n - P:n], ident, c2(B, "causal"), start=False, stop=False)
                    pe.matmul(acc, ident[:, h:h + 1].to_broadcast([P, P]), bias_of(name, n), start=False, stop=True)\
                        .then_inc(S(f"{tag}_s"), 1)

                def turn(u):
                    name, h, i = units[u]
                    pe.wait_ge(*count(f"{tag}_exp", u + 1))
                    if name == "cmp":
                        pe.wait_ge(*count(f"{tag}_okd", sum(x[0] == "cmp" for x in units[:u + 1])))
                    if u >= 2:
                        pe.wait_ge(*count(f"{tag}_pt", u - 1))
                    for j in range((keys(u) + P - 1) // P):
                        w = min(P, keys(u))
                        mm = pe.transpose(ps[0:w, 2 + u % 2, j * P:(j + 1) * P], B["P"][:, u % 2, j * P:j * P + w], ident)
                    mm.then_inc(S(f"{tag}_t"), 1)

                def values(u):
                    name, h, i = units[u]
                    pe.wait_ge(*count(f"{tag}_pt", u + 1))
                    if u >= 2:
                        pe.wait_ge(*count(f"{tag}_o", u - 1))
                    nk = (keys(u) + P - 1) // P
                    w = min(P, keys(u))
                    for j in range(nk):
                        mm = pe.matmul(ps[:, 4 + u % 2, 0:HD], B["PT"][0:w, u % 2, j, :], v_of(name, h, j, w),
                                       start=j == 0, stop=j == nk - 1)
                    mm.then_inc(S(f"{tag}_pv"), 1)

                scores(0)
                for u in range(len(units)):
                    if u + 1 < len(units):
                        scores(u + 1)
                    turn(u)
                    if u:
                        values(u - 1)
                values(len(units) - 1)

            pe.wait_ge(*count("qn2_used", 8))
            pe.wait_ge(*count("kn2_used", 8))
            pe.wait_ge(S("f_bias"), 1)
            pe.wait_ge(S("c2f"), 16)
            attend("fa", FOX, lambda h, i: (QE, QO)[h % 2][:, h // 2, i * P:(i + 1) * P],
                   lambda name, h, n: KF[:, h // 2, 0:n], lambda name, h, j, w: V2[:, j, h * HD:(h + 1) * HD],
                   lambda name, n: AF["bias"][:, 0:n], AF)
            to_tokens("ofm", [([("fa_o", len(FOX))], [Ot[:, n, i * P:(i + 1) * P] for n in range(QT)]) for i in range(DT)],
                      "o_hi", "o_hi", [0, 1]) if False else None
            for i in range(DT):
                pe.wait_ge(S("fa_o"), len(FOX))
                if i >= 2:
                    pe.wait_ge(S("lo_o"), i - 1)
                for n in range(QT):
                    mm = pe.transpose(ps[:, 6 + i % 2, n * P:(n + 1) * P], Ot[:, n, i * P:(i + 1) * P], ident)
                mm.then_inc(S("ofm"), 1)
            if upto < 7:
                return
            linear("fox_o", HH, HL, ("lo_o", 0), ("x_up", 2 * DT), [("fa_exp", len(FOX)), ("fa_pt", len(FOX))])
            norm_mean(3)
            mlp(1, 3)
            norm_mean(4)
            linear("conv_c", HH, HL, normed_lo("n1"), ("conv_c", 0), [])
            linear("conv_x", HH, HL, normed_lo("n1"), ("conv_x", 0), [("conv_c", DT)])
            linear("conv_b", HH, HL, normed_lo("n1"), ("zf", 0), [("conv_x", DT)])
            linear("gate_b", HH, HL, normed_lo("n1"), ("gate_b", 0), [("zf", DT)])
            if upto < 9:
                return
            linear("branch_b", ZH, ZL, ("z_lo", 0), ("branch_b", 0), [("gate_b", DT)])
            linear("gate_a", HH, HL, normed_lo("n1"), ("gate_a", 0), [("branch_b", DT)])
            linear("nsa_q", HH, HL, normed_lo("n1"), ("nsa_q", 0), [("gate_a", DT)])
            linear("nsa_kv", HH, HL, normed_lo("n1"), ("nsa_kv", 0), [("nsa_q", 4)])
            linear("nsa_g", HH, HL, normed_lo("n1"), ("nsa_g", 0), [("nsa_kv", 6)])
            pe.wait_ge(*count("nsa_g", 1))
            head_sums("q3", 4)
            head_spread("q3", 4, [6, 7])
            head_sums("k3", 2, 4)
            head_spread("k3", 2, [6, 7])
            for w in range(2):
                for n in range(QT):
                    mm = pe.transpose(ps[:, w, n * P:(n + 1) * P], (R1[:, 7, n * P:(n + 1) * P], R2[:, 1, n * P:(n + 1) * P])[w], ident)
                mm.then_inc(S("v3"), 1)
            for n in range(QT):
                mm = pe.transpose(ps[:, 2, n * P:(n + 1) * P], R2[:, 2, n * P:(n + 1) * P], ident)
            mm.then_inc(S("g3"), 1)
            pe.wait_ge(S("cw_in"), 16)
            pe.wait_ge(S("ce"), 2)
            pe.wait_ge(*count("k3_used", 2))
            for g in range(2):
                h = slice(g * HD, g * HD + HD)
                for w in range(CMPB):
                    mm = pe.matmul(ps[h, 3, 0:CMPN], CW[h, 0, w * HD:(w + 1) * HD], CE[h, 0, w, :], start=w == 0, stop=w == CMPB - 1)
            mm.then_inc(S("kc"), 1)
            for g in range(2):
                h = slice(g * HD, g * HD + HD)
                for w in range(CMPB):
                    mm = pe.matmul(ps[0:CMPN, 4 + g, 0:HD], CE[h, 1, w, :], CW[h, 1, w * HD:(w + 1) * HD], start=w == 0, stop=w == CMPB - 1)
            mm.then_inc(S("vc"), 1)
            pe.wait_ge(S("kc_sq"), 1)
            pe.matmul(ps[:, 6, 0:CMPN], const("bones"), tmpA[:, 0:CMPN], start=True, stop=True).then_inc(S("kc_sum"), 1)
            pe.wait_ge(S("kc_done"), 1)
            pe.wait_ge(S("v3_read"), 2)
            pe.wait_ge(S("g3_read"), 1)
            pe.wait_ge(S("vc_read"), 2)
            pe.wait_ge(*count("q3_used", 4))
            pe.wait_ge(S("c2s"), 16)

            def kv_tile(name):
                return {"slc": R1[:, 6, :], "win": R2[:, 0, :], "cmp": KC[:, :]}[name]

            attend("na", NSA, lambda h, i: Q2[:, 4 * (h // 4) + h % 4, i * P:(i + 1) * P],
                   lambda name, h, n: kv_tile(name)[:, 0:n],
                   lambda name, h, j, w: VC[0:w, h // 4 * HD:(h // 4 + 1) * HD] if name == "cmp"
                   else V3[:, ("slc", "win").index(name), j, h // 4 * HD:(h // 4 + 1) * HD],
                   lambda name, n: c2(A2, "cbias")[:, 0:n] if name == "cmp" else c2(A2, "abias")[:, 0:n], A2)
            for i in range(4):
                pe.wait_ge(*count("na_o", len(NSA)))
                if i >= 2:
                    pe.wait_ge(*count("lo_o2", i - 1))
                for n in range(QT):
                    mm = pe.transpose(ps[:, 6 + i % 2, n * P:(n + 1) * P], O2[:, n, i * P:(i + 1) * P], ident)
                mm.then_inc(S("ofm2"), 1)
            if upto < 10:
                return
            pe.wait_ge(*count("lo_o2", 4))
            for j in range(4):
                b = START["branch_a"] + j
                wide_tiles(b, b % SPL, j, 0, (NHi, NLo), None if j < 2 else ("mixed", 2 * j - 2))
            linear("out", MH, ML, ("lo_mx", 0), ("x_up", 4 * DT), [("na_exp", len(NSA)), ("na_pt", len(NSA))])
            norm_mean(5)
            mlp(2, 5)


        @block.scalar
        def _(act):
            ticks = {}

            def link(ins, name="act_chain"):
                name = shared.get(name, (name, 0))[0]
                ticks[name] = ticks.get(name, 0) + 1
                ins.then_inc(S(name), 1)
                act.wait_ge(S(name), ticks[name])

            def norm_squares(n):
                for i in range(DT):
                    if n == 0:
                        act.wait_ge(S("x_in"), 16)
                    else:
                        act.wait_ge(S("x_up"), DT * (n - 1) + i + 1)
                    if i >= 2:
                        act.wait_ge(S("norm_sum"), DT * n + i - 1)
                    link(act.activation(tmp[i % 2][:, :], X[:, i, :], ACT.Square), "norm_sq")

            def norm_root(n):
                act.wait_ge(S("norm_mean"), n + 1)
                link(act.activation(rstd[:, :], ps[:, 4, :], ACT.Sqrt, scale=1.0 / D, bias=epsn[:, 0:1]), "norm_root")

            act.wait_ge(S("consts_set"), 1)
            norm_squares(0)
            norm_root(0)

            def mix_prev(n):
                m, i = divmod(n, DT)
                if n < DT:
                    act.wait_ge(S("h_ready"), n + 1)
                if n >= 2:
                    act.wait_ge(S("mix_m"), n - 1)
                link(act.activation(mixT[:, n % 2, 1:T], H[:, i, 0:T - 1], ACT.Copy,
                               scale=vcol("mu", 8 * MIXES[m] + i)), "mix_t")

            def mix_hi(n):
                act.wait_ge(S("mix_m"), n + 1)
                if n >= 2:
                    mix_used(act, n - 2)
                link(act.activation(mixH[:, n % 2, :], mixM[:, n % 2, :], ACT.Copy), "mix_hi")

            def rkv_read(p):
                dst = (Rr, Kk, Vv)[p]
                for e in range(DT):
                    if e < 7:
                        act.wait_ge(S("rkv_done"), 7 * p + e + 1)
                    else:
                        act.wait_ge(S("blk"), START["r"] + DT * (p + 1))
                    link(act.activation(dst[:, e, :], ps[:, e, :], ACT.Copy), "rkv_read")

            last = 24 if upto < 2 else 48
            mix_prev(0)
            for n in range(last):
                if n == 18:
                    act.wait_ge(S("blk"), 1)
                    link(act.activation(loF[0:HD, 0, :], ps[0:HD, 0, :], ACT.Tanh), "lo_f")
                    link(act.activation(loF[HD:P, 1, :], ps[HD:P, 1, :], ACT.Copy), "lo_f")
                    act.wait_ge(S("lo_f"), 2)
                    link(act.activation(loH[:, :, :], loF[:, :, :], ACT.Copy), "lo_h")
                if n == 24:
                    lora_reads(act) if False else None
                if n + 1 < last:
                    mix_prev(n + 1)
                if n == 25:
                    act.wait_ge(S("blk"), 3)
                    link(act.activation(sgF[:, :, :], ps[:, 2:4, :], ACT.Sigmoid), "sg_ready")
                    for t in range(16):
                        m, e = divmod(t, DT)
                        if t < 15:
                            act.wait_ge(S("lora_up"), t + 1)
                        else:
                            act.wait_ge(S("blk"), 4)
                        link(act.activation((DEC, AG)[m][:, e, :], ps[:, (4 + t) % 8, :], ACT.Sigmoid,
                                       bias=vcol(("w0", "a0")[m], e)), "lora_read")
                if n >= 33 and (n - 33) % DT == 0:
                    rkv_read((n - 33) // DT)
                if 26 <= n < 30:
                    e = 2 * (n - 26)
                    act.wait_ge(S("lora_read"), e + 2)
                    link(act.activation(DEC[:, e:e + 2, :], DEC[:, e:e + 2, :], ACT.Exp, scale=DECAY), "decay")
                mix_hi(n)
            if upto < 2:
                act.wait_ge(S("blk"), 3)
                link(act.activation(sgF[:, :, :], ps[:, 2:4, :], ACT.Sigmoid), "sg_ready")
                for t in range(16):
                    m, e = divmod(t, DT)
                    act.wait_ge(S("lora_up") if t < 15 else S("blk"), t + 1 if t < 15 else 4)
                    link(act.activation((DEC, AG)[m][:, e, :], ps[:, (4 + t) % 8, :], ACT.Sigmoid,
                                   bias=vcol(("w0", "a0")[m], e)), "lora_read")
                act.wait_ge(S("lora_read"), 16)
                act.sem_inc(S("all_done"), 1)
                return
            rkv_read(2)
            for i in range(DT):
                act.wait_ge(S("kk_raw"), i + 1)
                if i >= 2:
                    act.wait_ge(S("kk_sum"), i - 1)
                link(act.activation(tmp[i % 2][:, :], KN[:, i, :], ACT.Square), "kk_sq")
            act.wait_ge(S("kk_sum"), DT)
            link(act.activation(rstd[0:48, :], ps[0:48, 5, :], ACT.Sqrt), "kk_norm")
            act.wait_ge(S("bo_sum"), DT)
            link(act.activation(tmpA[0:48, :], ps[0:48, 6, :], ACT.Copy), "bo_row")
            for u in range(0, 24, 2):
                n, g = divmod(u % 8, 2)
                act.wait_ge(S("tok_done"), u + 1)
                link(act.activation((Vtok, Ktok, Btok)[u // 8][:, n, g * 512:(g + 1) * 512], ps[:, 4 + u % 4, :], ACT.Copy), "tok_a")
            if upto < 3:
                return
            nseq = 0
            for n in range(QT):
                for hp in range(2):
                    act.wait_ge(S("p2"), 2 * n + hp + 1)
                    link(act.activation(mP2[:, hp, :, :], ps[:, 2 + hp, :].rearrange("p (a b) -> p a b", a=DT), ACT.Copy), "p2_read")
                for c in range(2):
                    k = slice(c * HD, c * HD + HD)
                    tc = slice((2 * n + c) * C, (2 * n + c + 1) * C)
                    act.wait_ge(S("y1"), nseq + 1)
                    link(act.activation(Rr[:, :, tc], ps[:, 5, :].rearrange("p (a b) -> p a b", a=DT), ACT.Copy), "y1_read")
                    act.wait_ge(S("u"), 2 * nseq + 1)
                    link(act.activation(mT[k, 0, :, :], ps[k, 2, :].rearrange("p (a b) -> p a b", a=DT), ACT.Copy), "u_new_a")
                    nseq += 1
            if upto < 4:
                return

            def read_tiles(phase, sem, dst, func=ACT.Copy, tiles=None):
                for e in range(COUNT[phase]):
                    act.wait_ge(S("blk"), START[phase] + e + 1)
                    link(act.activation(dst(e), ps[:, e % 4, :], func), sem)

            def normed_hi(tag, dst=None, n=DT):
                for i in range(n):
                    act.wait_ge(S("normed_hf"), DT * NORMED[tag] + i + 1)
                    link(act.activation((HH if dst is None else dst)[:, i, :], tmp[i % 2][:, :], ACT.Copy), "normed_hi")

            def head_squares(tag, n, src, after):
                for i in range(n):
                    act.wait_ge(*count(after[0], after[1] + i))
                    if i >= 2:
                        act.wait_ge(*count(f"{tag}_sum", i - 1))
                    link(act.activation(tmp[i % 2][:, :], src(i), ACT.Square), f"{tag}_sq")

            def head_root(tag, n, bank_, bias):
                act.wait_ge(*count(f"{tag}_sum", n))
                link(act.activation(rstd[0:48, :], ps[0:48, bank_, :], ACT.Sqrt, scale=1.0 / HD, bias=bias[0:48, 0:1]), f"{tag}_norm")

            def mlp(m, norm):
                base = START[f"mlp{m}"]

                def group(b, g, first=False):
                    for j in range(5):
                        if j < 4:
                            act.wait_ge(S("blk"), b + j + 1)
                            if not (first and j < 2):
                                act.wait_ge(S("full"), FT * m + g * 4 + j - 1)
                            act.activation(relT[:, j % 2, :], ps[:, j, :], ACT.Relu).then_inc(S("rel"), 1)
                        if j:
                            act.wait_ge(S("full"), FT * m + g * 4 + j)
                            dst = hid_of(g)
                            act.activation(dst[:, j - 1, :], sqrT[:, (j - 1) % 2, :], ACT.Copy).then_inc(S("hidhi"), 1)

                parity = [0]

                def hid_of(g):
                    return hidH[parity[0]]

                def turn(b, g, buf, first=False):
                    parity[0] = buf
                    group(b, g, first)

                turn(base, 0, 0, first=True)
                turn(base + 4, 1, 1)
                with act.Fori(0, 3) as i:
                    turn(base + 12 + i * 16, i * 2 + 2, 0)
                    turn(base + 20 + i * 16, i * 2 + 3, 1)

            act.wait_ge(S("y_done"), NCH)
            act.sem_inc(S("rec_done"), 1)
            link(act.activation(sgH[:, :, :], sgF[:, :, :], ACT.Copy), "sg_hi")
            for i in range(DT):
                act.wait_ge(S("gn_c"), i + 1)
                if i >= 2:
                    act.wait_ge(*count("gn_sum", i - 1))
                link(act.activation(tmp[i % 2][:, :], Rr[:, i, :], ACT.Square), "gn_sq")
            head_root("gn", DT, 5, epsg)
            for i in range(DT + 1):
                if i < DT:
                    act.wait_ge(*count("gn_used", i + 1))
                    link(act.activation(Rr[:, i, :], Rr[:, i, :], ACT.Identity, scale=vcol("lnx_w", i), bias=vcol("lnx_b", i)), "gn_aff")
                if i:
                    act.wait_ge(S("y_gated"), i)
                    link(act.activation(YH[:, i - 1, :], tmp[(i - 1) % 2][:, :], ACT.Copy), "y_hi")
            norm_squares(1)
            norm_root(1)
            normed_hi("m0")
            if upto < 5:
                return
            mlp(0, 1)
            norm_squares(2)
            norm_root(2)
            if upto < 6:
                return
            act.dma_start(AF["c2"][:, :], consts2).then_inc(S("c2f"), 16)
            normed_hi("kv")
            read_tiles("kv_k", "kv_k", lambda e: KF[:, e, :])
            read_tiles("kv_v", "kv_v", lambda e: VF[:, e, :])
            act.wait_ge(S("blk"), START["kv_f"] + 1)
            act.wait_ge(S("rstd_kept"), 1)
            link(act.activation(rstd[0:16, :], ps[0:16, 0, :], ACT.Identity, bias=vcol("f_bias")[0:16, :]), "kv_f")
            act.wait_ge(S("bias_clear"), 1)
            link(act.activation(tmpA[0:16, :], rstd[0:16, :], ACT.Abs))
            link(act.activation(tmpA[0:16, :], tmpA[0:16, :], ACT.Exp, scale=-1.0))
            link(act.activation(tmpA[0:16, :], tmpA[0:16, :], ACT.Ln, bias=1.0), "f_log")
            act.wait_ge(S("f_bias"), 1)
            normed_hi("q")
            for u in range(0, 8, 2):
                n, g = divmod(u, 2)
                act.wait_ge(S("v2"), u + 1)
                link(act.activation(V2[:, n, g * 512:(g + 1) * 512], ps[:, 4 + u % 4, :], ACT.Copy), "v2_a")
            act.wait_ge(S("normed_lo"), DT * NORMED["q"] + DT)
            read_tiles("fox_q", "fox_q", lambda e: QR[:, e, :])
            head_squares("kn2", DT, lambda i: KF[:, i, :], ("kv_k", 1))
            head_root("kn2", DT, 5, epsn)
            act.wait_ge(*count("kn2_used", DT))
            head_squares("qn2", DT, lambda i: QR[:, i, :], ("fox_q", 1))
            head_root("qn2", DT, 4, epsn)

            def attend(tag, units, B):
                def exps(u):
                    name, h, i = units[u]
                    n = CMPN if name == "cmp" else P * (i + 1)
                    act.wait_ge(*count(f"{tag}_max", u + 1))
                    if u >= 2:
                        act.wait_ge(*count(f"{tag}_t", u - 1))
                    if u >= 4:
                        act.wait_ge(*count(f"{tag}_o", u - 3))
                    link(act.activation(B["P"][:, u % 2, 0:n], ps[:, u % 2, 0:n], ACT.Exp, bias=B["col"][:, u % 4:u % 4 + 1],
                                        accum_out=B["col"][:, 4 + u % 4:5 + u % 4]), f"{tag}_exp")

                def transposed(u):
                    name, h, i = units[u]
                    act.wait_ge(*count(f"{tag}_t", u + 1))
                    if u >= 2:
                        act.wait_ge(*count(f"{tag}_pv", u - 1))
                    if name == "cmp":
                        link(act.activation(B["PT"][0:CMPN, u % 2, 0, :], ps[0:CMPN, 2 + u % 2, 0:P], ACT.Copy), f"{tag}_pt")
                    else:
                        link(act.activation(B["PT"][:, u % 2, 0:i + 1, :], ps[:, 2 + u % 2, 0:P * (i + 1)].rearrange("p (a b) -> p a b", b=P),
                                            ACT.Copy), f"{tag}_pt")

                exps(0)
                for u in range(len(units)):
                    if u + 1 < len(units):
                        exps(u + 1)
                    transposed(u)

            attend("fa", FOX, AF)
            for i in range(DT):
                act.wait_ge(S("ofm"), i + 1)
                link(act.activation(HH[:, i, :], ps[:, 6 + i % 2, :], ACT.Copy), "hi_o")
            if upto < 7:
                return
            norm_squares(3)
            norm_root(3)
            normed_hi("m1")
            mlp(1, 3)
            norm_squares(4)
            norm_root(4)
            normed_hi("n1")
            read_tiles("conv_c", "conv_c", lambda e: CC[:, e, :])
            for i in range(DT):
                act.wait_ge(S("zf"), i + 1)
                link(act.activation(ZH[:, i, :], tmp[i % 2][:, :], ACT.Copy), "z_hi")
            read_tiles("gate_b", "gate_b", lambda e: SG[:, e, :], ACT.Sigmoid)
            if upto < 9:
                act.wait_ge(*count("gate_b", DT))
                return
            act.wait_ge(S("branch_b"), DT)
            read_tiles("gate_a", "gate_a", lambda e: SG[:, e, :], ACT.Sigmoid)
            act.dma_start(A2["c2"][:, :], consts2).then_inc(S("c2s"), 16)
            read_tiles("nsa_q", "nsa_q", lambda e: R1[:, e, :])
            read_tiles("nsa_kv", "nsa_kv", lambda e: R1[:, 4 + e, :] if e < 4 else R2[:, e - 4, :])
            act.wait_ge(S("blk"), START["nsa_g"] + 1)
            act.dma_start(CW[:, :, :], cmpw).then_inc(S("cw_in"), 16)
            link(act.activation(R2[:, 2, :], ps[:, 0, :], ACT.Sigmoid), "nsa_g")
            head_squares("q3", 4, lambda i: R1[:, i, :], ("nsa_q", 1))
            head_root("q3", 4, 5, epsn)
            act.wait_ge(*count("q3_used", 4))
            head_squares("k3", 2, lambda i: (R1[:, 6, :], R2[:, 0, :])[i], ("nsa_kv", 5))
            head_root("k3", 2, 4, epsn)
            for w in range(2):
                act.wait_ge(S("v3"), w + 1)
                link(act.activation(V3[:, w, :, :], ps[:, w, :].rearrange("p (a b) -> p a b", b=P), ACT.Copy), "v3_read")
            act.wait_ge(S("g3"), 1)
            link(act.activation(GT[:, :, 0:24], ps[:, 2, :].rearrange("p (a b) -> p a b", b=P)[:, :, 0:24], ACT.Copy), "g3_read")
            act.wait_ge(S("kc"), 1)
            link(act.activation(KC[:, 0:CMPN], ps[:, 3, 0:CMPN], ACT.Copy), "kc_raw")
            act.wait_ge(*count("k3_sum", 2))
            link(act.activation(tmpA[:, 0:CMPN], KC[:, 0:CMPN], ACT.Square), "kc_sq")
            act.wait_ge(S("vc"), 1)
            for g in range(2):
                link(act.activation(VC[0:CMPN, g * HD:(g + 1) * HD], ps[0:CMPN, 4 + g, 0:HD], ACT.Copy), "vc_read")
            act.wait_ge(S("kc_sum"), 1)
            link(act.activation(tmpB[:, 0:CMPN], ps[:, 6, 0:CMPN], ACT.Sqrt, scale=1.0 / HD, bias=epsn[:, 0:1]), "kc_norm")
            attend("na", NSA, A2)
            for i in range(4):
                act.wait_ge(*count("ofm2", i + 1))
                link(act.activation(NHi[:, i, :], ps[:, 6 + i % 2, :], ACT.Copy), "hi_o2")
            if upto < 10:
                return
            for i in range(DT):
                act.wait_ge(S("mixed"), i + 1)
                link(act.activation(MH[:, i, :], MX[:, i, :], ACT.Copy), "hi_mx")
            norm_squares(5)
            norm_root(5)
            normed_hi("m2")
            mlp(2, 5)


        @block.vector
        def _(dve):
            ticks = {}

            def link(ins, name="dve_chain"):
                name = shared.get(name, (name, 0))[0]
                ticks[name] = ticks.get(name, 0) + 1
                ins.then_inc(S(name), 1)
                dve.wait_ge(S(name), ticks[name])

            def norm_sum(n, i):
                dve.wait_ge(S("norm_sq"), DT * n + i + 1)
                if i == 0:
                    link(dve.tensor_copy(ssq[:, :], tmp[0][:, :]), "norm_sum")
                else:
                    dve.wait_ge(S("norm_sum"), DT * n + i)
                    link(dve.tensor_tensor(ssq[:, :], ssq[:, :], tmp[i % 2][:, :], ALU.add), "norm_sum")

            def norm_recip(n):
                dve.wait_ge(S("norm_root"), n + 1)
                link(dve.reciprocal(rstd[:, :], rstd[:, :]))

            link(dve.memset(epsn[:, :], EPS))
            link(dve.memset(epsg[:, :], GN_EPS))
            link(dve.memset(mixT[:, :, 0:1], 0.0))
            link(dve.memset(loF[HD:P, 0, :], 0.0))
            link(dve.memset(loF[0:HD, 1, :], 0.0), "consts_set")
            for i in range(DT):
                norm_sum(0, i)
            dve.wait_ge(S("const_in"), 32)
            link(dve.tensor_scalar(omu[:, :], vec[:, VOFF["mu"]:VOFF["mu"] + 48], -1.0, 1.0, ALU.mult, ALU.add))
            norm_recip(0)
            for i in range(DT):
                link(dve.scalar_tensor_tensor(H[:, i, :], X[:, i, :], vcol("norm_g", i), rstd[:, :], ALU.mult, ALU.mult), "h_ready")
            dve.wait_ge(S("h_ready"), 8)

            def mix(n):
                m, i = divmod(n, DT)
                dve.wait_ge(S("mix_t"), n + 1)
                if n >= 2:
                    dve.wait_ge(S("mix_hi"), n - 1)
                link(dve.scalar_tensor_tensor(mixM[:, n % 2, :], H[:, i, :], omu[:, 8 * MIXES[m] + i:8 * MIXES[m] + i + 1],
                                         mixT[:, n % 2, :], ALU.mult, ALU.add), "mix_m")

            def mix_lo(n):
                dve.wait_ge(S("mix_hi"), n + 1)
                if n >= 2:
                    mix_used(dve, n - 2)
                link(dve.tensor_tensor(mixL[:, n % 2, :], mixM[:, n % 2, :], mixH[:, n % 2, :].bitcast(F32), ALU.subtract), "mix_lo")

            last = 24 if upto < 2 else 48
            mix(0)
            for n in range(last):
                if n + 1 < last:
                    mix(n + 1)
                mix_lo(n)
                if n == 17:
                    dve.wait_ge(S("lo_h"), 1)
                    link(dve.tensor_tensor(loL[:, :, :], loF[:, :, :], loH[:, :, :].bitcast(F32), ALU.subtract), "lo_split")
                if n == 30:
                    link(dve.memset(ssq[:, :], 0.0))
                if n >= 32:
                    e, second = divmod(n - 32, 2)
                    if not second:
                        dve.wait_ge(S("decay"), e // 2 + 1)
                        link(dve.tensor_copy(ssq[:, ::C], DEC[:, e, ::C]))
                        link(dve.memset(DEC[:, e, ::C], 0.0))
                        link(dve.tensor_tensor_scan(DEC[:, e, :], DEC[:, e, :], ssq[:, :], 0.0, ALU.mult, ALU.add))
                        link(dve.reciprocal(RD[:, e, 0:256], DEC[:, e, 0:256]))
                    else:
                        link(dve.reciprocal(RD[:, e, 256:T], DEC[:, e, 256:T]))
            if upto < 2:
                return
            for i in range(DT):
                dve.wait_ge(S("rkv_read"), 8 + i + 1)
                link(dve.tensor_scalar(KN[:, i, :], Kk[:, i, :], vcol("k_k", i), None, ALU.mult), "kk_raw")
            dve.wait_ge(S("kk_sum"), DT)
            for i in range(DT):
                link(dve.tensor_scalar(ssq[:, :], AG[:, i, :], -1.0, vcol("k_a", i), ALU.add, ALU.mult))
                link(dve.scalar_tensor_tensor(Kk[:, i, :], ssq[:, :], 1.0, Kk[:, i, :], ALU.add, ALU.mult))
                if i >= 2:
                    dve.wait_ge(S("bo_sum"), i - 1)
                link(dve.scalar_tensor_tensor(tmp[i % 2][:, :], Rr[:, i, :], vcol("r_k", i), Kk[:, i, :], ALU.mult, ALU.mult), "bo_sq")
            dve.wait_ge(S("kk_norm"), 1)
            link(dve.tensor_scalar(rstd[0:48, :], rstd[0:48, :], 1e-12, None, ALU.max))
            link(dve.reciprocal(rstd[0:48, :], rstd[0:48, :]), "kk_root")
            link(dve.tensor_copy(dch[:, :, :], DEC[:, :, C - 1::C]))
            for i in range(DT):
                dve.wait_ge(S("kk_spread"), i + 1)
                link(dve.tensor_tensor(KN[:, i, :], KN[:, i, :], ps[:, i % 2, :], ALU.mult))
                link(dve.tensor_tensor(AG[:, i, :], AG[:, i, :], KN[:, i, :], ALU.mult), "kk_used")
            for i in range(DT):
                dve.wait_ge(S("rkv_read"), 24)
                dve.wait_ge(S("bo_spread"), i + 1)
                link(dve.tensor_tensor(BON[:, i, :], Vv[:, i, :], ps[:, 2 + i % 2, :], ALU.mult), "bo_used")
            dve.wait_ge(S("bo_used"), 8)
            dve.wait_ge(S("kk_used"), 8)
            for i in range(DT):
                link(dve.tensor_tensor(Kk[:, i, :], Kk[:, i, :], RD[:, i, :], ALU.mult), "kt")
                link(dve.tensor_tensor(AG[:, i, :], AG[:, i, :], RD[:, i, :], ALU.mult), "bt")
                link(dve.tensor_tensor(Rr[:, i, :], Rr[:, i, :], DEC[:, i, :], ALU.mult), "rt")
                a = KN[:, i, :].rearrange("p (c t) -> p c t", t=C)
                d = DEC[:, i, :].rearrange("p (c t) -> p c t", t=C)
                link(dve.scalar_tensor_tensor(a[:, :, 1:C], a[:, :, 1:C], -1.0, d[:, :, 0:C - 1], ALU.mult, ALU.mult))
                link(dve.tensor_scalar(a[:, :, 0:1], a[:, :, 0:1], -1.0, None, ALU.mult), "kn")
            dve.sem_inc(S("bon"), 8) if False else None
            for u in range(1, 24, 2):
                n, g = divmod(u % 8, 2)
                dve.wait_ge(S("tok_done"), u + 1)
                link(dve.tensor_copy((Vtok, Ktok, Btok)[u // 8][:, n, g * 512:(g + 1) * 512], ps[:, 4 + u % 4, :]), "tok_d")
            if upto < 3:
                dve.wait_ge(S("tok_a"), 12)
                dve.wait_ge(S("tok_d"), 12)
                dve.sem_inc(S("all_done"), 1)
                return
            link(dve.memset(ST[:, :], 0.0), "s_new")

            def wide(m, name, a=0):
                return const(name, a, a + C).unsqueeze(1).to_broadcast([P, DT, C])

            def bank(b, k=slice(0, P)):
                return ps[k, b, :].rearrange("p (a b) -> p a b", a=DT)

            gram = nlev = nseq = 0
            for n in range(QT):
                for what in range(5):
                    for hp in range(2):
                        dve.wait_ge(S("gram"), gram + 1)
                        src = bank(gram % 10 % 8)
                        if what == 0:
                            link(dve.tensor_tensor(mN[:, hp, :, :], src, wide(mN, "ltN"), ALU.mult))
                            link(dve.tensor_tensor(mQ[:, hp, :, :], src, wide(mQ, "lvN1"), ALU.mult))
                            link(dve.tensor_tensor(mQ[:, hp, :, :], mQ[:, hp, :, :], wide(mQ, "id64"), ALU.add), "gram_read")
                        elif what == 1:
                            link(dve.tensor_tensor(mT[:, hp, :, :], src, wide(mT, "lvM"), ALU.mult))
                            link(dve.tensor_tensor(mT[:, hp, :, :], mT[:, hp, :, :], wide(mT, "id64"), ALU.add), "gram_read")
                        else:
                            dst = (mZ, mRB, mRK)[what - 2]
                            link(dve.tensor_tensor(dst[:, hp, :, :], src, wide(dst, "ltN" if what == 2 else "leT"), ALU.mult), "gram_read")
                        gram += 1
                for lv, s in enumerate(levels()):
                    for hp in range(2):
                        dve.wait_ge(S("z"), 2 * nlev + hp + 1)
                        link(dve.tensor_tensor(mZ[:, hp, :, :], bank(hp), wide(mZ, "lvM", (lv + 1) * C), ALU.mult), "z_new")
                    for hp in range(2):
                        if s < 32:
                            dve.wait_ge(S("t"), 8 * n + 2 * lv + hp + 1)
                            link(dve.tensor_tensor(mT[:, hp, :, :], mT[:, hp, :, :], bank(4 + hp), ALU.add), "t_new")
                        dve.wait_ge(S("q"), 2 * nlev + hp + 1)
                        link(dve.tensor_tensor(mQ[:, hp, :, :], mQ[:, hp, :, :], bank(6 + hp), ALU.add), "q_new")
                    nlev += 1
                for c in range(2):
                    k = slice(c * HD, c * HD + HD)
                    tc = slice((2 * n + c) * C, (2 * n + c + 1) * C)
                    for hp in range(2):
                        dve.wait_ge(S("as"), 2 * nseq + hp + 1)
                        dve.wait_ge(S("p2_read"), 2 * n + hp + 1)
                        link(dve.tensor_tensor(mN[k, hp, :, :], bank(hp, k), mP2[k, hp, :, :], ALU.add), "p_new")
                    dve.wait_ge(S("u"), 2 * nseq + 2)
                    link(dve.tensor_copy(mT[k, 1, :, :], bank(3, k)), "u_new_d")
                    dve.wait_ge(S("s"), nseq + 1)
                    sv = ST[:, :].rearrange("p (a b) -> p a b", a=DT)
                    link(dve.tensor_tensor(sv, sv, bank(4), ALU.add))
                    link(dve.tensor_tensor(sv, sv, dch[:, :, 2 * n + c].unsqueeze(2).to_broadcast([P, DT, HD]), ALU.mult), "s_new")
                    dve.wait_ge(S("y2"), nseq + 1)
                    dve.wait_ge(S("y1_read"), nseq + 1)
                    link(dve.tensor_tensor(Rr[:, :, tc], Rr[:, :, tc], bank(6), ALU.add), "y_done")
                    nseq += 1
            if upto < 4:
                dve.wait_ge(S("y_done"), NCH)
                dve.sem_inc(S("all_done"), 1)
                return

            def normed(tag, gain, g0=0, after=None):
                if after is not None:
                    dve.wait_ge(S("blk"), after)
                for i in range(DT + 1):
                    if i < DT:
                        if i >= 2:
                            dve.wait_ge(S("normed_hi"), DT * NORMED[tag] + i - 1)
                        link(dve.scalar_tensor_tensor(tmp[i % 2][:, :], X[:, i, :], vcol(gain, g0 + i), rstd[:, :], ALU.mult, ALU.mult), "normed_hf")
                    if i:
                        dve.wait_ge(S("normed_hi"), DT * NORMED[tag] + i)
                        link(dve.tensor_tensor(HL[:, i - 1, :], tmp[(i - 1) % 2][:, :], HH[:, i - 1, :].bitcast(F32), ALU.subtract), "normed_lo")

            def residual(phase, n):
                for e in range(DT + 1):
                    if e < DT:
                        dve.wait_ge(S("blk"), START[phase] + e + 1)
                        link(dve.tensor_tensor(X[:, e, :], X[:, e, :], ps[:, e % 4, :], ALU.add), "x_up")
                    if e:
                        norm_sum(n, e - 1)

            def head_recip(tag, factor=None):
                dve.wait_ge(*count(f"{tag}_norm", 1))
                if factor is None:
                    link(dve.reciprocal(rstd[0:48, :], rstd[0:48, :]), f"{tag}_root")
                else:
                    link(dve.reciprocal(rstd[0:48, :], rstd[0:48, :]))
                    link(dve.tensor_scalar(rstd[0:48, :], rstd[0:48, :], factor, None, ALU.mult), f"{tag}_root")

            def mlp(m, norm):
                base = START[f"mlp{m}"]

                def squares(g, buf, first=False):
                    for j in range(5):
                        if j < 4:
                            dve.wait_ge(S("rel"), FT * m + g * 4 + j + 1)
                            if not (first and j < 2):
                                dve.wait_ge(S("hid"), FT * m + g * 4 + j - 1)
                            dve.tensor_tensor(sqrT[:, j % 2, :], relT[:, j % 2, :], relT[:, j % 2, :], ALU.mult).then_inc(S("full"), 1)
                        if j:
                            dve.wait_ge(S("hidhi"), FT * m + g * 4 + j)
                            dve.tensor_tensor(hidL[buf][:, j - 1, :], sqrT[:, (j - 1) % 2, :], hidH[buf][:, j - 1, :].bitcast(F32),
                                              ALU.subtract).then_inc(S("hid"), 1)

                def add(b, last=False):
                    for j in range(4):
                        dve.wait_ge(S("blk"), b + j + 1)
                        for o in range(2):
                            e = 2 * j + o
                            ins = dve.tensor_tensor(X[:, e, :], X[:, e, :], ps[:, 4 + 2 * (j % 2) + o, :], ALU.add)
                            if last:
                                link(ins, "x_up")
                            elif o:
                                ins.then_inc(S("down"), 1)
                        if last and j and norm < 5:
                            norm_sum(norm + 1, 2 * j - 2)
                            norm_sum(norm + 1, 2 * j - 1)
                    if last and norm < 5:
                        norm_sum(norm + 1, 6)
                        norm_sum(norm + 1, 7)

                squares(0, 0, first=True)
                squares(1, 1)
                add(base + 8)
                with dve.Fori(0, 3) as i:
                    squares(i * 2 + 2, 0)
                    add(base + 16 + i * 16)
                    squares(i * 2 + 3, 1)
                    add(base + 24 + i * 16)
                add(base + 60, last=True)

            dve.wait_ge(S("sg_hi"), 1)
            link(dve.tensor_tensor(sgL[:, :, :], sgF[:, :, :], sgH[:, :, :].bitcast(F32), ALU.subtract), "sg_split")
            for i in range(DT):
                dve.wait_ge(S("gn_mean"), i + 1)
                link(dve.scalar_tensor_tensor(Rr[:, i, :], ps[:, i % 2, :], -1.0 / HD, Rr[:, i, :], ALU.mult, ALU.add), "gn_c")
            head_recip("gn")
            for i in range(DT):
                dve.wait_ge(*count("gn_spread", i + 1))
                link(dve.tensor_tensor(Rr[:, i, :], Rr[:, i, :], ps[:, 2 + i % 2, :], ALU.mult), "gn_used")
            for i in range(DT + 1):
                if i < DT:
                    dve.wait_ge(S("gn_aff"), i + 1)
                    link(dve.tensor_tensor(Rr[:, i, :], Rr[:, i, :], BON[:, i, :], ALU.add))
                    if i < 7:
                        dve.wait_ge(S("gate_up"), i + 1)
                    else:
                        dve.wait_ge(S("blk"), START["gate_up"] + 2)
                    if i >= 2:
                        dve.wait_ge(S("y_hi"), i - 1)
                    link(dve.tensor_tensor(tmp[i % 2][:, :], Rr[:, i, :], ps[:, 6 + i % 2, :], ALU.mult), "y_gated")
                if i:
                    dve.wait_ge(S("y_hi"), i)
                    link(dve.tensor_tensor(YL[:, i - 1, :], tmp[(i - 1) % 2][:, :], YH[:, i - 1, :].bitcast(F32), ALU.subtract), "y_lo")
            dve.wait_ge(S("x_again"), 16)
            residual("rwkv_o", 1)
            norm_recip(1)
            normed("m0", "mlp_g")
            if upto < 5:
                dve.sem_inc(S("all_done"), 1)
                return
            mlp(0, 1)
            norm_recip(2)
            if upto < 6:
                dve.sem_inc(S("all_done"), 1)
                return
            normed("kv", "kv_g", after=START["kv_k"])
            link(dve.memset(AF["bias"][:, :], 0.0), "bias_clear")
            normed_q = True
            link(dve.tensor_copy(ssq[:, :], rstd[:, :]), "rstd_kept")
            dve.wait_ge(*count("kv_f", 1))
            dve.wait_ge(S("f_log"), 1)
            link(dve.scalar_tensor_tensor(tmpA[0:16, :], rstd[0:16, :], 0.0, tmpA[0:16, :], ALU.min, ALU.subtract))
            link(dve.tensor_tensor_scan(tmpA[0:16, :], one[0:16, :].to_broadcast([16, T]), tmpA[0:16, :], 0.0, ALU.mult, ALU.add))
            link(dve.tensor_scalar(AF["bias"][0:16, :], tmpA[0:16, :], -1.0, None, ALU.mult))
            link(dve.tensor_copy(rstd[:, :], ssq[:, :]), "f_bias")
            normed("q", "attn_g", after=START["kv_f"] + 1)
            for u in range(1, 8, 2):
                n, g = divmod(u, 2)
                dve.wait_ge(S("v2"), u + 1)
                link(dve.tensor_copy(V2[:, n, g * 512:(g + 1) * 512], ps[:, 4 + u % 4, :]), "v2_d")
            link(dve.memset(QE[HD:P, :, :], 0.0))
            link(dve.memset(QO[0:HD, :, :], 0.0))
            head_recip("kn2")
            for i in range(DT):
                dve.wait_ge(*count("kn2_spread", i + 1))
                link(dve.scalar_tensor_tensor(KF[:, i, :], KF[:, i, :], vcol("kn_g", i), ps[:, 6 + i % 2, :], ALU.mult, ALU.mult), "kn2_used")
            head_recip("qn2", 1.0 / 8)
            for i in range(DT):
                dve.wait_ge(*count("qn2_spread", i + 1))
                link(dve.scalar_tensor_tensor(QE[0:HD, i, :], QR[0:HD, i, :], vcol("qn_g", i)[0:HD, :], ps[0:HD, 6 + i % 2, :], ALU.mult, ALU.mult))
                link(dve.scalar_tensor_tensor(QO[HD:P, i, :], QR[HD:P, i, :], vcol("qn_g", i)[HD:P, :], ps[HD:P, 6 + i % 2, :], ALU.mult, ALU.mult), "qn2_used")

            def attend(tag, units, B, finish):
                cmps = [0]

                def maxima(u):
                    name, h, i = units[u]
                    n = CMPN if name == "cmp" else P * (i + 1)
                    dve.wait_ge(*count(f"{tag}_s", u + 1))
                    if u >= 4:
                        dve.wait_ge(*count(f"{tag}_exp", u - 3))
                    link(dve.tensor_reduce(B["col"][:, u % 4:u % 4 + 1], ps[:, u % 2, 0:n], AX, ALU.max, negate=True), f"{tag}_max")

                def keep_visible(u):
                    name, h, i = units[u]
                    if name == "cmp":
                        dve.wait_ge(*count(f"{tag}_exp", u + 1))
                        link(dve.tensor_tensor(B["P"][:, u % 2, 0:CMPN], B["P"][:, u % 2, 0:CMPN], c2(B, "cok", i)[:, 0:CMPN], ALU.mult))
                        link(dve.tensor_reduce(B["col"][:, 4 + u % 4:5 + u % 4], B["P"][:, u % 2, 0:CMPN], AX, ALU.add))
                        link(dve.tensor_scalar(B["col"][:, 4 + u % 4:5 + u % 4], B["col"][:, 4 + u % 4:5 + u % 4], 1e-30, None, ALU.max), f"{tag}_okd")

                def output(u):
                    dve.wait_ge(*count(f"{tag}_exp", u + 1))
                    link(dve.reciprocal(B["col"][:, 8 + u % 4:9 + u % 4], B["col"][:, 4 + u % 4:5 + u % 4]))
                    dve.wait_ge(*count(f"{tag}_pv", u + 1))
                    finish(u, units[u], B["col"][:, 8 + u % 4:9 + u % 4], ps[:, 4 + u % 2, 0:HD])

                maxima(0)
                for u in range(len(units)):
                    if u + 1 < len(units):
                        maxima(u + 1)
                    keep_visible(u)
                    if u:
                        output(u - 1)
                output(len(units) - 1)

            def fox_finish(u, unit, inv, acc):
                _, h, i = unit
                link(dve.tensor_scalar(Ot[:, i, h * HD:(h + 1) * HD], acc, inv, None, ALU.mult), "fa_o")

            attend("fa", FOX, AF, fox_finish)
            for i in range(DT):
                dve.wait_ge(S("ofm"), i + 1)
                dve.wait_ge(S("hi_o"), i + 1)
                link(dve.tensor_tensor(HL[:, i, :], ps[:, 6 + i % 2, :], HH[:, i, :].bitcast(F32), ALU.subtract), "lo_o")
            if upto < 7:
                dve.sem_inc(S("all_done"), 1)
                return
            residual("fox_o", 3)
            norm_recip(3)
            normed("m1", "mlp_g", 8)
            mlp(1, 3)
            norm_recip(4)
            normed("n1", "norm1")
            for e in range(DT):
                dve.wait_ge(*count("conv_c", DT))
                dve.wait_ge(S("blk"), START["conv_x"] + e + 1)
                link(dve.tensor_tensor(CU[:, e, :], CC[:, e, :], ps[:, e % 4, :], ALU.mult), "conv_x")
            for e in range(DT):
                link(dve.tensor_scalar(CC[:, e, :], CU[:, e, :], vcol("conv", 16 + e), None, ALU.mult))
                link(dve.scalar_tensor_tensor(CC[:, e, 1:T], CU[:, e, 0:T - 1], vcol("conv", 8 + e), CC[:, e, 1:T], ALU.mult, ALU.add))
                link(dve.scalar_tensor_tensor(CC[:, e, 2:T], CU[:, e, 0:T - 2], vcol("conv", e), CC[:, e, 2:T], ALU.mult, ALU.add))
                dve.wait_ge(S("blk"), START["conv_b"] + e + 1)
                if e >= 2:
                    dve.wait_ge(S("z_hi"), e - 1)
                link(dve.tensor_tensor(tmp[e % 2][:, :], CC[:, e, :], ps[:, e % 4, :], ALU.mult), "zf")
                dve.wait_ge(S("z_hi"), e + 1)
                link(dve.tensor_tensor(ZL[:, e, :], tmp[e % 2][:, :], ZH[:, e, :].bitcast(F32), ALU.subtract), "z_lo")
            if upto < 9:
                dve.wait_ge(*count("gate_b", DT))
                dve.sem_inc(S("all_done"), 1)
                return
            for e in range(DT):
                dve.wait_ge(*count("gate_b", DT))
                dve.wait_ge(S("blk"), START["branch_b"] + e + 1)
                link(dve.tensor_tensor(MX[:, e, :], SG[:, e, :], ps[:, e % 4, :], ALU.mult), "branch_b")
            link(dve.memset(Q2[HD:P, 0:4, :], 0.0))
            link(dve.memset(Q2[0:HD, 4:8, :], 0.0))
            head_recip("q3", 1.0 / 8)
            for i in range(4):
                dve.wait_ge(*count("q3_spread", i + 1))
                for g in range(2):
                    h = slice(g * HD, g * HD + HD)
                    link(dve.scalar_tensor_tensor(Q2[h, 4 * g + i, :], R1[h, i, :], vcol("qn2")[h, :], ps[h, 6 + i % 2, :], ALU.mult, ALU.mult),
                         "q3_used" if g else "dve_chain")
            head_recip("k3")
            for i in range(2):
                dve.wait_ge(*count("k3_spread", i + 1))
                kt = (R1[:, 6, :], R2[:, 0, :])[i]
                link(dve.scalar_tensor_tensor(kt, kt, vcol("kn2", 1 + i), ps[:, 6 + i % 2, :], ALU.mult, ALU.mult), "k3_used")
            for w in range(2):
                for g in range(2):
                    n = (CMPN + 1 - g) // 2
                    src = R1[:, 4 + w, 16 * g:16 * g + 32 * n].rearrange("p (c w) -> p w c", w=CMPB)
                    pos = vec[:, VOFF["pos_k"] + CMPB * w:VOFF["pos_k"] + CMPB * (w + 1)].unsqueeze(2).to_broadcast([P, CMPB, n])
                    link(dve.tensor_tensor(CE[:, w, :, g::2], src, pos, ALU.add), "ce" if g else "dve_chain")
            dve.wait_ge(S("kc_norm"), 1)
            link(dve.reciprocal(tmpB[:, 0:CMPN], tmpB[:, 0:CMPN]))
            link(dve.scalar_tensor_tensor(KC[:, 0:CMPN], KC[:, 0:CMPN], vcol("kn2", 0), tmpB[:, 0:CMPN], ALU.mult, ALU.mult), "kc_done")

            def nsa_finish(u, unit, inv, acc):
                name, h, i = unit
                row = {"cmp": 0, "slc": 1, "win": 2}[name]
                link(dve.tensor_tensor(A2["col"][:, 12:13], inv, GT[:, i, 8 * row + h:8 * row + h + 1], ALU.mult))
                o = O2[:, i, h * HD:(h + 1) * HD]
                if name == "slc":
                    link(dve.tensor_scalar(o, acc, A2["col"][:, 12:13], None, ALU.mult), "na_o")
                else:
                    link(dve.scalar_tensor_tensor(o, acc, A2["col"][:, 12:13], o, ALU.mult, ALU.add), "na_o")

            attend("na", NSA, A2, nsa_finish)
            for i in range(4):
                dve.wait_ge(*count("ofm2", i + 1))
                dve.wait_ge(*count("hi_o2", i + 1))
                link(dve.tensor_tensor(NLo[:, i, :], ps[:, 6 + i % 2, :], NHi[:, i, :].bitcast(F32), ALU.subtract), "lo_o2")
            if upto < 10:
                dve.sem_inc(S("all_done"), 1)
                return
            for j in range(4):
                dve.wait_ge(S("blk"), START["branch_a"] + j + 1)
                for o in range(2):
                    e = 2 * j + o
                    link(dve.tensor_tensor(tmp[o][:, :], SG[:, e, :], ps[:, 4 + 2 * (j % 2) + o, :], ALU.mult))
                    link(dve.tensor_tensor(MX[:, e, :], MX[:, e, :], tmp[o][:, :], ALU.add), "mixed")
                    dve.wait_ge(S("hi_mx"), e + 1)
                    link(dve.tensor_tensor(ML[:, e, :], MX[:, e, :], MH[:, e, :].bitcast(F32), ALU.subtract), "lo_mx")
            residual("out", 5)
            norm_recip(5)
            normed("m2", "norm2")
            mlp(2, 5)


def arrange(x):
    f = {k: np.asarray(v) for k, v in x.items()}
    kmajor = lambda w: w.reshape(DT, P, -1, P).transpose(2, 1, 0, 3).reshape(-1, P, D)
    rows = lambda w: w.reshape(-1, P, D)

    def padded(w, rows_, cols):
        return np.pad(w, ((0, rows_ - w.shape[0]), (0, cols - w.shape[1])))

    def mlp(w_in, w_out):
        up = kmajor(w_in).reshape(8, 4, P, D)
        down = w_out.reshape(8, 4, P, 4, 2, P).transpose(0, 3, 2, 4, 1, 5).reshape(8, 4, P, D)
        order = [up[0]]
        for g in range(7):
            order += [up[g + 1], down[g]]
        return np.concatenate(order + [down[7]])

    g1 = padded(f["rwkv_g1"][0], D, 2 * P)
    g2 = padded(f["rwkv_g2"][0], 2 * P, D)
    heads = np.arange(D // 2).reshape(2, 4, HD).transpose(1, 0, 2).reshape(-1)
    win = f["w_in_2"][0]
    cut = np.cumsum([0, 512] + [128] * 6 + [24] + [D] * 5)
    part = [win[:, cut[i]:cut[i + 1]] for i in range(13)]
    wa = f["w_branch_a_2"][0].reshape(4, P, 4, 2, P).transpose(2, 1, 3, 0, 4).reshape(4, P, D)
    blocks = [
        kmajor(np.concatenate([f["rwkv_w1"][0], f["rwkv_a1"][0]], 1)), kmajor(g1),
        np.concatenate([f["rwkv_w2"][0], f["rwkv_a2"][0]])[None],
        rows(f["rwkv_w_rkv"][0, 0]), rows(f["rwkv_w_rkv"][0, 1]), rows(f["rwkv_w_rkv"][0, 2]), rows(g2),
        kmajor(f["rwkv_w_o"][0]), mlp(f["mlp_w_in"][0], f["mlp_w_out"][0]),
        kmajor(f["kv_w"][:, :D]), kmajor(f["kv_w"][:, D:2 * D]), kmajor(padded(f["kv_w"][:, 2 * D:], D, P)),
        kmajor(f["attn_w_q"][0]), kmajor(f["attn_w_o"][0]), mlp(f["mlp_w_in"][1], f["mlp_w_out"][1]),
        kmajor(part[9]), kmajor(part[10]), kmajor(part[8]), kmajor(part[12]), kmajor(f["w_branch_b_2"][0]),
        kmajor(part[11]), kmajor(part[0][:, heads]), kmajor(np.concatenate(part[1:7], 1)),
        kmajor(padded(part[7], D, P)), wa, kmajor(f["w_out_2"][0]), mlp(f["w_up_2"][0], f["w_down_2"][0]),
    ]
    stream = np.ascontiguousarray(np.concatenate(blocks))
    assert stream.shape == (NBLK, P, D), stream.shape

    col = lambda v: v.reshape(-1, P).T
    dup = lambda v: np.concatenate([v, v], 0)
    fb = np.pad(f["kv_f_bias"], (0, P - NH)).reshape(P, 1)
    v = dict(norm_g=col(f["rwkv_norm_g"]), mu=col(f["rwkv_mu"]), w0=col(f["rwkv_w0"]), a0=col(f["rwkv_a0"]),
             k_k=col(f["rwkv_k_k"]), k_a=col(f["rwkv_k_a"]), r_k=col(f["rwkv_r_k"]), lnx_w=col(f["rwkv_lnx_w"]),
             lnx_b=col(f["rwkv_lnx_b"]), kv_g=col(f["kv_norm_g"]), attn_g=col(f["attn_norm_g"]),
             kn_g=col(f["k_norm_g"]), qn_g=col(f["q_norm_g"]), mlp_g=col(f["mlp_norm_g"]), norm1=col(f["norm1_g_2"]),
             norm2=col(f["norm2_g_2"]), conv=col(f["conv_w_2"]), qn2=dup(f["q_norm_g_2"].T), kn2=dup(f["k_norm_g_2"][0].T),
             pos_k=dup(f["cmp_pos_k_2"][0].T), pos_v=dup(f["cmp_pos_v_2"][0].T), f_bias=fb)
    vecs = np.ascontiguousarray(np.concatenate([v[n] for n, _ in VECS], 1))
    cmpw = np.stack([dup(f[n][0].reshape(CMPB, HD, HD).transpose(1, 0, 2).reshape(HD, -1))
                     for n in ("w_cmp_k_2", "w_cmp_v_2")], 1)
    xT = np.ascontiguousarray(f["x"][0].T.reshape(DT, P, T).transpose(1, 0, 2))
    first, second = constants()
    return dict(xT=xT, stream=stream, vecs=vecs, consts=first, consts2=second, cmpw=np.ascontiguousarray(cmpw))


def kernel(**inputs):
    from concourse import bacc
    from concourse.bass_utils import run_bass_kernel_spmd

    arrays = arrange(inputs)
    nc = bacc.Bacc("TRN2", target_bir_lowering=False, num_devices=1)
    aps = {n: nc.dram_tensor(n, a.shape, mybir.dt.from_np(a.dtype), kind="ExternalInput").ap() for n, a in arrays.items()}
    aps["out"] = nc.dram_tensor("out", (P, DT, T), F32, kind="ExternalOutput").ap()
    build(nc, **aps)
    r = run_bass_kernel_spmd(nc, [arrays], core_ids=[0])
    return r.results[0]["out"].transpose(1, 0, 2).reshape(1, D, T).transpose(0, 2, 1)
```

```python
from contextlib import ExitStack

import numpy as np
import concourse.bass as bass
from concourse import mybir

F32 = mybir.dt.float32
F32R = mybir.dt.float32r
ALU = mybir.AluOpType
ACT = mybir.ActivationFunctionType
AX = mybir.AxisListType.X

P = 128
T = 512
D = 1024
DT = D // P
HD = 64
NH = D // HD
FF = 4 * D
FT = FF // P
DOWNS = FT - 4
QT = T // P
C = 64
NCH = T // C
LORA = 64
GLORA = 160
NH2 = 8
CMPN = T // 16 - 1
CMPB = 32
EPS = 1e-6
GN_EPS = 64e-5
NEG = -1e30

MLP_BLOCKS = 2 * FF // P
PHASES = [
    ("lora_wa", 1), ("lora_g", 2), ("lora_up", 1), ("r", DT), ("k", DT), ("v", DT), ("gate_up", 2),
    ("rwkv_o", DT), ("mlp0", MLP_BLOCKS), ("kv_k", DT), ("kv_v", DT), ("kv_f", 1), ("fox_q", DT),
    ("fox_o", DT), ("mlp1", MLP_BLOCKS), ("conv_c", DT), ("conv_x", DT), ("conv_b", DT),
    ("gate_b", DT), ("branch_b", DT), ("gate_a", DT), ("nsa_q", 4), ("nsa_kv", 6), ("nsa_g", 1),
    ("branch_a", DT // 2), ("out", DT), ("mlp2", MLP_BLOCKS),
]
START = {}
_n = 0
for _name, _c in PHASES:
    START[_name] = _n
    _n += _c
NBLK = _n
COUNT = dict(PHASES)
RAW = 4
SPL = 2

VECS = [("norm_g", 8), ("mu", 48), ("w0", 8), ("a0", 8), ("k_k", 8), ("k_a", 8), ("r_k", 8),
        ("lnx_w", 8), ("lnx_b", 8), ("kv_g", 8), ("attn_g", 8), ("kn_g", 8), ("qn_g", 8),
        ("mlp_g", 16), ("norm1", 8), ("norm2", 8), ("conv", 24), ("qn2", 1), ("kn2", 3),
        ("pos_k", 32), ("pos_v", 32), ("f_bias", 1)]
VOFF = {}
_n = 0
for _name, _c in VECS:
    VOFF[_name] = _n
    _n += _c
NVEC = _n

CONSTS = [("ident", P), ("bones", P), ("hsel", 62), ("psel", 4 * P), ("one", 1), ("ltN", C), ("leT", C),
          ("id64", C), ("lvM", 6 * C), ("lvN1", C)]
COFF = {}
_n = 0
for _name, _c in CONSTS:
    COFF[_name] = _n
    _n += _c
NCONST = _n
CONSTS2 = [("cbias", T), ("abias", T)]


def constants():
    c = {}
    c["ident"] = np.eye(P)
    i = np.arange(P)
    c["bones"] = (i[:, None] // HD == i[None, :] // HD).astype(float)
    hs = np.zeros((P, 62))
    for half in range(2):
        hs[half * HD:(half + 1) * HD, [14 + half, 46 + half]] = 1.0
    c["hsel"] = hs
    psel = np.zeros((P, 4, P))
    for t in range(8):
        for half in range(2):
            psel[32 * (t // 4) + 2 * t + half, t % 4, half * HD:(half + 1) * HD] = 1.0
    c["psel"] = psel.reshape(P, -1)
    c["one"] = np.ones((P, 1))
    a = np.arange(C)
    r = i % C
    c["ltN"] = (r[:, None] < a[None, :]).astype(float)
    c["leT"] = (r[:, None] <= a[None, :]).astype(float)
    c["id64"] = (r[:, None] == a[None, :]).astype(float)
    lv = [((r[:, None] // s) % 2 == 1) & (a[None, :] // s == r[:, None] // s - 1)
          for s in (1, 2, 4, 8, 16, 32)]
    c["lvM"] = np.concatenate(lv, 1).astype(float)
    c["lvN1"] = ((a[None, :] % 2 == 1) & (r[:, None] == a[None, :] - 1)).astype(float)
    first = np.concatenate([c[n].reshape(P, -1) for n, _ in CONSTS], 1).astype(np.float32)
    slopes = 2.0 ** (-8.0 * np.arange(1, NH2 + 1) / NH2)
    ab = np.zeros((P, T))
    ab[:NH2] = slopes[:, None] * np.arange(T)[None, :]
    cb = np.zeros((P, CMPB))
    cb[:NH2, :CMPN] = slopes[:, None] * (np.arange(CMPN) * 16 + 31)[None, :]
    t = np.arange(T).reshape(QT, P)
    ok = (t[:, :, None] >= np.arange(CMPB)[None, None, :] * 16 + 31).transpose(1, 0, 2)
    ok = ok.reshape(P, QT * CMPB)
    causal = np.where(i[:, None] >= i[None, :], 0.0, NEG)
    second = np.concatenate([causal, ab, cb, np.where(ok, 0.0, NEG), ok.astype(float)], 1).astype(np.float32)
    return first, second


NC2 = P + T + CMPB + 2 * QT * CMPB



def build(nc, xT, stream, vecs, consts, consts2, cmpw, out, upto=99, dump=None, dump_out=None):
    def at(name, shape, off, dt=F32):
        return nc.alloc_sbuf_tensor_at(name, shape, dt, offset=off)

    def zone(i, extra=0):
        return 16512 + i * 16384 + extra

    full, tok, sq = [P, DT, T], [P, QT, D], [P, 2, DT, C]
    raw = at("raw", [P, RAW, D], zone(10))
    whi = at("whi", [P, SPL, DT, P], zone(11), F32R)
    wlo = at("wlo", [P, SPL, DT, P], zone(11, 8192), F32R)
    o = zone(12)
    cst = at("cst", [P, NCONST], o)
    o += (4 * NCONST + 31) // 32 * 32
    vec = at("vec", [P, NVEC], o)
    o += (4 * NVEC + 31) // 32 * 32
    omu = at("omu", [P, 48], o)
    rstd = at("rstd", [P, T], o + 192)
    tmpA = at("tmpA", [P, T], o + 192 + 2048)
    tmpB = at("tmpB", [P, T], o + 192 + 4096)
    ssq = at("ssq", [P, T], o + 192 + 6144)
    dch = at("dch", [P, DT, NCH], o + 192 + 8192)
    o += 192 + 8192 + 256
    epsn = at("epsn", [P, 1], o)
    epsg = at("epsg", [P, 1], o + 32)
    oka = at("oka", [P, DT], o + 64)
    o += 96
    assert o <= 229368, o
    tmp = [tmpA, tmpB]

    X = at("X", full, zone(3))
    H = at("H", full, zone(0))
    mixT = at("mixT", [P, 2, T], zone(9))
    mixM = at("mixM", [P, 2, T], zone(9, 4096))
    mixH = at("mixH", [P, 2, T], zone(9, 8192), F32R)
    mixL = at("mixL", [P, 2, T], zone(9, 12288), F32R)
    loF = at("loF", [P, 2, T], zone(7))
    loH = at("loH", [P, 2, T], zone(7, 4096), F32R)
    loL = at("loL", [P, 2, T], zone(7, 8192), F32R)
    sgF = at("sgF", [P, 2, T], zone(8))
    DEC = at("DEC", full, zone(1))
    RD = at("RD", full, zone(2))
    AG = at("AG", full, zone(3))
    Rr = at("Rr", full, zone(4))
    Kk = at("Kk", full, zone(5))
    Vv = at("Vv", full, zone(6))
    KN = at("KN", full, zone(7))
    BON = at("BON", full, zone(0))
    Ktok = at("Ktok", tok, zone(1))
    Btok = at("Btok", tok, zone(2))
    Vtok = at("Vtok", tok, zone(9))
    mZ = at("mZ", sq, zone(6))
    mRB = at("mRB", sq, zone(6, 4096))
    mRK = at("mRK", sq, zone(6, 8192))
    kfac = at("kfac", [P, 2, T], zone(8, 4096))
    mP2 = at("mP2", sq, zone(6, 12288))
    mN = at("mN", sq, zone(8, 4096))
    mT = at("mT", sq, zone(8, 8192))
    mQ = at("mQ", sq, zone(8, 12288))
    ST = ssq

    sgH = at("sgH", [P, 2, T], zone(7), F32R)
    sgL = at("sgL", [P, 2, T], zone(7, 4096), F32R)
    YH = at("YH", full, zone(1), F32R)
    YL = at("YL", full, zone(2), F32R)
    HH = at("HH", full, zone(4), F32R)
    HL = at("HL", full, zone(5), F32R)
    HQ = at("HQ", full, zone(6), F32R)
    LQ = at("LQ", full, zone(7), F32R)
    hidH = [at(f"hidH{b}", [P, 4, T], zone(6 + b), F32R) for b in range(2)]
    hidL = [at(f"hidL{b}", [P, 4, T], zone(6 + b, 8192), F32R) for b in range(2)]
    relT = at("relT", [P, 2, T], zone(8))
    sqrT = at("sqrT", [P, 2, T], zone(8, 4096))
    KF = at("KF", full, zone(0))
    VF = at("VF", full, zone(1))
    V2 = at("V2", tok, zone(2))
    KH = at("KH", full, zone(4), F32R)
    KL = at("KL", full, zone(5), F32R)
    QR = at("QR", full, zone(8))
    OH = at("OH", full, zone(0), F32R)
    OL = at("OL", full, zone(1), F32R)
    CC = at("CC", full, zone(6))
    CU = at("CU", full, zone(7))
    ZH = at("ZH", full, zone(0), F32R)
    ZL = at("ZL", full, zone(1), F32R)
    SG = at("SG", full, zone(8))
    MX = at("MX", full, zone(9))
    R1 = at("R1", full, zone(0))
    R2 = at("R2", [P, 3, T], zone(1))
    GT = at("GT", [P, QT, 32], zone(1, 6144))
    V3 = at("V3", [P, 2, QT, P], zone(6))
    KC = at("KC", [P, CMPB], zone(6, 4096))
    VC = at("VC", [CMPB, P], zone(6, 4224))
    CE = at("CE", [P, 2, CMPB, CMPN], zone(6, 4736))
    KCR = at("KCR", [P, 2, CMPB], zone(6, 12800), F32R)
    K2 = at("K2", [P, 4, T], zone(4, 8192), F32R)
    CW = at("CW", [P, 2, 2048], zone(5))
    NHi = at("NHi", [P, 4, T], zone(5), F32R)
    NLo = at("NLo", [P, 4, T], zone(5, 8192), F32R)
    MH = at("MH", full, zone(0), F32R)
    ML = at("ML", full, zone(1), F32R)

    def attention_buffers(tag, work, pairs, consts_at):
        return dict(P=at("pr" + tag, [P, 3, T], zone(work)), PT=at("pt" + tag, [P, 2, QT, P], zone(work, 6144)),
                    col=at("cl" + tag, [P, 16], zone(work, 14336)),
                    Q=at("qp" + tag, [P, 2, 4, T], zone(pairs), F32R),
                    c2=at("c2" + tag, [P, NC2], zone(consts_at)), c2r=at("cr" + tag, [P, NC2], zone(consts_at, 3744), F32R),
                    id=at("ir" + tag, [P, P], zone(consts_at, 7488), F32R))

    AF, A2 = attention_buffers("f", 9, 6, 7), attention_buffers("s", 7, 2, 4)
    fbias = at("fbias", [P, T], zone(7, 8192))
    fbiasR = at("fbiasR", [P, 2, T], zone(7, 10240), F32R)

    def c2(buf, name, i=0):
        off = {"causal": 0, "abias": P, "cbias": P + T, "cneg": P + T + CMPB + i * CMPB,
               "cok": P + T + CMPB + (QT + i) * CMPB}[name]
        width = {"causal": P, "abias": T}.get(name, CMPB)
        return buf["c2" if name == "cok" else "c2r"][:, off:off + width]

    FOX = [("fox", p, hp, i) for p in range(DT) for hp in range(2) for i in range(QT)]
    NSA = [(b, p, hp, i) for p in range(4) for hp in range(2) for i in range(QT) for b in ("slc", "win", "cmp")]

    bufs = dict( MX=MX, OH=OH, NHi=NHi, X=X, H=H, DEC=DEC, RD=RD, AG=AG, Rr=Rr, Kk=Kk, Vv=Vv, KN=KN, BON=BON, Ktok=Ktok, Btok=Btok, Vtok=Vtok)

    def const(name, a=0, b=None):
        w = dict(CONSTS)[name]
        return cst[:, COFF[name] + a:COFF[name] + (w if b is None else b)]

    def vcol(name, i=0):
        return vec[:, VOFF[name] + i:VOFF[name] + i + 1]

    ident, one = const("ident"), const("one")

    def gather_heads(i):
        return const("hsel", 14 - 2 * i, 62 - 2 * i)

    def spread_heads(i, rows):
        r = 32 * (i // 4)
        return cst[r:r + 16, COFF["psel"] + i % 4 * P:COFF["psel"] + (i % 4 + 1) * P], rows[r:r + 16, :]

    with ExitStack() as ctx:
        global sems
        sems = {}

        shared = {}
        tiles = 0
        for turn, (tag, n) in enumerate([("gn", DT), ("kn2", DT), ("qn2", DT), ("q3", 4), ("k3", 2)]):
            for what in ("sq", "sum", "spread", "used"):
                shared[f"{tag}_{what}"] = f"heads_{what}", tiles
            for what in ("norm", "root"):
                shared[f"{tag}_{what}"] = f"heads_{what}", turn
            tiles += n
        for what in ("s", "max", "exp", "pn", "t", "pt", "pv"):
            shared[f"na_{what}"] = f"fa_{what}", len(FOX)
        for what in ("q_hi", "q_lo", "out_hi", "out_lo"):
            shared[f"na_{what}"] = f"fa_{what}", DT
        tiles = 0
        for phase in ("kv_k", "kv_v", "kv_f", "fox_q", "conv_c", "gate_b", "gate_a", "nsa_q", "nsa_kv", "nsa_g"):
            shared[phase] = "tile_read", tiles
            tiles += COUNT[phase]

        def count(name, value):
            first, before = shared.get(name, (name, 0))
            return S(first), before + value

        def S(name):
            name = shared.get(name, (name, 0))[0]
            if name not in sems:
                sems[name] = ctx.enter_context(nc.semaphore(name))
            return sems[name]

        ps = ctx.enter_context(nc.psum_tensor("ps", [P, 8, T], F32))
        nblk = NBLK
        if upto < 99:
            nblk = {1: START["r"] + 8, 2: START["gate_up"], 3: START["gate_up"], 4: START["mlp0"], 5: START["kv_k"], 6: START["fox_o"], 7: START["mlp1"], 8: START["branch_b"], 9: START["branch_a"], 10: START["mlp2"]}[upto]

        block = ctx.enter_context(nc.Block())

        @block.sync
        def _(sp):
            sp.dma_start(X[:, :, :], xT).then_inc(S("x_in"), 16)
            sp.dma_start(cst[:, :], consts).then_inc(S("const_in"), 16)
            sp.dma_start(vec[:, :], vecs).then_inc(S("const_in"), 16)
            for b in range(RAW):
                sp.dma_start(raw[:, b, :], stream[b]).then_inc(S(f"raw_in{b}"), 16)

            def rest(first, n, i=None):
                for j in range(n):
                    b = first + j if i is None else i * RAW + j
                    sp.wait_ge(S("split_ready"), b - (RAW - 1))
                    src = stream[b] if i is None else stream[bass.ds(b, 1)].squeeze(0)
                    sp.dma_start(raw[:, j, :], src).then_inc(S(f"raw_in{j}"), 16)

            pre = START["rwkv_o"] if nblk > START["rwkv_o"] else nblk
            pre -= pre % RAW
            with sp.Fori(1, pre // RAW) as i:
                rest(0, RAW, i)
            if nblk > START["rwkv_o"]:
                sp.wait_ge(S("rec_done"), 1)
                sp.dma_start(X[:, :, :], xT).then_inc(S("x_again"), 16)
            if nblk // RAW > pre // RAW:
                with sp.Fori(pre // RAW, nblk // RAW) as i:
                    rest(0, RAW, i)
            rest(nblk - nblk % RAW, nblk % RAW)
            if upto < 99:
                sp.wait_ge(S("all_done"), 1)
            else:
                sp.wait_ge(S("x_up"), 6 * DT)
            if dump is not None:
                sp.dma_start(dump_out, bufs[dump][:].bitcast(F32)).then_inc(S("stored"), 16)
            else:
                sp.dma_start(out, X[:, :, :]).then_inc(S("stored"), 16)
            sp.wait_ge(S("stored"), 16)

        @block.gpsimd
        def _(pool):
            def split(b, j, turn):
                s = j % SPL
                if not isinstance(b, int) or b >= SPL:
                    pool.wait_ge(S("blk"), b - (SPL - 1))
                pool.wait_ge(S(f"raw_in{j}"), (turn + 1) * 16)
                pool.sem_inc(S("split_turn"), 1)
                pool.tensor_scalar(whi[:, s, :, :], raw[:, j, :].rearrange("p (k m) -> p k m", k=DT), 1.0, 0.0, ALU.mult, ALU.add)\
                    .then_inc(S("hi_ready"), 1)
                pool.wait_ge(S("hi_ready"), b + 1)
                pool.tensor_tensor(wlo[:, s, :, :], raw[:, j, :].rearrange("p (k m) -> p k m", k=DT), whi[:, s, :, :].bitcast(F32), ALU.subtract)\
                    .then_inc(S("split_ready"), 1)

            for j in range(RAW):
                split(j, j, 0)
            before = min(START["gate_up"], nblk) // RAW
            with pool.Fori(1, before) as i:
                for j in range(RAW):
                    split(i * RAW + j, j, i)
            if upto >= 2:
                for n, (x, by, name) in enumerate(((Kk, RD, "kt"), (Rr, DEC, "rt"))):
                    for i in range(DT):
                        if n == 0:
                            pool.wait_ge(S("bo_sq"), i + 1)
                        pool.tensor_tensor(x[:, i, :], x[:, i, :], by[:, i, :], ALU.mult).then_inc(S(name), 1)
            if nblk // RAW > before:
                with pool.Fori(before, nblk // RAW) as i:
                    for j in range(RAW):
                        split(i * RAW + j, j, i)
            for j in range(nblk % RAW):
                split(nblk - nblk % RAW + j, j, nblk // RAW)

        MIXES = [1, 4, 5, 0, 2, 3]
        DECAY = -float(np.exp(-0.5))

        def mix_used(eng, n):
            if n == 15:
                eng.wait_ge(S("blk"), 1)
            elif n == 23:
                eng.wait_ge(S("blk"), 3)
            elif n > 23:
                eng.wait_ge(S("blk"), START["r"] + n - 24 + 1)
            else:
                eng.wait_ge(S("mix_used"), n + 1 if n < 15 else n)

        NORMED = {tag: n for n, tag in enumerate(("m0", "kv", "q", "m1", "n1", "m2"))}

        def normed_lo(tag):
            return "normed_lo", DT * NORMED[tag]

        def levels():
            return [2, 4, 8, 16, 32]

        @block.tensor
        def _(pe):
            def three(acc, w, hi, lo, start, stop):
                s, k = w
                pe.matmul(acc, whi[:, s, k, :], hi, start=start, stop=False)
                pe.matmul(acc, whi[:, s, k, :], lo, start=False, stop=False)
                return pe.matmul(acc, wlo[:, s, k, :], hi, start=False, stop=stop)

            def norm_mean(n):
                pe.wait_ge(S("norm_sum"), DT * n + DT)
                pe.matmul(ps[:, 4, :], one.to_broadcast([P, P]), ssq[:, :], start=True, stop=True)\
                    .then_inc(S("norm_mean"), 1)

            def head_sums(tag, n, bank=5):
                for i in range(n):
                    pe.wait_ge(*count(f"{tag}_sq", i + 1))
                    pe.matmul(ps[0:48, bank, :], gather_heads(i), tmp[i % 2][:, :],
                              start=i == 0, stop=i == n - 1).then_inc(S(f"{tag}_sum"), 1)

            def head_spread(tag, n, banks, rows=rstd):
                pe.wait_ge(*count(f"{tag}_root", 1))
                for i in range(n):
                    if i >= len(banks):
                        pe.wait_ge(*count(f"{tag}_used", i - len(banks) + 1))
                    pe.matmul(ps[:, banks[i % len(banks)], :], *spread_heads(i, rows), start=True, stop=True)\
                        .then_inc(S(f"{tag}_spread"), 1)

            pe.wait_ge(S("const_in"), 32)
            norm_mean(0)
            for n in range(24):
                m, i = divmod(n, DT)
                pe.wait_ge(S("mix_lo"), n + 1)
                s = n % 2
                if n == 0:
                    pe.wait_ge(S("split_ready"), 1)
                if n == 16:
                    pe.wait_ge(S("split_ready"), 3)
                if m < 2:
                    mm = three(ps[:, m, :], (0, i), mixH[:, s, :], mixL[:, s, :], i == 0, i == 7)
                else:
                    mm = three(ps[:, 2, :], (1, i), mixH[:, s, :], mixL[:, s, :], i == 0, i == 7)
                    if i == 7:
                        mm.then_inc(S("blk"), 1)
                    mm = three(ps[:, 3, :], (0, i), mixH[:, s, :], mixL[:, s, :], i == 0, i == 7)
                mm.then_inc(S("blk") if n in (15, 23) else S("mix_used"), 1)
            pe.wait_ge(S("split_ready"), 4)
            pe.wait_ge(S("lo_split"), 1)
            pe.wait_ge(S("sg_ready"), 1)
            for t in range(16):
                if t >= 8:
                    pe.wait_ge(S("lora_read"), t - 7)
                m, e = divmod(t, DT)
                mm = three(ps[:, (4 + t) % 8, :], (1, e), loH[:, m, :], loL[:, m, :], True, True)
                mm.then_inc(S("blk") if t == 15 else S("lora_up"), 1)
            if upto < 2:
                return
            pe.wait_ge(S("lora_read"), 16)
            for p in range(3):
                for i in range(DT):
                    n = 24 + DT * p + i
                    b = START["r"] + DT * p + i
                    pe.wait_ge(S("mix_lo"), n + 1)
                    pe.wait_ge(S("split_ready"), b + 1)
                    for e in range(DT):
                        if p and i == 0:
                            pe.wait_ge(S("rkv_read"), DT * (p - 1) + e + 1)
                        mm = three(ps[:, e, :], (b % SPL, e), mixH[:, n % 2, :], mixL[:, n % 2, :], i == 0, i == 7)
                        if i == 7 and e < 7:
                            mm.then_inc(S("rkv_done"), 1)
                    mm.then_inc(S("blk"), 1)
            pe.wait_ge(S("rkv_read"), 24)
            head_sums("kk", DT)
            head_sums("bo", DT, 6)

            def tokens(u):
                src, ready = [(Vv, ()), (AG, ("bt", "kt")), (Kk, ("kn", "rt"))][u // 8]
                n, g = divmod(u % 8, 2)
                for name in ready:
                    pe.wait_ge(S(name), 8)
                if 4 <= u < 20:
                    pe.wait_ge(S("tok_a"), u - 3)
                elif u >= 20 and u % 2 == 0:
                    pe.wait_ge(S("tok_a"), 16 + (u - 20) // 2 + 1)
                elif u >= 20:
                    pe.wait_ge(S("tok_d"), (u - 20) // 2 + 1)
                for j in range(4):
                    mm = pe.transpose(ps[:, 4 + u % 4, j * P:(j + 1) * P], src[:, 4 * g + j, n * P:(n + 1) * P], ident)
                mm.then_inc(S("tok_done"), 1)

            pe.wait_ge(S("kk_root"), 1)
            pe.wait_ge(S("bo_row"), 1)
            for i in range(DT):
                if i >= 2:
                    pe.wait_ge(S("kk_used"), i - 1)
                pe.matmul(ps[:, i % 2, :], *spread_heads(i, rstd), start=True, stop=True).then_inc(S("kk_spread"), 1)
                tokens(i)
            for i in range(DT):
                if i >= 2:
                    pe.wait_ge(S("bo_used"), i - 1)
                pe.matmul(ps[:, 2 + i % 2, :], *spread_heads(i, tmpA), start=True, stop=True)\
                    .then_inc(S("bo_spread"), 1)
                tokens(DT + i)
            for u in range(16, 24):
                tokens(u)
            pe.wait_ge(S("tok_a"), 20)
            pe.wait_ge(S("tok_d"), 4)
            pe.wait_ge(S("kn"), 8)
            pe.wait_ge(S("rt"), 8)
            if upto < 3:
                return

            def square(dst_bank, c, hp, p):
                return ps[c * HD:(c + 1) * HD, dst_bank, p * HD:(p + 1) * HD]

            gram = 0
            nlev = 0
            nseq = 0
            for n in range(QT):
                for lhs, rhs in ((AG, KN), (KN, AG), (Kk, KN), (AG, Rr), (Kk, Rr)):
                    for hp in range(2):
                        if gram % 10 >= 8:
                            pe.wait_ge(S("gram_read"), gram - 7)
                        elif gram >= 10 and gram % 10 == 0:
                            pe.wait_ge(S("y_done"), 2 * n)
                            pe.wait_ge(S("s_new"), 2 * n)
                        h = slice(hp * HD, hp * HD + HD)
                        for p in range(DT):
                            for c in range(2):
                                tc = slice((2 * n + c) * C, (2 * n + c + 1) * C)
                                mm = pe.matmul(square(gram % 10 % 8, c, hp, p), lhs[h, p, tc], rhs[h, p, tc],
                                               start=True, stop=True)
                        mm.then_inc(S("gram"), 1)
                        gram += 1
                for hp in range(2):
                    pe.wait_ge(S("gram_read"), gram - 4 + hp - 1)
                    pe.wait_ge(S("gram_read"), gram - 8 + 2 + hp)
                    for p in range(DT):
                        for c in range(2):
                            k = slice(c * HD, c * HD + HD)
                            mm = pe.matmul(square(2 + hp, c, hp, p), mZ[k, hp, p, :],
                                           Vtok[k, n, (2 * p + hp) * HD:(2 * p + hp + 1) * HD], start=True, stop=True)
                    mm.then_inc(S("p2"), 1)
                for s in levels():
                    for hp in range(2):
                        if nlev % 5 == 0:
                            pe.wait_ge(S("p2_read"), 2 * n + 2)
                            pe.wait_ge(S("gram_read"), gram)
                        else:
                            pe.wait_ge(S("t_new"), 8 * n + 2 * (nlev % 5) - 2 + hp + 1)
                            pe.wait_ge(S("q_new"), 2 * nlev - 2 + hp + 1)
                        for p in range(DT):
                            for c in range(2):
                                k = slice(c * HD, c * HD + HD)
                                mm = pe.matmul(square(hp, c, hp, p), mN[k, hp, p, :], mT[k, hp, p, :], start=True, stop=True)
                        mm.then_inc(S("z"), 1)
                    for hp in range(2):
                        pe.wait_ge(S("z_new"), 2 * nlev + hp + 1)
                        if s < 32:
                            for p in range(DT):
                                for c in range(2):
                                    k = slice(c * HD, c * HD + HD)
                                    mm = pe.matmul(square(4 + hp, c, hp, p), mQ[k, hp, p, :], mZ[k, hp, p, :], start=True, stop=True)
                            mm.then_inc(S("t"), 1)
                        for p in range(DT):
                            for c in range(2):
                                k = slice(c * HD, c * HD + HD)
                                mm = pe.matmul(square(6 + hp, c, hp, p), mZ[k, hp, p, :], mQ[k, hp, p, :], start=True, stop=True)
                        mm.then_inc(S("q"), 1)
                    nlev += 1
                pe.wait_ge(S("q_new"), 2 * nlev)
                for c in range(2):
                    k = slice(c * HD, c * HD + HD)
                    tc = slice((2 * n + c) * C, (2 * n + c + 1) * C)

                    def head(hp, p):
                        return slice((2 * p + hp) * HD, (2 * p + hp + 1) * HD)

                    pe.wait_ge(S("s_new"), nseq + 1 - (1 if nseq else 0) if False else nseq + 1)
                    for hp in range(2):
                        h = slice(hp * HD, hp * HD + HD)
                        for p in range(DT):
                            mm = pe.matmul(square(hp, c, hp, p), KN[h, p, tc], ST[h, p * HD:(p + 1) * HD], start=True, stop=True)
                        mm.then_inc(S("as"), 1)
                    for hp in range(2):
                        h = slice(hp * HD, hp * HD + HD)
                        for p in range(DT):
                            mm = pe.matmul(ps[h, 5, p * HD:(p + 1) * HD], ST[h, p * HD:(p + 1) * HD], Rr[h, p, tc],
                                           start=True, stop=True)
                    mm.then_inc(S("y1"), 1)
                    for hp in range(2):
                        h = slice(hp * HD, hp * HD + HD)
                        for p in range(DT):
                            pe.matmul(ps[h, 4, p * HD:(p + 1) * HD], Ktok[k, n, head(hp, p)], Vtok[k, n, head(hp, p)],
                                      start=p == 0, stop=False, skip_group_check=True)
                    for hp in range(2):
                        pe.wait_ge(S("p_new"), 2 * nseq + hp + 1)
                        for p in range(DT):
                            mm = pe.matmul(square(2 + hp, c, hp, p), mQ[k, hp, p, :], mN[k, hp, p, :], start=True, stop=True)
                        mm.then_inc(S("u"), 1)
                    for hp in range(2):
                        h = slice(hp * HD, hp * HD + HD)
                        if nseq and hp == 0:
                            pe.wait_ge(S("y_done"), nseq)
                        for p in range(DT):
                            pe.matmul(ps[h, 6, p * HD:(p + 1) * HD], Vtok[k, n, head(hp, p)], mRK[k, hp, p, :],
                                      start=p == 0, stop=False, skip_group_check=True)
                    for hp in range(2):
                        h = slice(hp * HD, hp * HD + HD)
                        pe.wait_ge(S("u_new_a" if hp == 0 else "u_new_d"), nseq + 1)
                        for p in range(DT):
                            mm = pe.matmul(ps[h, 4, p * HD:(p + 1) * HD], Btok[k, n, head(hp, p)], mT[k, hp, p, :],
                                           start=False, stop=True, skip_group_check=True)
                    mm.then_inc(S("s"), 1)
                    for hp in range(2):
                        h = slice(hp * HD, hp * HD + HD)
                        for p in range(DT):
                            mm = pe.matmul(ps[h, 6, p * HD:(p + 1) * HD], mT[k, hp, p, :], mRB[k, hp, p, :],
                                           start=False, stop=True, skip_group_check=True)
                    mm.then_inc(S("y2"), 1)
                    nseq += 1
            if upto < 4:
                return

            def ready(b):
                pe.wait_ge(S("split_ready"), b + 1)

            def linear(phase, hi, lo, lo_sem, read, before, norm=None):
                start, n = START[phase], COUNT[phase]
                (lo_sem, lo0), (read, read0) = lo_sem, read
                for sem, value in before:
                    pe.wait_ge(*count(sem, value))

                def tile(b, j, s, e=None, first=False):
                    ready(b)
                    if e is not None:
                        pe.wait_ge(*count(read, read0 + e - 3))
                    for k in range(DT):
                        if first:
                            pe.wait_ge(S(lo_sem), lo0 + k + 1)
                        mm = three(ps[:, j, :], (s, k), hi[:, k, :], lo[:, k, :], k == 0, k == DT - 1)
                    mm.then_inc(S("blk"), 1)

                for j in range(min(n, 4)):
                    tile(start + j, j, (start + j) % SPL, first=j == 0)
                    if j == 0 and norm is not None:
                        norm_mean(norm)
                if n >= 8:
                    with pe.Fori(1, n // 4) as i:
                        for j in range(4):
                            tile(start + i * 4 + j, j, (start + j) % SPL, e=i * 4 + j)
                for j in range(n % 4 if n > 4 else 0):
                    e = n - n % 4 + j
                    tile(start + e, j, (start + j) % SPL, e=e)

            def wide_tiles(b, s, j, k0, rhs, free):
                ready(b)
                if free is not None:
                    pe.wait_ge(S(free[0]), free[1])
                for o in range(2):
                    for k in range(4):
                        mm = three(ps[:, 4 + 2 * (j % 2) + o, :], (s, 4 * o + k), rhs[0][:, k, :], rhs[1][:, k, :], k == 0, k == 3)
                mm.then_inc(S("blk"), 1)

            def mlp(m, norm, hi, lo):
                base = START[f"mlp{m}"]

                def up(b, g, first=False, free=True):
                    for j in range(4):
                        ready(b + j)
                        if first:
                            pe.wait_ge(S("x_up"), DT * norm - 3 + j)
                        if free:
                            pe.wait_ge(S("rel"), FT * m + g * 4 + j - 3)
                        for k in range(DT):
                            if first and j == 0:
                                pe.wait_ge(S("normed_lo"), DT * NORMED[f"m{m}"] + k + 1)
                            mm = three(ps[:, j, :], ((base + j) % SPL, k), hi[:, k, :], lo[:, k, :], k == 0, k == DT - 1)
                        mm.then_inc(S("blk"), 1)
                        if first and j == 0:
                            norm_mean(norm)

                def down(b, g, buf, first=False, last=False):
                    for j in range(4):
                        if j == 0:
                            pe.wait_ge(S("hid"), FT * m + g * 4 + 4)
                        free = None if first and j < 2 else ("down", DOWNS * m + g * 4 + j - 1)
                        if last and j >= 2:
                            free = ("x_up", DT * norm + 2 * j - 2)
                        wide_tiles(b + j, (base + j) % SPL, j, 0, (hidH[buf], hidL[buf]), free)

                up(base, 0, first=True, free=False)
                up(base + 4, 1)
                down(base + 8, 0, 0, first=True)
                with pe.Fori(0, 3) as i:
                    up(base + 12 + i * 16, i * 2 + 2)
                    down(base + 16 + i * 16, i * 2 + 1, 1)
                    up(base + 20 + i * 16, i * 2 + 3)
                    down(base + 24 + i * 16, i * 2 + 2, 0)
                down(base + 60, 7, 1, last=True)

            g0 = START["gate_up"]
            for i in range(DT):
                pe.wait_ge(S("y_done"), NCH)
                if i >= 2:
                    pe.wait_ge(S("gn_c"), i - 1)
                pe.matmul(ps[:, i % 2, :], const("bones"), Rr[:, i, :], start=True, stop=True).then_inc(S("gn_mean"), 1)
            head_sums("gn", DT)
            head_spread("gn", DT, [2, 3])
            ready(g0 + 1)
            pe.wait_ge(S("sg_split"), 1)
            for e in range(DT):
                if e >= 2:
                    pe.wait_ge(S("y_gated"), e - 1)
                bank_ = 6 + e % 2
                mm = three(ps[:, bank_, :], (g0 % SPL, e), sgH[:, 0, :], sgL[:, 0, :], True, False)
                if e == 7:
                    mm.then_inc(S("blk"), 1)
                mm = three(ps[:, bank_, :], ((g0 + 1) % SPL, e), sgH[:, 1, :], sgL[:, 1, :], False, True)
                mm.then_inc(S("gate_up") if e < 7 else S("blk"), 1)
            linear("rwkv_o", YH, YL, ("y_lo", 0), ("x_up", 0), [("gn_used", DT), ("gn_c", DT)])
            if upto < 5:
                return
            mlp(0, 1, HH, HL)
            if upto < 6:
                return
            linear("kv_k", HH, HL, normed_lo("kv"), ("kv_k", 0), [], norm=2)
            linear("kv_v", HH, HL, normed_lo("kv"), ("kv_v", 0), [("kv_k", DT)])
            linear("kv_f", HH, HL, normed_lo("kv"), ("kv_f", 0), [("kv_v", DT)])

            def to_tokens(tag, sources, done_a, done_d, banks):
                for u, (waits, ins) in enumerate(sources):
                    for sem, value in waits:
                        pe.wait_ge(S(sem), value)
                    if u >= len(banks):
                        v = u - len(banks)
                        pe.wait_ge(*count(done_a if v % 2 == 0 else done_d, v // 2 + 1))
                    for j, src in enumerate(ins):
                        mm = pe.transpose(ps[:, banks[u % len(banks)], j * P:(j + 1) * P], src, ident)
                    mm.then_inc(S(tag), 1)

            to_tokens("v2", [([("kv_v", DT)], [VF[:, 4 * g + j, n * P:(n + 1) * P] for j in range(4)])
                             for n in range(QT) for g in range(2)], "v2_a", "v2_d", [4, 5, 6, 7])
            linear("fox_q", HQ, LQ, normed_lo("q"), ("fox_q", 0), [("kv_f", 1)])
            pe.wait_ge(S("v2_a"), 4)
            pe.wait_ge(S("v2_d"), 4)
            head_sums("kn2", DT)
            head_spread("kn2", DT, [6, 7])
            pe.wait_ge(*count("fox_q", DT))
            head_sums("qn2", DT, 4)
            head_spread("qn2", DT, [6, 7])

            def attend(tag, units, B, keys_of, values_of, bias_of):
                per_pair = len([x for x in units if x[1] == 0])

                def keys(u):
                    return CMPB if units[u][0] == "cmp" else P * (units[u][3] + 1)

                def scores(u):
                    name, p, hp, i = units[u]
                    n = keys(u)
                    if u % per_pair == 0:
                        pe.wait_ge(*count(f"{tag}_q_lo", p + 1))
                    if u >= 3:
                        pe.wait_ge(*count(f"{tag}_exp", u - 2))
                    acc = ps[:, u % 3, 0:n]
                    qh, ql = (B["Q"][:, p % 2, 2 * hp + half, i * P:(i + 1) * P] for half in range(2))
                    kh, kl = keys_of(name, p, n)
                    pe.matmul(acc, qh, kh, start=True, stop=False)
                    pe.matmul(acc, qh, kl, start=False, stop=False)
                    pe.matmul(acc, ql, kh, start=False, stop=False)
                    if name == "cmp":
                        pe.matmul(acc, B["id"][:, :], c2(B, "cneg", i)[:, 0:n], start=False, stop=False)
                    else:
                        pe.matmul(ps[:, u % 3, n - P:n], B["id"][:, :], c2(B, "causal"), start=False, stop=False)
                    rows, head = bias_of(name, p, hp, n)
                    for r, row in enumerate(rows):
                        mm = pe.matmul(acc, B["id"][:, head:head + 1].to_broadcast([P, P]), row, start=False, stop=r == len(rows) - 1)
                    mm.then_inc(S(f"{tag}_s"), 1)

                def turn(u):
                    pe.wait_ge(*count(f"{tag}_pn", u + 1))
                    if u >= 2:
                        pe.wait_ge(*count(f"{tag}_pt", u - 1))
                    w = min(P, keys(u))
                    for j in range((keys(u) + P - 1) // P):
                        mm = pe.transpose(ps[0:w, 3 + u % 2, j * P:(j + 1) * P], B["P"][:, u % 3, j * P:j * P + w], ident)
                    mm.then_inc(S(f"{tag}_t"), 1)

                def values(u):
                    name, p, hp, i = units[u]
                    pe.wait_ge(*count(f"{tag}_pt", u + 1))
                    if u % per_pair == 0 and p >= 2:
                        pe.wait_ge(*count(f"{tag}_out_lo", p - 1))
                    nk = (keys(u) + P - 1) // P
                    w = min(P, keys(u))
                    first = name in ("fox", "slc")
                    last = name in ("fox", "cmp")
                    for j in range(nk):
                        mm = pe.matmul(ps[hp * HD:(hp + 1) * HD, 5 + p % 2, i * P:(i + 1) * P], values_of(name, p, hp, j, w),
                                       B["PT"][0:w, u % 2, j, :], start=first and j == 0, stop=last and j == nk - 1)
                    mm.then_inc(S(f"{tag}_pv"), 1)

                scores(0)
                scores(1)
                for u in range(len(units)):
                    if u + 2 < len(units):
                        scores(u + 2)
                    turn(u)
                    if u:
                        values(u - 1)
                values(len(units) - 1)

            pe.wait_ge(*count("qn2_used", 8))
            pe.wait_ge(S("kn_lo"), 8)
            pe.wait_ge(S("f_bias"), 1)
            attend("fa", FOX, AF, lambda name, p, n: (KH[:, p, 0:n], KL[:, p, 0:n]),
                   lambda name, p, hp, j, w: V2[:, j, (2 * p + hp) * HD:(2 * p + hp + 1) * HD],
                   lambda name, p, hp, n: ((fbiasR[:, 0, 0:n], fbiasR[:, 1, 0:n]), 2 * p + hp))
            if upto < 7:
                return
            pe.wait_ge(*count("fa_out_lo", DT))
            linear("fox_o", OH, OL, ("fa_out_lo", 0), ("x_up", 2 * DT), [])
            mlp(1, 3, HH, HL)
            linear("conv_c", HH, HL, normed_lo("n1"), ("conv_c", 0), [], norm=4)
            linear("conv_x", HH, HL, normed_lo("n1"), ("conv_x", 0), [("conv_c", DT)])
            linear("conv_b", HH, HL, normed_lo("n1"), ("zf", 0), [("conv_x", DT)])
            linear("gate_b", HH, HL, normed_lo("n1"), ("gate_b", 0), [("zf", DT)])
            if upto < 9:
                return
            linear("branch_b", ZH, ZL, ("z_lo", 0), ("branch_b", 0), [("gate_b", DT)])
            linear("gate_a", HH, HL, normed_lo("n1"), ("gate_a", 0), [("branch_b", DT)])
            linear("nsa_q", HH, HL, normed_lo("n1"), ("nsa_q", 0), [("gate_a", DT)])
            linear("nsa_kv", HH, HL, normed_lo("n1"), ("nsa_kv", 0), [("nsa_q", 4)])
            linear("nsa_g", HH, HL, normed_lo("n1"), ("nsa_g", 0), [("nsa_kv", 6)])
            pe.wait_ge(*count("nsa_g", 1))
            head_sums("q3", 4)
            head_spread("q3", 4, [6, 7])
            head_sums("k3", 2, 4)
            head_spread("k3", 2, [6, 7])
            for w in range(2):
                for n in range(QT):
                    mm = pe.transpose(ps[:, w, n * P:(n + 1) * P], (R1[:, 7, n * P:(n + 1) * P], R2[:, 1, n * P:(n + 1) * P])[w], ident)
                mm.then_inc(S("v3"), 1)
            for n in range(QT):
                mm = pe.transpose(ps[:, 2, n * P:(n + 1) * P], R2[:, 2, n * P:(n + 1) * P], ident)
            mm.then_inc(S("g3"), 1)
            pe.wait_ge(S("cw_in"), 16)
            pe.wait_ge(S("ce"), 2)
            pe.wait_ge(*count("k3_used", 2))
            for g in range(2):
                h = slice(g * HD, g * HD + HD)
                for w in range(CMPB):
                    mm = pe.matmul(ps[h, 3, 0:CMPN], CW[h, 0, w * HD:(w + 1) * HD], CE[h, 0, w, :], start=w == 0, stop=w == CMPB - 1)
            mm.then_inc(S("kc"), 1)
            for g in range(2):
                h = slice(g * HD, g * HD + HD)
                for w in range(CMPB):
                    mm = pe.matmul(ps[0:CMPN, 4 + g, 0:HD], CE[h, 1, w, :], CW[h, 1, w * HD:(w + 1) * HD], start=w == 0, stop=w == CMPB - 1)
            mm.then_inc(S("vc"), 1)
            pe.wait_ge(S("kc_sq"), 1)
            pe.matmul(ps[:, 6, 0:CMPN], const("bones"), tmpA[:, 0:CMPN], start=True, stop=True).then_inc(S("kc_sum"), 1)
            pe.wait_ge(S("kc_done"), 1)
            pe.wait_ge(S("v3_read"), 2)
            pe.wait_ge(S("g3_read"), 1)
            pe.wait_ge(S("vc_read"), 2)
            pe.wait_ge(*count("q3_used", 4))
            pe.wait_ge(S("k2_lo"), 2)

            def nsa_keys(name, p, n):
                if name == "cmp":
                    return KCR[:, 0, 0:n], KCR[:, 1, 0:n]
                w = ("slc", "win").index(name)
                return K2[:, 2 * w, 0:n], K2[:, 2 * w + 1, 0:n]

            attend("na", NSA, A2, nsa_keys,
                   lambda name, p, hp, j, w: VC[0:w, hp * HD:(hp + 1) * HD] if name == "cmp"
                   else V3[:, ("slc", "win").index(name), j, hp * HD:(hp + 1) * HD],
                   lambda name, p, hp, n: ((c2(A2, "cbias" if name == "cmp" else "abias")[:, 0:n],), 4 * hp + p))
            if upto < 10:
                return
            pe.wait_ge(*count("na_out_lo", 4))
            for j in range(4):
                b = START["branch_a"] + j
                wide_tiles(b, b % SPL, j, 0, (NHi, NLo), None if j < 2 else ("mixed", 2 * j - 2))
            linear("out", MH, ML, ("lo_mx", 0), ("x_up", 4 * DT), [])
            mlp(2, 5, HH, HL)


        @block.scalar
        def _(act):
            ticks = {}

            def link(ins, name="act_chain"):
                name = shared.get(name, (name, 0))[0]
                ticks[name] = ticks.get(name, 0) + 1
                ins.then_inc(S(name), 1)
                act.wait_ge(S(name), ticks[name])

            def mark(ins, name):
                first = shared.get(name, (name, 0))[0]
                ticks[first] = ticks.get(first, 0) + 1
                ins.then_inc(S(first), 1)

            def norm_squares(n, tag=None, gain=None, g0=0, hi=None):
                for i in range(DT):
                    if n == 0:
                        act.wait_ge(S("x_in"), 16)
                    else:
                        act.wait_ge(S("x_up"), DT * (n - 1) + i + 1)
                    if tag is not None:
                        mark(act.activation(hi[:, i, :], X[:, i, :], ACT.Copy, scale=vcol(gain, g0 + i)), "normed_hi")
                    if i >= 2:
                        act.wait_ge(S("norm_sum"), DT * n + i - 1)
                    mark(act.activation(tmp[i % 2][:, :], X[:, i, :], ACT.Square), "norm_sq")

            def norm_root(n):
                act.wait_ge(S("norm_mean"), n + 1)
                mark(act.activation(rstd[:, :], ps[:, 4, :], ACT.Sqrt, scale=1.0 / D, bias=epsn[:, 0:1]), "norm_root")

            act.wait_ge(S("consts_set"), 1)
            norm_squares(0)
            norm_root(0)

            def mix_prev(n):
                m, i = divmod(n, DT)
                if n < DT:
                    act.wait_ge(S("h_ready"), n + 1)
                if n >= 2:
                    act.wait_ge(S("mix_m"), n - 1)
                mark(act.activation(mixT[:, n % 2, 1:T], H[:, i, 0:T - 1], ACT.Copy,
                               scale=vcol("mu", 8 * MIXES[m] + i)), "mix_t")

            def mix_hi(n):
                act.wait_ge(S("mix_m"), n + 1)
                if n >= 2:
                    mix_used(act, n - 2)
                mark(act.activation(mixH[:, n % 2, :], mixM[:, n % 2, :], ACT.Copy), "mix_hi")

            def rkv_read(p):
                dst = (Rr, Kk, Vv)[p]
                for e in range(DT):
                    if e < 7:
                        act.wait_ge(S("rkv_done"), 7 * p + e + 1)
                    else:
                        act.wait_ge(S("blk"), START["r"] + DT * (p + 1))
                    mark(act.activation(dst[:, e, :], ps[:, e, :], ACT.Copy), "rkv_read")

            last = 24 if upto < 2 else 48
            mix_prev(0)
            for n in range(last):
                if n == 18:
                    act.wait_ge(S("blk"), 1)
                    mark(act.activation(loF[0:HD, 0, :], ps[0:HD, 0, :], ACT.Tanh), "lo_f")
                    mark(act.activation(loF[HD:P, 1, :], ps[HD:P, 1, :], ACT.Copy), "lo_f")
                    act.wait_ge(S("lo_f"), 2)
                    mark(act.activation(loH[:, :, :], loF[:, :, :], ACT.Copy), "lo_h")
                if n == 24:
                    lora_reads(act) if False else None
                if n + 1 < last:
                    mix_prev(n + 1)
                if n == 25:
                    act.wait_ge(S("blk"), 3)
                    mark(act.activation(sgF[:, :, :], ps[:, 2:4, :], ACT.Sigmoid), "sg_ready")
                    for t in range(16):
                        m, e = divmod(t, DT)
                        if t < 15:
                            act.wait_ge(S("lora_up"), t + 1)
                        else:
                            act.wait_ge(S("blk"), 4)
                        mark(act.activation((DEC, AG)[m][:, e, :], ps[:, (4 + t) % 8, :], ACT.Sigmoid,
                                       bias=vcol(("w0", "a0")[m], e)), "lora_read")
                if n >= 33 and (n - 33) % DT == 0:
                    rkv_read((n - 33) // DT)
                if n == 42:
                    act.wait_ge(S("rkv_read"), 16)
                    for i in range(DT):
                        mark(act.activation(KN[:, i, :], Kk[:, i, :], ACT.Copy, scale=vcol("k_k", i)), "kk_raw")
                if 26 <= n < 30:
                    e = 2 * (n - 26)
                    act.wait_ge(S("lora_read"), e + 2)
                    mark(act.activation(DEC[:, e:e + 2, :], DEC[:, e:e + 2, :], ACT.Exp, scale=DECAY), "decay")
                mix_hi(n)
            if upto < 2:
                act.wait_ge(S("blk"), 3)
                mark(act.activation(sgF[:, :, :], ps[:, 2:4, :], ACT.Sigmoid), "sg_ready")
                for t in range(16):
                    m, e = divmod(t, DT)
                    act.wait_ge(S("lora_up") if t < 15 else S("blk"), t + 1 if t < 15 else 4)
                    mark(act.activation((DEC, AG)[m][:, e, :], ps[:, (4 + t) % 8, :], ACT.Sigmoid,
                                   bias=vcol(("w0", "a0")[m], e)), "lora_read")
                act.wait_ge(S("lora_read"), 16)
                act.sem_inc(S("all_done"), 1)
                return
            rkv_read(2)
            for i in range(DT):
                act.wait_ge(S("kk_raw"), i + 1)
                if i >= 2:
                    act.wait_ge(S("kk_sum"), i - 1)
                mark(act.activation(tmp[i % 2][:, :], KN[:, i, :], ACT.Square), "kk_sq")
                if i >= 2:
                    act.wait_ge(S("k_scaled"), i - 1)
                mark(act.activation(kfac[:, i % 2, :], AG[:, i, :], ACT.Identity, scale=vcol("k_a", i), bias=oka[:, i:i + 1]), "k_factor")
            act.wait_ge(S("kk_sum"), DT)
            mark(act.activation(rstd[0:48, :], ps[0:48, 5, :], ACT.Sqrt), "kk_norm")
            act.wait_ge(S("bo_sum"), DT)
            mark(act.activation(tmpA[0:48, :], ps[0:48, 6, :], ACT.Copy), "bo_row")
            for u in list(range(16)) + list(range(16, 24, 2)):
                n, g = divmod(u % 8, 2)
                act.wait_ge(S("tok_done"), u + 1)
                mark(act.activation((Vtok, Btok, Ktok)[u // 8][:, n, g * 512:(g + 1) * 512], ps[:, 4 + u % 4, :], ACT.Copy), "tok_a")
            if upto < 3:
                return
            nseq = 0
            for n in range(QT):
                for hp in range(2):
                    act.wait_ge(S("p2"), 2 * n + hp + 1)
                    mark(act.activation(mP2[:, hp, :, :], ps[:, 2 + hp, :].rearrange("p (a b) -> p a b", a=DT), ACT.Copy), "p2_read")
                for c in range(2):
                    k = slice(c * HD, c * HD + HD)
                    tc = slice((2 * n + c) * C, (2 * n + c + 1) * C)
                    act.wait_ge(S("y1"), nseq + 1)
                    mark(act.activation(Rr[:, :, tc], ps[:, 5, :].rearrange("p (a b) -> p a b", a=DT), ACT.Copy), "y1_read")
                    act.wait_ge(S("u"), 2 * nseq + 1)
                    mark(act.activation(mT[k, 0, :, :], ps[k, 2, :].rearrange("p (a b) -> p a b", a=DT), ACT.Copy), "u_new_a")
                    nseq += 1
            if upto < 4:
                return

            def head_squares(tag, n, src, after):
                for i in range(n):
                    act.wait_ge(*count(after[0], after[1] + i))
                    if i >= 2:
                        act.wait_ge(*count(f"{tag}_sum", i - 1))
                    mark(act.activation(tmp[i % 2][:, :], src(i), ACT.Square), f"{tag}_sq")

            def head_root(tag, n, bank_, bias):
                act.wait_ge(*count(f"{tag}_sum", n))
                mark(act.activation(rstd[0:48, :], ps[0:48, bank_, :], ACT.Sqrt, scale=1.0 / HD, bias=bias[0:48, 0:1]), f"{tag}_norm")

            def mlp(m, norm):
                base = START[f"mlp{m}"]

                def group(b, g, first=False):
                    for j in range(5):
                        if j < 4:
                            act.wait_ge(S("rel"), FT * m + g * 4 + j + 1)
                            if not (first and j < 2):
                                act.wait_ge(S("hid"), FT * m + g * 4 + j - 1)
                            act.activation(sqrT[:, j % 2, :], relT[:, j % 2, :], ACT.Square).then_inc(S("full"), 1)
                        if j:
                            act.wait_ge(S("full"), FT * m + g * 4 + j)
                            dst = hid_of(g)
                            act.activation(dst[:, j - 1, :], sqrT[:, (j - 1) % 2, :], ACT.Copy).then_inc(S("hidhi"), 1)

                parity = [0]

                def hid_of(g):
                    return hidH[parity[0]]

                def turn(b, g, buf, first=False):
                    parity[0] = buf
                    group(b, g, first)

                turn(base, 0, 0, first=True)
                turn(base + 4, 1, 1)
                with act.Fori(0, 3) as i:
                    turn(base + 12 + i * 16, i * 2 + 2, 0)
                    turn(base + 20 + i * 16, i * 2 + 3, 1)

            act.wait_ge(S("y_done"), NCH)
            act.sem_inc(S("rec_done"), 1)
            mark(act.activation(sgH[:, :, :], sgF[:, :, :], ACT.Copy), "sg_hi")
            for i in range(DT):
                act.wait_ge(S("gn_c"), i + 1)
                if i >= 2:
                    act.wait_ge(*count("gn_sum", i - 1))
                mark(act.activation(tmp[i % 2][:, :], Rr[:, i, :], ACT.Square), "gn_sq")
            head_root("gn", DT, 5, epsg)
            for i in range(DT + 1):
                if i < DT:
                    act.wait_ge(*count("gn_used", i + 1))
                    mark(act.activation(Rr[:, i, :], Rr[:, i, :], ACT.Identity, scale=vcol("lnx_w", i), bias=vcol("lnx_b", i)), "gn_aff")
                if i:
                    act.wait_ge(S("y_gated"), i)
                    mark(act.activation(YH[:, i - 1, :], tmp[(i - 1) % 2][:, :], ACT.Copy), "y_hi")
            norm_squares(1, "m0", "mlp_g", 0, HH)
            if upto < 5:
                return
            norm_root(1)
            mlp(0, 1)
            norm_squares(2, "kv", "kv_g", 0, HH)
            if upto < 6:
                return
            norm_root(2)
            for i in range(DT):
                mark(act.activation(HQ[:, i, :], X[:, i, :], ACT.Copy, scale=vcol("attn_g", i)), "normed_hi")
            act.wait_ge(*count("kv_f", 1))
            link(act.activation(ssq[0:16, :], ssq[0:16, :], ACT.Identity, bias=vcol("f_bias")[0:16, :]), "f_logit")
            act.wait_ge(S("bias_clear"), 1)
            link(act.activation(tmpA[0:16, :], ssq[0:16, :], ACT.Abs))
            link(act.activation(tmpA[0:16, :], tmpA[0:16, :], ACT.Exp, scale=-1.0))
            mark(act.activation(tmpA[0:16, :], tmpA[0:16, :], ACT.Ln, bias=1.0), "f_log")
            for u in range(0, 8, 2):
                n, g = divmod(u, 2)
                act.wait_ge(S("v2"), u + 1)
                mark(act.activation(V2[:, n, g * 512:(g + 1) * 512], ps[:, 4 + u % 4, :], ACT.Copy), "v2_a")
            head_squares("kn2", DT, lambda i: KF[:, i, :], ("kv_k", 1))
            act.wait_ge(*count("fox_q", DT))
            act.dma_start(AF["c2"][:, :], consts2).then_inc(S("c2f"), 16)
            head_root("kn2", DT, 5, epsn)
            for i in range(DT):
                act.wait_ge(*count("kn2_used", i + 1))
                mark(act.activation(KH[:, i, :], tmp[i % 2][:, :], ACT.Copy), "kn_hi")
            act.wait_ge(S("kn_lo"), DT)
            act.wait_ge(S("f_bias"), 1)
            mark(act.activation(fbiasR[:, 0, :], fbias[:, :], ACT.Copy), "f_bias_hi")
            head_squares("qn2", DT, lambda i: QR[:, i, :], ("fox_q", 1))
            head_root("qn2", DT, 4, epsn)

            def attention_consts(B, dma):
                act.wait_ge(S(dma), 16)
                link(act.activation(B["c2r"][:, :], B["c2"][:, :], ACT.Copy))
                link(act.activation(B["id"][:, :], ident, ACT.Copy))

            def attend(tag, units, B, src, dst, used):
                per_pair = len([x for x in units if x[1] == 0])
                pairs = len(units) // per_pair

                def queries(p):
                    if p >= 2:
                        act.wait_ge(*count(f"{tag}_s", (p - 1) * per_pair))
                    act.wait_ge(*count(used, p + 1))
                    link(act.activation(B["Q"][0:HD, p % 2, 0, :], src(p)[0:HD, :], ACT.Copy))
                    mark(act.activation(B["Q"][HD:P, p % 2, 2, :], src(p)[HD:P, :], ACT.Copy), f"{tag}_q_hi")

                def exps(u):
                    name, p, hp, i = units[u]
                    n = CMPB if name == "cmp" else P * (i + 1)
                    act.wait_ge(*count(f"{tag}_max", u + 1))
                    if u >= 3:
                        act.wait_ge(*count(f"{tag}_t", u - 2))
                    if u >= 4:
                        act.wait_ge(*count(f"{tag}_pn", u - 3))
                    mark(act.activation(B["P"][:, u % 3, 0:n], ps[:, u % 3, 0:n], ACT.Exp, bias=B["col"][:, u % 4:u % 4 + 1],
                                        accum_out=B["col"][:, 4 + u % 4:5 + u % 4]), f"{tag}_exp")

                def transposed(u):
                    name, p, hp, i = units[u]
                    act.wait_ge(*count(f"{tag}_t", u + 1))
                    if u >= 2:
                        act.wait_ge(*count(f"{tag}_pv", u - 1))
                    if name == "cmp":
                        mark(act.activation(B["PT"][0:CMPB, u % 2, 0, :], ps[0:CMPB, 3 + u % 2, 0:P], ACT.Copy), f"{tag}_pt")
                    else:
                        mark(act.activation(B["PT"][:, u % 2, 0:i + 1, :], ps[:, 3 + u % 2, 0:P * (i + 1)].rearrange("p (a b) -> p a b", b=P),
                                            ACT.Copy), f"{tag}_pt")

                def output(p):
                    act.wait_ge(*count(f"{tag}_pv", (p + 1) * per_pair))
                    mark(act.activation(dst[:, p, :], ps[:, 5 + p % 2, :], ACT.Copy), f"{tag}_out_hi")

                queries(0)
                exps(0)
                for u in range(len(units)):
                    p, v = divmod(u, per_pair)
                    if u + 1 < len(units):
                        exps(u + 1)
                    transposed(u)
                    if v == 0 and p + 1 < pairs:
                        queries(p + 1)
                    if v == 2 and p:
                        output(p - 1)
                output(pairs - 1)

            attention_consts(AF, "c2f")
            attend("fa", FOX, AF, lambda p: QR[:, p, :], OH, "qn2_used")
            if upto < 7:
                return
            norm_squares(3, "m1", "mlp_g", 8, HH)
            norm_root(3)
            mlp(1, 3)
            norm_squares(4, "n1", "norm1", 0, HH)
            norm_root(4)
            for i in range(DT):
                act.wait_ge(S("zf"), i + 1)
                mark(act.activation(ZH[:, i, :], tmp[i % 2][:, :], ACT.Copy), "z_hi")
            for gate in ("gate_b", "gate_a"):
                for e in range(DT):
                    act.wait_ge(*count(gate, e + 1))
                    mark(act.activation(SG[:, e, :], SG[:, e, :], ACT.Sigmoid), "gated")
            act.wait_ge(*count("nsa_g", 1))
            act.dma_start(A2["c2"][:, :], consts2).then_inc(S("c2s"), 16)
            act.dma_start(CW[:, :, :], cmpw).then_inc(S("cw_in"), 16)
            mark(act.activation(R2[:, 2, :], R2[:, 2, :], ACT.Sigmoid), "gates")
            head_squares("q3", 4, lambda i: R1[:, i, :], ("nsa_q", 1))
            head_root("q3", 4, 5, epsn)
            act.wait_ge(*count("q3_used", 4))
            head_squares("k3", 2, lambda i: (R1[:, 6, :], R2[:, 0, :])[i], ("nsa_kv", 5))
            head_root("k3", 2, 4, epsn)
            for w in range(2):
                act.wait_ge(*count("k3_used", w + 1))
                mark(act.activation(K2[:, 2 * w, :], tmp[w][:, :], ACT.Copy), "k2_hi")
            for w in range(2):
                act.wait_ge(S("v3"), w + 1)
                mark(act.activation(V3[:, w, :, :], ps[:, w, :].rearrange("p (a b) -> p a b", b=P), ACT.Copy), "v3_read")
            act.wait_ge(S("g3"), 1)
            mark(act.activation(GT[:, :, 0:24], ps[:, 2, :].rearrange("p (a b) -> p a b", b=P)[:, :, 0:24], ACT.Copy), "g3_read")
            act.wait_ge(S("kc"), 1)
            act.wait_ge(S("cmp_clear"), 1)
            link(act.activation(KC[:, 0:CMPN], ps[:, 3, 0:CMPN], ACT.Copy), "kc_raw")
            act.wait_ge(S("k2_lo"), 2)
            mark(act.activation(tmpA[:, 0:CMPN], KC[:, 0:CMPN], ACT.Square), "kc_sq")
            act.wait_ge(S("vc"), 1)
            for g in range(2):
                mark(act.activation(VC[0:CMPN, g * HD:(g + 1) * HD], ps[0:CMPN, 4 + g, 0:HD], ACT.Copy), "vc_read")
            act.wait_ge(S("kc_sum"), 1)
            mark(act.activation(tmpB[:, 0:CMPN], ps[:, 6, 0:CMPN], ACT.Sqrt, scale=1.0 / HD, bias=epsn[:, 0:1]), "kc_norm")
            act.wait_ge(S("kc_f"), 1)
            mark(act.activation(KCR[:, 0, :], KC[:, :], ACT.Copy), "kc_hi")
            attention_consts(A2, "c2s")
            attend("na", NSA, A2, lambda p: R1[:, p, :], NHi, "q3_used")
            if upto < 10:
                return
            for i in range(DT):
                act.wait_ge(S("mixed"), i + 1)
                mark(act.activation(MH[:, i, :], MX[:, i, :], ACT.Copy), "hi_mx")
            norm_squares(5, "m2", "norm2", 0, HH)
            norm_root(5)
            mlp(2, 5)


        @block.vector
        def _(dve):
            ticks = {}

            def link(ins, name="dve_chain"):
                name = shared.get(name, (name, 0))[0]
                ticks[name] = ticks.get(name, 0) + 1
                ins.then_inc(S(name), 1)
                dve.wait_ge(S(name), ticks[name])

            def mark(ins, name):
                first = shared.get(name, (name, 0))[0]
                ticks[first] = ticks.get(first, 0) + 1
                ins.then_inc(S(first), 1)

            def norm_sum(n, i):
                dve.wait_ge(S("norm_sq"), DT * n + i + 1)
                if i == 0:
                    mark(dve.tensor_copy(ssq[:, :], tmp[0][:, :]), "norm_sum")
                else:
                    dve.wait_ge(S("norm_sum"), DT * n + i)
                    mark(dve.tensor_tensor(ssq[:, :], ssq[:, :], tmp[i % 2][:, :], ALU.add), "norm_sum")

            def norm_recip(n):
                dve.wait_ge(S("norm_root"), n + 1)
                link(dve.reciprocal(rstd[:, :], rstd[:, :]))

            link(dve.memset(epsn[:, :], EPS))
            link(dve.memset(epsg[:, :], GN_EPS))
            link(dve.memset(mixT[:, :, 0:1], 0.0))
            link(dve.memset(loF[HD:P, 0, :], 0.0))
            mark(dve.memset(loF[0:HD, 1, :], 0.0), "consts_set")
            for i in range(DT):
                norm_sum(0, i)
            dve.wait_ge(S("const_in"), 32)
            link(dve.tensor_scalar(omu[:, :], vec[:, VOFF["mu"]:VOFF["mu"] + 48], -1.0, 1.0, ALU.mult, ALU.add))
            link(dve.tensor_scalar(oka[:, :], vec[:, VOFF["k_a"]:VOFF["k_a"] + DT], -1.0, 1.0, ALU.mult, ALU.add))
            norm_recip(0)
            for i in range(DT):
                mark(dve.scalar_tensor_tensor(H[:, i, :], X[:, i, :], vcol("norm_g", i), rstd[:, :], ALU.mult, ALU.mult), "h_ready")
            dve.wait_ge(S("h_ready"), 8)

            def mix(n):
                m, i = divmod(n, DT)
                dve.wait_ge(S("mix_t"), n + 1)
                if n >= 2:
                    dve.wait_ge(S("mix_hi"), n - 1)
                mark(dve.scalar_tensor_tensor(mixM[:, n % 2, :], H[:, i, :], omu[:, 8 * MIXES[m] + i:8 * MIXES[m] + i + 1],
                                         mixT[:, n % 2, :], ALU.mult, ALU.add), "mix_m")

            def mix_lo(n):
                dve.wait_ge(S("mix_hi"), n + 1)
                if n >= 2:
                    mix_used(dve, n - 2)
                link(dve.tensor_tensor(mixL[:, n % 2, :], mixM[:, n % 2, :], mixH[:, n % 2, :].bitcast(F32), ALU.subtract), "mix_lo")

            last = 24 if upto < 2 else 48
            mix(0)
            for n in range(last):
                if n + 1 < last:
                    mix(n + 1)
                mix_lo(n)
                if n == 17:
                    dve.wait_ge(S("lo_h"), 1)
                    mark(dve.tensor_tensor(loL[:, :, :], loF[:, :, :], loH[:, :, :].bitcast(F32), ALU.subtract), "lo_split")
                if n == 30:
                    link(dve.memset(ssq[:, :], 0.0))
                if n >= 32:
                    e, second = divmod(n - 32, 2)
                    if not second:
                        dve.wait_ge(S("decay"), e // 2 + 1)
                        link(dve.tensor_copy(ssq[:, ::C], DEC[:, e, ::C]))
                        link(dve.memset(DEC[:, e, ::C], 0.0))
                        link(dve.tensor_tensor_scan(DEC[:, e, :], DEC[:, e, :], ssq[:, :], 0.0, ALU.mult, ALU.add))
                        link(dve.reciprocal(RD[:, e, 0:256], DEC[:, e, 0:256]))
                    else:
                        link(dve.reciprocal(RD[:, e, 256:T], DEC[:, e, 256:T]))
            if upto < 2:
                return
            for i in range(DT):
                dve.wait_ge(S("rkv_read"), 24)
                dve.wait_ge(S("k_factor"), i + 1)
                mark(dve.tensor_tensor(Kk[:, i, :], kfac[:, i % 2, :], Kk[:, i, :], ALU.mult), "k_scaled")
            dve.wait_ge(S("k_scaled"), DT)
            dve.wait_ge(S("kk_sum"), DT)
            for i in range(DT):
                if i >= 2:
                    dve.wait_ge(S("bo_sum"), i - 1)
                mark(dve.scalar_tensor_tensor(tmp[i % 2][:, :], Rr[:, i, :], vcol("r_k", i), Kk[:, i, :], ALU.mult, ALU.mult), "bo_sq")
            dve.wait_ge(S("kk_norm"), 1)
            link(dve.tensor_scalar(rstd[0:48, :], rstd[0:48, :], 1e-12, None, ALU.max))
            mark(dve.reciprocal(rstd[0:48, :], rstd[0:48, :]), "kk_root")
            link(dve.tensor_copy(dch[:, :, :], DEC[:, :, C - 1::C]))
            for i in range(DT):
                dve.wait_ge(S("kk_spread"), i + 1)
                link(dve.tensor_tensor(KN[:, i, :], KN[:, i, :], ps[:, i % 2, :], ALU.mult), "kk_used")
                link(dve.tensor_tensor(AG[:, i, :], AG[:, i, :], KN[:, i, :], ALU.mult))
                mark(dve.tensor_tensor(AG[:, i, :], AG[:, i, :], RD[:, i, :], ALU.mult), "bt")
            for i in range(DT):
                a = KN[:, i, :].rearrange("p (c t) -> p c t", t=C)
                d = DEC[:, i, :].rearrange("p (c t) -> p c t", t=C)
                mark(dve.scalar_tensor_tensor(a[:, :, 1:C], a[:, :, 1:C], -1.0, d[:, :, 0:C - 1], ALU.mult, ALU.mult), "kn_rest")
                mark(dve.tensor_scalar(a[:, :, 0:1], a[:, :, 0:1], -1.0, None, ALU.mult), "kn")
            for i in range(DT):
                dve.wait_ge(S("bo_spread"), i + 1)
                mark(dve.tensor_tensor(BON[:, i, :], Vv[:, i, :], ps[:, 2 + i % 2, :], ALU.mult), "bo_used")
            for u in range(17, 24, 2):
                n, g = divmod(u % 8, 2)
                dve.wait_ge(S("tok_done"), u + 1)
                mark(dve.tensor_copy(Ktok[:, n, g * 512:(g + 1) * 512], ps[:, 4 + u % 4, :]), "tok_d")
            dve.wait_ge(S("bo_used"), DT)
            dve.wait_ge(S("tok_d"), 4)
            if upto < 3:
                dve.wait_ge(S("tok_a"), 20)
                dve.sem_inc(S("all_done"), 1)
                return
            mark(dve.memset(ST[:, :], 0.0), "s_new")

            def wide(m, name, a=0):
                return const(name, a, a + C).unsqueeze(1).to_broadcast([P, DT, C])

            def bank(b, k=slice(0, P)):
                return ps[k, b, :].rearrange("p (a b) -> p a b", a=DT)

            gram = nlev = nseq = 0
            for n in range(QT):
                for what in range(5):
                    for hp in range(2):
                        dve.wait_ge(S("gram"), gram + 1)
                        src = bank(gram % 10 % 8)
                        if what == 0:
                            link(dve.tensor_tensor(mN[:, hp, :, :], src, wide(mN, "ltN"), ALU.mult))
                            link(dve.tensor_tensor(mQ[:, hp, :, :], src, wide(mQ, "lvN1"), ALU.mult))
                            mark(dve.tensor_tensor(mQ[:, hp, :, :], mQ[:, hp, :, :], wide(mQ, "id64"), ALU.add), "gram_read")
                        elif what == 1:
                            link(dve.tensor_tensor(mT[:, hp, :, :], src, wide(mT, "lvM"), ALU.mult))
                            mark(dve.tensor_tensor(mT[:, hp, :, :], mT[:, hp, :, :], wide(mT, "id64"), ALU.add), "gram_read")
                        else:
                            dst = (mZ, mRB, mRK)[what - 2]
                            mark(dve.tensor_tensor(dst[:, hp, :, :], src, wide(dst, "ltN" if what == 2 else "leT"), ALU.mult), "gram_read")
                        gram += 1
                for lv, s in enumerate(levels()):
                    for hp in range(2):
                        dve.wait_ge(S("z"), 2 * nlev + hp + 1)
                        mark(dve.tensor_tensor(mZ[:, hp, :, :], bank(hp), wide(mZ, "lvM", (lv + 1) * C), ALU.mult), "z_new")
                    for hp in range(2):
                        if s < 32:
                            dve.wait_ge(S("t"), 8 * n + 2 * lv + hp + 1)
                            mark(dve.tensor_tensor(mT[:, hp, :, :], mT[:, hp, :, :], bank(4 + hp), ALU.add), "t_new")
                        dve.wait_ge(S("q"), 2 * nlev + hp + 1)
                        mark(dve.tensor_tensor(mQ[:, hp, :, :], mQ[:, hp, :, :], bank(6 + hp), ALU.add), "q_new")
                    nlev += 1
                for c in range(2):
                    k = slice(c * HD, c * HD + HD)
                    tc = slice((2 * n + c) * C, (2 * n + c + 1) * C)
                    for hp in range(2):
                        dve.wait_ge(S("as"), 2 * nseq + hp + 1)
                        dve.wait_ge(S("p2_read"), 2 * n + hp + 1)
                        mark(dve.tensor_tensor(mN[k, hp, :, :], bank(hp, k), mP2[k, hp, :, :], ALU.add), "p_new")
                    dve.wait_ge(S("u"), 2 * nseq + 2)
                    mark(dve.tensor_copy(mT[k, 1, :, :], bank(3, k)), "u_new_d")
                    dve.wait_ge(S("s"), nseq + 1)
                    sv = ST[:, :].rearrange("p (a b) -> p a b", a=DT)
                    link(dve.tensor_tensor(sv, sv, bank(4), ALU.add))
                    mark(dve.tensor_tensor(sv, sv, dch[:, :, 2 * n + c].unsqueeze(2).to_broadcast([P, DT, HD]), ALU.mult), "s_new")
                    dve.wait_ge(S("y2"), nseq + 1)
                    dve.wait_ge(S("y1_read"), nseq + 1)
                    mark(dve.tensor_tensor(Rr[:, :, tc], Rr[:, :, tc], bank(6), ALU.add), "y_done")
                    nseq += 1
            if upto < 4:
                dve.wait_ge(S("y_done"), NCH)
                dve.sem_inc(S("all_done"), 1)
                return

            def split_input(i, gain, g0, hi, lo):
                dve.wait_ge(S("normed_hi"), ticks.get("normed_lo", 0) + 1)
                mark(dve.scalar_tensor_tensor(lo[:, i, :], X[:, i, :], vcol(gain, g0 + i), hi[:, i, :].bitcast(F32), ALU.mult, ALU.subtract), "normed_lo")

            def residual(phase, n, after):
                for e in range(DT + 1):
                    if e < DT:
                        dve.wait_ge(S("blk"), START[phase] + e + 1)
                        mark(dve.tensor_tensor(X[:, e, :], X[:, e, :], ps[:, e % 4, :], ALU.add), "x_up")
                    if e:
                        split_input(e - 1, *after)
                        norm_sum(n, e - 1)

            def scaled(phase, dst, factor=None):
                for e in range(COUNT[phase]):
                    dve.wait_ge(S("blk"), START[phase] + e + 1)
                    mark(dve.tensor_tensor(dst(e), ps[:, e % 4, :], (rstd if factor is None else factor)[:, :], ALU.mult), phase)

            def head_recip(tag, factor=None):
                dve.wait_ge(*count(f"{tag}_norm", 1))
                if factor is None:
                    mark(dve.reciprocal(rstd[0:48, :], rstd[0:48, :]), f"{tag}_root")
                else:
                    link(dve.reciprocal(rstd[0:48, :], rstd[0:48, :]))
                    mark(dve.tensor_scalar(rstd[0:48, :], rstd[0:48, :], factor, None, ALU.mult), f"{tag}_root")

            def mlp(m, norm, after=None):
                base = START[f"mlp{m}"]

                def squares(b, g, buf, first=False):
                    for j in range(5):
                        if j < 4:
                            dve.wait_ge(S("blk"), b + j + 1)
                            if not (first and j < 2):
                                dve.wait_ge(S("full"), FT * m + g * 4 + j - 1)
                            dve.scalar_tensor_tensor(relT[:, j % 2, :], ps[:, j, :], 0.0, rstd[:, :], ALU.max, ALU.mult).then_inc(S("rel"), 1)
                        if j:
                            dve.wait_ge(S("hidhi"), FT * m + g * 4 + j)
                            dve.tensor_tensor(hidL[buf][:, j - 1, :], sqrT[:, (j - 1) % 2, :], hidH[buf][:, j - 1, :].bitcast(F32),
                                              ALU.subtract).then_inc(S("hid"), 1)

                def add(b, last=False):
                    for j in range(4):
                        dve.wait_ge(S("blk"), b + j + 1)
                        for o in range(2):
                            e = 2 * j + o
                            ins = dve.tensor_tensor(X[:, e, :], X[:, e, :], ps[:, 4 + 2 * (j % 2) + o, :], ALU.add)
                            if last:
                                mark(ins, "x_up")
                            elif o:
                                ins.then_inc(S("down"), 1)
                        if last and norm < 5:
                            for e in ((2 * j - 2, 2 * j - 1) if j else ()) + ((6, 7) if j == 3 else ()):
                                split_input(e, *after)
                                norm_sum(norm + 1, e)

                squares(base, 0, 0, first=True)
                squares(base + 4, 1, 1)
                add(base + 8)
                with dve.Fori(0, 3) as i:
                    squares(base + 12 + i * 16, i * 2 + 2, 0)
                    add(base + 16 + i * 16)
                    squares(base + 20 + i * 16, i * 2 + 3, 1)
                    add(base + 24 + i * 16)
                add(base + 60, last=True)

            def clear_queries(B):
                link(dve.memset(B["Q"][HD:P, :, 0:2, :].bitcast(F32), 0.0))
                mark(dve.memset(B["Q"][0:HD, :, 2:4, :].bitcast(F32), 0.0), "q_clear")

            dve.wait_ge(S("sg_hi"), 1)
            mark(dve.tensor_tensor(sgL[:, :, :], sgF[:, :, :], sgH[:, :, :].bitcast(F32), ALU.subtract), "sg_split")
            for i in range(DT):
                dve.wait_ge(S("gn_mean"), i + 1)
                mark(dve.scalar_tensor_tensor(Rr[:, i, :], ps[:, i % 2, :], -1.0 / HD, Rr[:, i, :], ALU.mult, ALU.add), "gn_c")
            head_recip("gn")
            for i in range(DT):
                dve.wait_ge(*count("gn_spread", i + 1))
                mark(dve.tensor_tensor(Rr[:, i, :], Rr[:, i, :], ps[:, 2 + i % 2, :], ALU.mult), "gn_used")
            for i in range(DT + 1):
                if i < DT:
                    dve.wait_ge(S("gn_aff"), i + 1)
                    link(dve.tensor_tensor(Rr[:, i, :], Rr[:, i, :], BON[:, i, :], ALU.add))
                    if i < 7:
                        dve.wait_ge(S("gate_up"), i + 1)
                    else:
                        dve.wait_ge(S("blk"), START["gate_up"] + 2)
                    if i >= 2:
                        dve.wait_ge(S("y_hi"), i - 1)
                    mark(dve.tensor_tensor(tmp[i % 2][:, :], Rr[:, i, :], ps[:, 6 + i % 2, :], ALU.mult), "y_gated")
                if i:
                    dve.wait_ge(S("y_hi"), i)
                    mark(dve.tensor_tensor(YL[:, i - 1, :], tmp[(i - 1) % 2][:, :], YH[:, i - 1, :].bitcast(F32), ALU.subtract), "y_lo")
            dve.wait_ge(S("x_again"), 16)
            residual("rwkv_o", 1, ("mlp_g", 0, HH, HL))
            if upto < 5:
                dve.sem_inc(S("all_done"), 1)
                return
            norm_recip(1)
            mlp(0, 1, ("kv_g", 0, HH, HL))
            if upto < 6:
                dve.sem_inc(S("all_done"), 1)
                return
            norm_recip(2)
            for i in range(DT):
                split_input(i, "attn_g", 0, HQ, LQ)
            scaled("kv_k", lambda e: KF[:, e, :])
            scaled("kv_v", lambda e: VF[:, e, :])
            mark(dve.memset(tmpA[:, :], 0.0), "bias_clear")
            scaled("kv_f", lambda e: ssq[:, :])
            dve.wait_ge(S("f_log"), 1)
            link(dve.scalar_tensor_tensor(tmpA[0:16, :], ssq[0:16, :], 0.0, tmpA[0:16, :], ALU.min, ALU.subtract))
            link(dve.tensor_tensor_scan(ssq[0:16, :], one[0:16, :].to_broadcast([16, T]), tmpA[0:16, :], 0.0, ALU.mult, ALU.add))
            for u in range(1, 8, 2):
                n, g = divmod(u, 2)
                dve.wait_ge(S("v2"), u + 1)
                mark(dve.tensor_copy(V2[:, n, g * 512:(g + 1) * 512], ps[:, 4 + u % 4, :]), "v2_d")
            scaled("fox_q", lambda e: QR[:, e, :])
            clear_queries(AF)
            link(dve.memset(fbias[:, :], 0.0))
            mark(dve.tensor_scalar(fbias[0:16, :], ssq[0:16, :], -1.0, None, ALU.mult), "f_bias")
            head_recip("kn2")
            for i in range(DT + 1):
                if i < DT:
                    dve.wait_ge(*count("kn2_spread", i + 1))
                    mark(dve.scalar_tensor_tensor(tmp[i % 2][:, :], KF[:, i, :], vcol("kn_g", i), ps[:, 6 + i % 2, :], ALU.mult, ALU.mult), "kn2_used")
                if i:
                    dve.wait_ge(S("kn_hi"), i)
                    link(dve.tensor_tensor(KL[:, i - 1, :], tmp[(i - 1) % 2][:, :], KH[:, i - 1, :].bitcast(F32), ALU.subtract), "kn_lo")
            dve.wait_ge(S("f_bias_hi"), 1)
            mark(dve.tensor_tensor(fbiasR[:, 1, :], fbias[:, :], fbiasR[:, 0, :].bitcast(F32), ALU.subtract), "f_bias_lo")
            head_recip("qn2", 1.0 / 8)
            for i in range(DT):
                dve.wait_ge(*count("qn2_spread", i + 1))
                mark(dve.scalar_tensor_tensor(QR[:, i, :], QR[:, i, :], vcol("qn_g", i), ps[:, 6 + i % 2, :], ALU.mult, ALU.mult), "qn2_used")

            def attend(tag, units, B, src, dst, lo, gate=None):
                per_pair = len([x for x in units if x[1] == 0])
                pairs = len(units) // per_pair

                def keys(u):
                    return CMPB if units[u][0] == "cmp" else P * (units[u][3] + 1)

                def queries(p):
                    dve.wait_ge(*count(f"{tag}_q_hi", p + 1))
                    for hp in range(2):
                        h = slice(hp * HD, hp * HD + HD)
                        mark(dve.tensor_tensor(B["Q"][h, p % 2, 2 * hp + 1, :], src(p)[h, :], B["Q"][h, p % 2, 2 * hp, :].bitcast(F32), ALU.subtract),
                             f"{tag}_q_lo" if hp else "dve_chain")

                def maxima(u):
                    dve.wait_ge(*count(f"{tag}_s", u + 1))
                    if u >= 4:
                        dve.wait_ge(*count(f"{tag}_exp", u - 3))
                    mark(dve.tensor_reduce(B["col"][:, u % 4:u % 4 + 1], ps[:, u % 3, 0:keys(u)], AX, ALU.max, negate=True), f"{tag}_max")

                def normalise(u):
                    name, p, hp, i = units[u]
                    total, factor = (B["col"][:, 4 * r + u % 4:4 * r + 1 + u % 4] for r in (1, 2))
                    probs = B["P"][:, u % 3, 0:keys(u)]
                    dve.wait_ge(*count(f"{tag}_exp", u + 1))
                    if name == "cmp":
                        link(dve.tensor_tensor(probs, probs, c2(B, "cok", i), ALU.mult))
                        link(dve.tensor_reduce(total, probs, AX, ALU.add))
                        link(dve.tensor_scalar(total, total, 1e-30, None, ALU.max))
                    link(dve.reciprocal(factor, total))
                    if gate is None:
                        mark(dve.tensor_scalar(probs, probs, factor, None, ALU.mult), f"{tag}_pn")
                    else:
                        mark(dve.tensor_scalar(probs, probs, factor, gate(name, p, hp, i), ALU.mult, ALU.mult), f"{tag}_pn")

                def output(p):
                    dve.wait_ge(*count(f"{tag}_out_hi", p + 1))
                    mark(dve.tensor_tensor(lo[:, p, :], ps[:, 5 + p % 2, :], dst[:, p, :].bitcast(F32), ALU.subtract), f"{tag}_out_lo")

                queries(0)
                maxima(0)
                for u in range(len(units)):
                    p, v = divmod(u, per_pair)
                    if u + 1 < len(units):
                        maxima(u + 1)
                    normalise(u)
                    if v == 1 and p + 1 < pairs:
                        queries(p + 1)
                    if v == 3 and p:
                        output(p - 1)
                output(pairs - 1)

            attend("fa", FOX, AF, lambda p: QR[:, p, :], OH, OL)
            if upto < 7:
                dve.sem_inc(S("all_done"), 1)
                return
            residual("fox_o", 3, ("mlp_g", 8, HH, HL))
            norm_recip(3)
            mlp(1, 3, ("norm1", 0, HH, HL))
            norm_recip(4)
            link(dve.tensor_tensor(ssq[:, :], rstd[:, :], rstd[:, :], ALU.mult))
            scaled("conv_c", lambda e: CC[:, e, :], ssq)
            for e in range(DT):
                dve.wait_ge(S("blk"), START["conv_x"] + e + 1)
                mark(dve.tensor_tensor(CU[:, e, :], CC[:, e, :], ps[:, e % 4, :], ALU.mult), "conv_x")
            for e in range(DT):
                link(dve.tensor_scalar(CC[:, e, :], CU[:, e, :], vcol("conv", 16 + e), None, ALU.mult))
                link(dve.scalar_tensor_tensor(CC[:, e, 1:T], CU[:, e, 0:T - 1], vcol("conv", 8 + e), CC[:, e, 1:T], ALU.mult, ALU.add))
                link(dve.scalar_tensor_tensor(CC[:, e, 2:T], CU[:, e, 0:T - 2], vcol("conv", e), CC[:, e, 2:T], ALU.mult, ALU.add))
                link(dve.tensor_tensor(CC[:, e, :], CC[:, e, :], rstd[:, :], ALU.mult))
                dve.wait_ge(S("blk"), START["conv_b"] + e + 1)
                if e >= 2:
                    dve.wait_ge(S("z_hi"), e - 1)
                mark(dve.tensor_tensor(tmp[e % 2][:, :], CC[:, e, :], ps[:, e % 4, :], ALU.mult), "zf")
                dve.wait_ge(S("z_hi"), e + 1)
                mark(dve.tensor_tensor(ZL[:, e, :], tmp[e % 2][:, :], ZH[:, e, :].bitcast(F32), ALU.subtract), "z_lo")
            scaled("gate_b", lambda e: SG[:, e, :])
            if upto < 9:
                dve.sem_inc(S("all_done"), 1)
                return
            for e in range(DT):
                dve.wait_ge(S("gated"), e + 1)
                dve.wait_ge(S("blk"), START["branch_b"] + e + 1)
                mark(dve.tensor_tensor(MX[:, e, :], SG[:, e, :], ps[:, e % 4, :], ALU.mult), "branch_b")
            scaled("gate_a", lambda e: SG[:, e, :])
            scaled("nsa_q", lambda e: R1[:, e, :])
            scaled("nsa_kv", lambda e: R1[:, 4 + e, :] if e < 4 else R2[:, e - 4, :])
            scaled("nsa_g", lambda e: R2[:, 2, :])
            clear_queries(A2)
            link(dve.memset(KC[:, :], 0.0))
            mark(dve.memset(VC[:, :], 0.0), "cmp_clear")
            head_recip("q3", 1.0 / 8)
            for i in range(4):
                dve.wait_ge(*count("q3_spread", i + 1))
                mark(dve.scalar_tensor_tensor(R1[:, i, :], R1[:, i, :], vcol("qn2"), ps[:, 6 + i % 2, :], ALU.mult, ALU.mult), "q3_used")
            head_recip("k3")
            for i in range(2):
                dve.wait_ge(*count("k3_spread", i + 1))
                kt = (R1[:, 6, :], R2[:, 0, :])[i]
                mark(dve.scalar_tensor_tensor(tmp[i][:, :], kt, vcol("kn2", 1 + i), ps[:, 6 + i % 2, :], ALU.mult, ALU.mult), "k3_used")
            for i in range(2):
                dve.wait_ge(S("k2_hi"), i + 1)
                mark(dve.tensor_tensor(K2[:, 2 * i + 1, :], tmp[i][:, :], K2[:, 2 * i, :].bitcast(F32), ALU.subtract), "k2_lo")
            for w in range(2):
                for g in range(2):
                    n = (CMPN + 1 - g) // 2
                    src = R1[:, 4 + w, 16 * g:16 * g + 32 * n].rearrange("p (c w) -> p w c", w=CMPB)
                    pos = vec[:, VOFF["pos_k"] + CMPB * w:VOFF["pos_k"] + CMPB * (w + 1)].unsqueeze(2).to_broadcast([P, CMPB, n])
                    mark(dve.tensor_tensor(CE[:, w, :, g::2], src, pos, ALU.add), "ce" if g else "dve_chain")
            dve.wait_ge(S("kc_norm"), 1)
            link(dve.reciprocal(tmpB[:, 0:CMPN], tmpB[:, 0:CMPN]))
            mark(dve.scalar_tensor_tensor(KC[:, 0:CMPN], KC[:, 0:CMPN], vcol("kn2", 0), tmpB[:, 0:CMPN], ALU.mult, ALU.mult), "kc_f")
            dve.wait_ge(S("kc_hi"), 1)
            mark(dve.tensor_tensor(KCR[:, 1, :], KC[:, :], KCR[:, 0, :].bitcast(F32), ALU.subtract), "kc_done")

            attend("na", NSA, A2, lambda p: R1[:, p, :], NHi, NLo,
                   lambda name, p, hp, i: GT[:, i, 8 * ("cmp", "slc", "win").index(name) + 4 * hp + p:][:, 0:1])
            if upto < 10:
                dve.sem_inc(S("all_done"), 1)
                return
            for j in range(4):
                dve.wait_ge(S("blk"), START["branch_a"] + j + 1)
                for o in range(2):
                    e = 2 * j + o
                    link(dve.tensor_tensor(tmp[o][:, :], SG[:, e, :], ps[:, 4 + 2 * (j % 2) + o, :], ALU.mult))
                    mark(dve.tensor_tensor(MX[:, e, :], MX[:, e, :], tmp[o][:, :], ALU.add), "mixed")
                    dve.wait_ge(S("hi_mx"), e + 1)
                    mark(dve.tensor_tensor(ML[:, e, :], MX[:, e, :], MH[:, e, :].bitcast(F32), ALU.subtract), "lo_mx")
            residual("out", 5, ("norm2", 0, HH, HL))
            norm_recip(5)
            mlp(2, 5)


def arrange(x):
    f = {k: np.asarray(v) for k, v in x.items()}
    kmajor = lambda w: w.reshape(DT, P, -1, P).transpose(2, 1, 0, 3).reshape(-1, P, D)
    rows = lambda w: w.reshape(-1, P, D)

    def padded(w, rows_, cols):
        return np.pad(w, ((0, rows_ - w.shape[0]), (0, cols - w.shape[1])))

    def mlp(w_in, w_out):
        up = kmajor(w_in).reshape(8, 4, P, D)
        down = w_out.reshape(8, 4, P, 4, 2, P).transpose(0, 3, 2, 4, 1, 5).reshape(8, 4, P, D)
        order = [up[0]]
        for g in range(7):
            order += [up[g + 1], down[g]]
        return np.concatenate(order + [down[7]])

    g1 = padded(f["rwkv_g1"][0], D, 2 * P)
    g2 = padded(f["rwkv_g2"][0], 2 * P, D)
    heads = np.arange(D // 2).reshape(2, 4, HD).transpose(1, 0, 2).reshape(-1)
    win = f["w_in_2"][0]
    cut = np.cumsum([0, 512] + [128] * 6 + [24] + [D] * 5)
    part = [win[:, cut[i]:cut[i + 1]] for i in range(13)]
    wa = f["w_branch_a_2"][0][heads].reshape(4, P, 4, 2, P).transpose(2, 1, 3, 0, 4).reshape(4, P, D)
    blocks = [
        kmajor(np.concatenate([f["rwkv_w1"][0], f["rwkv_a1"][0]], 1)), kmajor(g1),
        np.concatenate([f["rwkv_w2"][0], f["rwkv_a2"][0]])[None],
        rows(f["rwkv_w_rkv"][0, 0]), rows(f["rwkv_w_rkv"][0, 1]), rows(f["rwkv_w_rkv"][0, 2]), rows(g2),
        kmajor(f["rwkv_w_o"][0]), mlp(f["mlp_w_in"][0], f["mlp_w_out"][0]),
        kmajor(f["kv_w"][:, :D]), kmajor(f["kv_w"][:, D:2 * D]), kmajor(padded(f["kv_w"][:, 2 * D:], D, P)),
        kmajor(f["attn_w_q"][0]), kmajor(f["attn_w_o"][0]), mlp(f["mlp_w_in"][1], f["mlp_w_out"][1]),
        kmajor(part[9]), kmajor(part[10]), kmajor(part[8]), kmajor(part[12]), kmajor(f["w_branch_b_2"][0]),
        kmajor(part[11]), kmajor(part[0][:, heads]), kmajor(np.concatenate(part[1:7], 1)),
        kmajor(padded(part[7], D, P)), wa, kmajor(f["w_out_2"][0]), mlp(f["w_up_2"][0], f["w_down_2"][0]),
    ]
    stream = np.ascontiguousarray(np.concatenate(blocks))
    assert stream.shape == (NBLK, P, D), stream.shape

    col = lambda v: v.reshape(-1, P).T
    dup = lambda v: np.concatenate([v, v], 0)
    fb = np.pad(f["kv_f_bias"], (0, P - NH)).reshape(P, 1)
    v = dict(norm_g=col(f["rwkv_norm_g"]), mu=col(f["rwkv_mu"]), w0=col(f["rwkv_w0"]), a0=col(f["rwkv_a0"]),
             k_k=col(f["rwkv_k_k"]), k_a=col(f["rwkv_k_a"]), r_k=col(f["rwkv_r_k"]), lnx_w=col(f["rwkv_lnx_w"]),
             lnx_b=col(f["rwkv_lnx_b"]), kv_g=col(f["kv_norm_g"]), attn_g=col(f["attn_norm_g"]),
             kn_g=col(f["k_norm_g"]), qn_g=col(f["q_norm_g"]), mlp_g=col(f["mlp_norm_g"]), norm1=col(f["norm1_g_2"]),
             norm2=col(f["norm2_g_2"]), conv=col(f["conv_w_2"]), qn2=dup(f["q_norm_g_2"].T), kn2=dup(f["k_norm_g_2"][0].T),
             pos_k=dup(f["cmp_pos_k_2"][0].T), pos_v=dup(f["cmp_pos_v_2"][0].T), f_bias=fb)
    vecs = np.ascontiguousarray(np.concatenate([v[n] for n, _ in VECS], 1))
    cmpw = np.stack([dup(f[n][0].reshape(CMPB, HD, HD).transpose(1, 0, 2).reshape(HD, -1))
                     for n in ("w_cmp_k_2", "w_cmp_v_2")], 1)
    xT = np.ascontiguousarray(f["x"][0].T.reshape(DT, P, T).transpose(1, 0, 2))
    first, second = constants()
    return dict(xT=xT, stream=stream, vecs=vecs, consts=first, consts2=second, cmpw=np.ascontiguousarray(cmpw))


def kernel(**inputs):
    from concourse import bacc
    from concourse.bass_utils import run_bass_kernel_spmd

    arrays = arrange(inputs)
    nc = bacc.Bacc("TRN2", target_bir_lowering=False, num_devices=1)
    aps = {n: nc.dram_tensor(n, a.shape, mybir.dt.from_np(a.dtype), kind="ExternalInput").ap() for n, a in arrays.items()}
    aps["out"] = nc.dram_tensor("out", (P, DT, T), F32, kind="ExternalOutput").ap()
    build(nc, **aps)
    r = run_bass_kernel_spmd(nc, [arrays], core_ids=[0])
    return r.results[0]["out"].transpose(1, 0, 2).reshape(1, D, T).transpose(0, 2, 1)
```
